# Optimizing a Trainium2 kernel written in Bass

```python
import jax, jax.numpy as jnp
from jax import lax
import numpy as np

D_MODEL = 1024
BATCH = 1
SEQ = 256
DEPTH = 2

CTX_LEN = 256
GRID_W = 64
N_Q_HEADS = 8
N_KV_HEADS = 2
HEAD_DIM = 64
Q_PER_KV = N_Q_HEADS // N_KV_HEADS
ATTN_WIDTH = N_Q_HEADS * HEAD_DIM
KV_WIDTH = N_KV_HEADS * HEAD_DIM
WINDOW = 128
BLOCK = 128
ROPE_BASE = 10000.0
POOL_GROUPS = 4
POOL_GROUP_DIM = 64
POOL_WIDTH = POOL_GROUPS * POOL_GROUP_DIM
POOL_WINDOWS = (2, 4, 8, 16)
FOURIER_GROUPS = 4
FOURIER_GROUP_DIM = 64
FOURIER_WIDTH = FOURIER_GROUPS * FOURIER_GROUP_DIM
N_BRANCHES = 3
IN_SPLITS = (KV_WIDTH, 2 * KV_WIDTH, 2 * KV_WIDTH + ATTN_WIDTH,
             2 * KV_WIDTH + ATTN_WIDTH + POOL_WIDTH,
             2 * KV_WIDTH + ATTN_WIDTH + POOL_WIDTH + FOURIER_WIDTH)
IN_WIDTH = 2 * KV_WIDTH + ATTN_WIDTH + POOL_WIDTH + FOURIER_WIDTH + N_BRANCHES * D_MODEL
D_FF = 2816
CONV_WIDTH = 3
N_MOD = 6
EPS = 1e-6
NEG_INF = -1e30


def rms_norm(x, g):
    xf = x.astype(jnp.float32)
    y = xf * lax.rsqrt(jnp.mean(xf * xf, axis=-1, keepdims=True) + EPS)
    return (y * g.astype(jnp.float32)).astype(x.dtype)

def adaln_params(cond, w_mod, b_mod):
    m = jax.nn.silu(cond) @ w_mod + b_mod
    return jnp.split(m[..., None, :], N_MOD, axis=-1)

def modulate(h, shift, scale):
    return h * (1 + scale) + shift

def axial_rope_tables(n_tokens):
    rows = n_tokens // GRID_W
    row = jnp.repeat(jnp.arange(rows, dtype=jnp.int32), GRID_W).astype(jnp.float32)
    col = jnp.tile(jnp.arange(GRID_W, dtype=jnp.int32), rows).astype(jnp.float32)
    n_freq = HEAD_DIM // 4
    inv_freq = ROPE_BASE ** (-jnp.arange(n_freq, dtype=jnp.float32) / n_freq)
    ang = jnp.stack([row[:, None] * inv_freq[None, :], col[:, None] * inv_freq[None, :]], axis=1)
    return jnp.cos(ang), jnp.sin(ang)

def apply_rope(x, cos, sin):
    B, T, H, _ = x.shape
    xr = x.astype(jnp.float32).reshape(B, T, H, 2, 2, HEAD_DIM // 4)
    c = cos[None, :, None, :, :]
    s = sin[None, :, None, :, :]
    x1, x2 = xr[..., 0, :], xr[..., 1, :]
    out = jnp.stack([x1 * c - x2 * s, x2 * c + x1 * s], axis=-2)
    return out.reshape(x.shape).astype(x.dtype)

def sink_column(sink, lead_shape):
    s = sink.astype(jnp.float32).reshape((1, N_KV_HEADS, Q_PER_KV) + (1,) * (len(lead_shape) - 2))
    return jnp.broadcast_to(s, tuple(lead_shape) + (1,))

def latent_attention(q, k, v, kc, vc, sink):
    B, T = q.shape[:2]
    nb = T // BLOCK
    ctx_len = kc.shape[1]
    scale = HEAD_DIM ** -0.5
    qb = q.reshape(B, nb, BLOCK, N_KV_HEADS, Q_PER_KV, HEAD_DIM)

    def band(a):
        a = a.reshape(B, nb, BLOCK, N_KV_HEADS, HEAD_DIM)
        pad = jnp.zeros_like(a[:, :1])
        ap = jnp.concatenate([pad, a, pad], axis=1)
        return jnp.concatenate([ap[:, :-2], ap[:, 1:-1], ap[:, 2:]], axis=2)

    kb, vb = band(k), band(v)
    s_lat = jnp.einsum('bnqhgd,bnkhd->bhgnqk', qb, kb).astype(jnp.float32) * scale
    blk = jnp.arange(nb, dtype=jnp.int32)[:, None]
    qpos = blk * BLOCK + jnp.arange(BLOCK, dtype=jnp.int32)[None, :]
    kpos = (blk - 1) * BLOCK + jnp.arange(3 * BLOCK, dtype=jnp.int32)[None, :]
    rel = kpos[:, None, :] - qpos[:, :, None]
    valid = (jnp.abs(rel) <= WINDOW) & (kpos[:, None, :] >= 0) & (kpos[:, None, :] < T)
    s_lat = jnp.where(valid, s_lat, NEG_INF)
    s_ctx = jnp.einsum('bnqhgd,bchd->bhgnqc', qb, kc).astype(jnp.float32) * scale
    s_all = jnp.concatenate([s_lat, s_ctx, sink_column(sink, s_lat.shape[:-1])], axis=-1)
    p = jax.nn.softmax(s_all, axis=-1)
    p_lat = p[..., :3 * BLOCK].astype(v.dtype)
    p_ctx = p[..., 3 * BLOCK:3 * BLOCK + ctx_len].astype(v.dtype)
    o = (jnp.einsum('bhgnqk,bnkhd->bnqhgd', p_lat, vb)
         + jnp.einsum('bhgnqc,bchd->bnqhgd', p_ctx, vc))
    return o.reshape(B, T, ATTN_WIDTH)

def context_attention(qc, kc, vc, sink):
    B, L = qc.shape[:2]
    scale = HEAD_DIM ** -0.5
    qg = qc.reshape(B, L, N_KV_HEADS, Q_PER_KV, HEAD_DIM)
    s = jnp.einsum('bqhgd,bkhd->bhgqk', qg, kc).astype(jnp.float32) * scale
    s_all = jnp.concatenate([s, sink_column(sink, s.shape[:-1])], axis=-1)
    p = jax.nn.softmax(s_all, axis=-1)[..., :L].astype(vc.dtype)
    o = jnp.einsum('bhgqk,bkhd->bqhgd', p, vc)
    return o.reshape(B, L, ATTN_WIDTH)

def multiscale_pool(u, pool_w, pool_scale):
    B, T = u.shape[:2]
    ug = u.reshape(B, T, POOL_GROUPS, POOL_GROUP_DIM).astype(jnp.float32)
    cs = jnp.concatenate([jnp.zeros_like(ug[:, :1]), jnp.cumsum(ug, axis=1)], axis=1)
    w = jnp.array(POOL_WINDOWS, dtype=jnp.int32)[None, :]
    t = jnp.arange(T, dtype=jnp.int32)[:, None]
    lo = jnp.clip(t - w // 2, 0, T)
    hi = jnp.clip(t - w // 2 + w, 0, T)
    gidx = jnp.arange(POOL_GROUPS, dtype=jnp.int32)[None, :]
    win_sum = cs[:, hi, gidx] - cs[:, lo, gidx]
    cnt = (hi - lo).astype(jnp.float32)[None, :, :, None]
    pooled = (win_sum / cnt - ug).astype(u.dtype)
    y = jnp.einsum('btgc,gcd->btgd', pooled, pool_w).reshape(B, T, POOL_WIDTH)
    return y * pool_scale

def fourier_mix(f):
    B, T = f.shape[:2]
    fg = f.reshape(B, T, FOURIER_GROUPS, FOURIER_GROUP_DIM).astype(jnp.float32)
    y = jnp.fft.fft2(fg, axes=(1, 3), norm='ortho').real
    return y.astype(f.dtype).reshape(B, T, FOURIER_WIDTH)

def merge_branches(o_attn, pool_in, four_in, gate_in, pool_w, pool_scale,
                   w_br_attn, w_br_pool, w_br_four, w_out):
    g_a, g_p, g_f = jnp.split(jax.nn.sigmoid(gate_in), N_BRANCHES, axis=-1)
    y = (g_a * (o_attn @ w_br_attn)
         + g_p * (multiscale_pool(pool_in, pool_w, pool_scale) @ w_br_pool)
         + g_f * (fourier_mix(four_in) @ w_br_four))
    return y @ w_out

def dwconv_centred(u, w):
    T = u.shape[1]
    up = jnp.pad(u, ((0, 0), (1, 1), (0, 0)))
    return up[:, :T] * w[0] + up[:, 1:T + 1] * w[1] + up[:, 2:] * w[2]

def conv_ffn(h, w_up, conv_w, w_down):
    a = dwconv_centred(h @ w_up, conv_w)
    val, gate = jnp.split(a, 2, axis=-1)
    return (val * jax.nn.silu(gate)) @ w_down

def first_inputs(seed: int = 0) -> dict:
    key = jax.random.key(seed)
    ks = jax.random.split(key, 24)
    f32 = jnp.float32
    n = lambda k, shape, s: jax.random.normal(k, shape, f32) * s
    return {
        'x': n(ks[0], (BATCH, SEQ, D_MODEL), 1.0),
        'c': n(ks[1], (BATCH, D_MODEL), 1.0),
        'ctx': n(ks[2], (BATCH, CTX_LEN, D_MODEL), 1.0),
        'c_ctx': n(ks[3], (D_MODEL,), 1.0),
        'w_mod': n(ks[4], (DEPTH, D_MODEL, N_MOD * D_MODEL), 0.5 * D_MODEL ** -0.5),
        'b_mod': n(ks[5], (DEPTH, N_MOD * D_MODEL), 0.02),
        'norm_mix': 1.0 + n(ks[6], (DEPTH, D_MODEL), 0.02),
        'norm_ffn': 1.0 + n(ks[7], (DEPTH, D_MODEL), 0.02),
        'w_in': n(ks[8], (DEPTH, D_MODEL, IN_WIDTH), D_MODEL ** -0.5),
        'attn_sink': n(ks[9], (DEPTH, N_Q_HEADS), 0.5),
        'pool_w': n(ks[10], (DEPTH, POOL_GROUPS, POOL_GROUP_DIM, POOL_GROUP_DIM), POOL_GROUP_DIM ** -0.5),
        'pool_scale': 1.0 + n(ks[11], (DEPTH, POOL_WIDTH), 0.02),
        'w_br_attn': n(ks[12], (DEPTH, ATTN_WIDTH, D_MODEL), ATTN_WIDTH ** -0.5),
        'w_br_pool': n(ks[13], (DEPTH, POOL_WIDTH, D_MODEL), POOL_WIDTH ** -0.5),
        'w_br_four': n(ks[14], (DEPTH, FOURIER_WIDTH, D_MODEL), FOURIER_WIDTH ** -0.5),
        'w_out': n(ks[15], (DEPTH, D_MODEL, D_MODEL), D_MODEL ** -0.5),
        'w_up': n(ks[16], (DEPTH, D_MODEL, 2 * D_FF), D_MODEL ** -0.5),
        'conv_w': n(ks[17], (DEPTH, CONV_WIDTH, 2 * D_FF), CONV_WIDTH ** -0.5),
        'w_down': n(ks[18], (DEPTH, D_FF, D_MODEL), D_FF ** -0.5),
        'norm_final': 1.0 + n(ks[19], (D_MODEL,), 0.02),
    }

def first_block(x, c, ctx, c_ctx, w_mod, b_mod, norm_mix, norm_ffn, w_in, attn_sink, pool_w, pool_scale,
              w_br_attn, w_br_pool, w_br_four, w_out, w_up, conv_w, w_down, norm_final):
    B, T, _ = x.shape
    cos, sin = axial_rope_tables(T)
    xc = ctx
    for l in range(DEPTH):
        last = l == DEPTH - 1
        sh1, sc1, g1, sh2, sc2, g2 = adaln_params(c, w_mod[l], b_mod[l])
        csh1, csc1, cg1, csh2, csc2, cg2 = adaln_params(c_ctx, w_mod[l], b_mod[l])

        h = modulate(rms_norm(x, norm_mix[l]), sh1, sc1)
        hc = modulate(rms_norm(xc, norm_mix[l]), csh1, csc1)
        k, v, q, u, f, gt = jnp.split(h @ w_in[l], IN_SPLITS, axis=-1)
        if last:
            kc, vc = jnp.split(hc @ w_in[l][:, :2 * KV_WIDTH], 2, axis=-1)
        else:
            kc, vc, qc, uc, fc, gtc = jnp.split(hc @ w_in[l], IN_SPLITS, axis=-1)
        L = hc.shape[1]
        q = apply_rope(q.reshape(B, T, N_Q_HEADS, HEAD_DIM), cos, sin)
        k = apply_rope(k.reshape(B, T, N_KV_HEADS, HEAD_DIM), cos, sin)
        v = v.reshape(B, T, N_KV_HEADS, HEAD_DIM)
        kc = kc.reshape(B, L, N_KV_HEADS, HEAD_DIM)
        vc = vc.reshape(B, L, N_KV_HEADS, HEAD_DIM)
        o = latent_attention(q, k, v, kc, vc, attn_sink[l])
        x = x + g1 * merge_branches(o, u, f, gt, pool_w[l], pool_scale[l],
                                    w_br_attn[l], w_br_pool[l], w_br_four[l], w_out[l])
        if not last:
            oc = context_attention(qc.reshape(B, L, N_Q_HEADS, HEAD_DIM), kc, vc, attn_sink[l])
            xc = xc + cg1 * merge_branches(oc, uc, fc, gtc, pool_w[l], pool_scale[l],
                                           w_br_attn[l], w_br_pool[l], w_br_four[l], w_out[l])

        hf = modulate(rms_norm(x, norm_ffn[l]), sh2, sc2)
        x = x + g2 * conv_ffn(hf, w_up[l], conv_w[l], w_down[l])
        if not last:
            hcf = modulate(rms_norm(xc, norm_ffn[l]), csh2, csc2)
            xc = xc + cg2 * conv_ffn(hcf, w_up[l], conv_w[l], w_down[l])
    return rms_norm(x, norm_final)


HEAD_DIM_2 = D_MODEL // 16
SB_HEADS = 6
ML_HEADS = 6
SG_GROUPS = 4
SB_WIDTH = SB_HEADS * HEAD_DIM_2
ML_WIDTH = ML_HEADS * HEAD_DIM_2
SG_WIDTH = SG_GROUPS * HEAD_DIM_2
MIX_HEADS = SB_HEADS + ML_HEADS + SG_GROUPS
MIX_WIDTH = SB_WIDTH + ML_WIDTH + SG_WIDTH
IN_SIZES = (SB_WIDTH, SB_WIDTH, SB_WIDTH, 2 * ML_WIDTH, ML_WIDTH, ML_WIDTH, ML_HEADS, ML_HEADS, 2 * SG_WIDTH)
IN_WIDTH_2 = sum(IN_SIZES)
Q_BLOCK = 128
ML_CHUNK = 128
SG_CHUNK = 128
CONV_WIDTH_2 = 4
PEER_HEADS = 8
PEER_NKEYS = 128
PEER_EXPERTS = PEER_NKEYS * PEER_NKEYS
PEER_SUBDIM = 128
PEER_TOPK = 16
PEER_BLOCK = 128
NORM_EPS = 1e-6


def rms_norm_2(x, g):
    x32 = x.astype(jnp.float32)
    return x32 * lax.rsqrt(jnp.mean(x32 * x32, axis=-1, keepdims=True) + NORM_EPS) * g.astype(jnp.float32)

def split_heads(t, n_heads):
    b, s, _ = t.shape
    return t.reshape(b, s, n_heads, HEAD_DIM_2).transpose(0, 2, 1, 3)

def causal_conv(t, w, b):
    s = t.shape[1]
    tp = jnp.pad(t, ((0, 0), (CONV_WIDTH_2 - 1, 0), (0, 0)))
    out = b.astype(jnp.float32)
    for j in range(CONV_WIDTH_2):
        out = out + tp[:, j:j + s] * w[j]
    return out

def stick_breaking_attention(q, k, v):
    s_len = q.shape[2]
    scale = HEAD_DIM_2 ** -0.5
    outs = []
    for blk in range(s_len // Q_BLOCK):
        start = blk * Q_BLOCK
        end = start + Q_BLOCK
        z = jnp.einsum('bhqd,bhkd->bhqk', q[:, :, start:end], k[:, :, :end]) * scale
        before = jnp.arange(end)[None, :] < (start + jnp.arange(Q_BLOCK))[:, None]
        log_keep = jnp.where(before, -jax.nn.softplus(z), 0.0)
        log_keep_after = lax.cumsum(log_keep, axis=3, reverse=True) - log_keep
        w = jnp.where(before, jnp.exp(jax.nn.log_sigmoid(z) + log_keep_after), 0.0)
        outs.append(jnp.einsum('bhqk,bhkd->bhqd', w, v[:, :, :end]))
    return jnp.concatenate(outs, axis=2)

def mlstm_chunkwise(q, k, v, i_pre, f_pre):
    b, h, s_len, d = q.shape
    nc = s_len // ML_CHUNK
    log_f = jax.nn.log_sigmoid(f_pre)

    def chunks(t):
        return jnp.moveaxis(t.reshape(b, h, nc, ML_CHUNK, *t.shape[3:]), 2, 0)

    tril = jnp.tril(jnp.ones((ML_CHUNK, ML_CHUNK), dtype=bool))

    def step(carry, inp):
        c_mat, n_vec, m = carry
        qc, kc, vc, ic, lfc = inp
        bcum = jnp.cumsum(lfc, axis=-1)
        dmat = jnp.where(tril, bcum[..., :, None] - bcum[..., None, :] + ic[..., None, :], -jnp.inf)
        m_inter = bcum + m[..., None]
        m_t = jnp.maximum(m_inter, jnp.max(dmat, axis=-1))
        inter_scale = jnp.exp(m_inter - m_t)
        qk = jnp.einsum('bhtd,bhsd->bhts', qc, kc) * jnp.exp(dmat - m_t[..., None])
        num = jnp.einsum('bhts,bhsd->bhtd', qk, vc) + inter_scale[..., None] * jnp.einsum('bhtd,bhde->bhte', qc, c_mat)
        den = jnp.sum(qk, axis=-1) + inter_scale * jnp.einsum('bhtd,bhd->bht', qc, n_vec)
        h_out = num / jnp.maximum(jnp.abs(den), jnp.exp(-m_t))[..., None]
        b_last = bcum[..., -1]
        g_s = b_last[..., None] - bcum + ic
        m_new = jnp.maximum(b_last + m, jnp.max(g_s, axis=-1))
        w_s = jnp.exp(g_s - m_new[..., None])
        decay = jnp.exp(b_last + m - m_new)
        c_new = decay[..., None, None] * c_mat + jnp.einsum('bhs,bhsd,bhse->bhde', w_s, kc, vc)
        n_new = decay[..., None] * n_vec + jnp.einsum('bhs,bhsd->bhd', w_s, kc)
        return (c_new, n_new, m_new), h_out

    init = (jnp.zeros((b, h, d, d), jnp.float32), jnp.zeros((b, h, d), jnp.float32), jnp.zeros((b, h), jnp.float32))
    _, hs = lax.scan(step, init, (chunks(q), chunks(k), chunks(v), chunks(i_pre), chunks(log_f)))
    return jnp.moveaxis(hs, 0, 2).reshape(b, h, s_len, d)

def spatial_gating(u, v, w_s, b_s):
    b, s_len, _ = u.shape
    nc = s_len // SG_CHUNK
    tril = jnp.tril(jnp.ones((SG_CHUNK, SG_CHUNK), dtype=jnp.float32))
    v5 = v.reshape(b, nc, SG_CHUNK, SG_GROUPS, HEAD_DIM_2)
    gate = jnp.einsum('gts,bcsgd->bctgd', w_s.astype(jnp.float32) * tril, v5) + b_s.astype(jnp.float32).T[:, :, None]
    return (u.reshape(b, nc, SG_CHUNK, SG_GROUPS, HEAD_DIM_2) * gate).reshape(b, s_len, SG_GROUPS, HEAD_DIM_2)

def mixing_sublayer(xn, w_in, sb_qn_g, sb_kn_g, ml_conv_w, ml_conv_b, ml_i_b, ml_f_b,
                    sg_vn_g, sg_w, sg_b, out_g, w_out):
    b, s_len, _ = xn.shape
    z = jnp.matmul(xn, w_in).astype(jnp.float32)
    cuts = [int(c) for c in np.cumsum(IN_SIZES)[:-1]]
    sb_q, sb_k, sb_v, ml_qk, ml_v, ml_o, ml_i, ml_f, sg_uv = jnp.split(z, cuts, axis=-1)
    head_g = out_g.astype(jnp.float32).reshape(MIX_HEADS, HEAD_DIM_2)

    q = rms_norm_2(split_heads(sb_q, SB_HEADS), sb_qn_g)
    k = rms_norm_2(split_heads(sb_k, SB_HEADS), sb_kn_g)
    y_sb = stick_breaking_attention(q, k, split_heads(sb_v, SB_HEADS)).transpose(0, 2, 1, 3)
    y_sb = rms_norm_2(y_sb, head_g[:SB_HEADS])

    qk = jax.nn.silu(causal_conv(ml_qk, ml_conv_w.astype(jnp.float32), ml_conv_b))
    mq = split_heads(qk[..., :ML_WIDTH], ML_HEADS)
    mk = split_heads(qk[..., ML_WIDTH:], ML_HEADS) * (HEAD_DIM_2 ** -0.5)
    i_pre = (ml_i + ml_i_b.astype(jnp.float32)).transpose(0, 2, 1)
    f_pre = (ml_f + ml_f_b.astype(jnp.float32)).transpose(0, 2, 1)
    y_ml = mlstm_chunkwise(mq, mk, split_heads(ml_v, ML_HEADS), i_pre, f_pre).transpose(0, 2, 1, 3)
    o_gate = jax.nn.sigmoid(ml_o).reshape(b, s_len, ML_HEADS, HEAD_DIM_2)
    y_ml = rms_norm_2(y_ml, head_g[SB_HEADS:SB_HEADS + ML_HEADS]) * o_gate

    uv = jax.nn.gelu(sg_uv)
    u = uv[..., :SG_WIDTH]
    v = rms_norm_2(uv[..., SG_WIDTH:].reshape(b, s_len, SG_GROUPS, HEAD_DIM_2),
                 sg_vn_g.reshape(SG_GROUPS, HEAD_DIM_2)).reshape(b, s_len, SG_WIDTH)
    y_sg = rms_norm_2(spatial_gating(u, v, sg_w, sg_b), head_g[SB_HEADS + ML_HEADS:])

    y = jnp.concatenate([y_sb, y_ml, y_sg], axis=2).reshape(b, s_len, MIX_WIDTH)
    return jnp.matmul(y.astype(xn.dtype), w_out)

def peer_ffn(xn, wq, sub_keys, u_tab, v_tab):
    b, s_len, d = xn.shape
    t = b * s_len
    xt = xn.reshape(t, d)
    q = jnp.matmul(xt, wq).astype(jnp.float32).reshape(t, PEER_HEADS, 2, PEER_SUBDIM)
    scores = jnp.einsum('thcd,hcnd->thcn', q, sub_keys.astype(jnp.float32))
    sv, si = lax.top_k(scores, PEER_TOPK)
    cand_s = (sv[:, :, 0, :, None] + sv[:, :, 1, None, :]).reshape(t, PEER_HEADS, PEER_TOPK * PEER_TOPK)
    cand_i = (si[:, :, 0, :, None] * PEER_NKEYS + si[:, :, 1, None, :]).reshape(t, PEER_HEADS, PEER_TOPK * PEER_TOPK)
    best_s, best_p = lax.top_k(cand_s, PEER_TOPK)
    idx = jnp.take_along_axis(cand_i, best_p, axis=-1)
    gate = jax.nn.softmax(best_s, axis=-1)
    nb = t // PEER_BLOCK

    def expert_block(args):
        xb, ib, gb = args
        act = jnp.einsum('td,thkd->thk', xb.astype(jnp.float32), u_tab[ib].astype(jnp.float32))
        wgt = jax.nn.gelu(act) * gb
        return jnp.einsum('thk,thkd->td', wgt, v_tab[ib].astype(jnp.float32))

    y = lax.map(expert_block, (xt.reshape(nb, PEER_BLOCK, d),
                               idx.reshape(nb, PEER_BLOCK, PEER_HEADS, PEER_TOPK),
                               gate.reshape(nb, PEER_BLOCK, PEER_HEADS, PEER_TOPK)))
    return y.reshape(b, s_len, d)

def second_inputs(seed: int = 0) -> dict:
    key = jax.random.key(seed)
    ks = jax.random.split(key, 20)
    f32 = jnp.float32
    nrm = lambda k, shape, scale: jax.random.normal(k, shape, f32) * scale
    return {
        "x": nrm(ks[0], (BATCH, SEQ, D_MODEL), 1.0),
        "norm1_g": 1.0 + nrm(ks[1], (DEPTH, D_MODEL), 0.02),
        "w_in": nrm(ks[2], (DEPTH, D_MODEL, IN_WIDTH_2), D_MODEL ** -0.5),
        "sb_qn_g": 1.0 + nrm(ks[3], (DEPTH, HEAD_DIM_2), 0.02),
        "sb_kn_g": 1.0 + nrm(ks[4], (DEPTH, HEAD_DIM_2), 0.02),
        "ml_conv_w": nrm(ks[5], (DEPTH, CONV_WIDTH_2, 2 * ML_WIDTH), CONV_WIDTH_2 ** -0.5),
        "ml_conv_b": nrm(ks[6], (DEPTH, 2 * ML_WIDTH), 0.02),
        "ml_i_b": nrm(ks[7], (DEPTH, ML_HEADS), 0.1),
        "ml_f_b": jnp.linspace(3.0, 6.0, ML_HEADS, dtype=f32)[None, :] + nrm(ks[8], (DEPTH, ML_HEADS), 0.02),
        "sg_vn_g": 1.0 + nrm(ks[9], (DEPTH, SG_WIDTH), 0.02),
        "sg_w": nrm(ks[10], (DEPTH, SG_GROUPS, SG_CHUNK, SG_CHUNK), SG_CHUNK ** -0.5),
        "sg_b": 1.0 + nrm(ks[11], (DEPTH, SG_GROUPS, SG_CHUNK), 0.02),
        "out_g": 1.0 + nrm(ks[12], (DEPTH, MIX_WIDTH), 0.02),
        "w_out": nrm(ks[13], (DEPTH, MIX_WIDTH, D_MODEL), MIX_WIDTH ** -0.5),
        "norm2_g": 1.0 + nrm(ks[14], (DEPTH, D_MODEL), 0.02),
        "peer_wq": nrm(ks[15], (DEPTH, D_MODEL, PEER_HEADS * 2 * PEER_SUBDIM), D_MODEL ** -0.5),
        "peer_keys": nrm(ks[16], (DEPTH, PEER_HEADS, 2, PEER_NKEYS, PEER_SUBDIM), PEER_SUBDIM ** -0.5),
        "peer_u": nrm(ks[17], (DEPTH, PEER_EXPERTS, D_MODEL), D_MODEL ** -0.5),
        "peer_v": nrm(ks[18], (DEPTH, PEER_EXPERTS, D_MODEL), (PEER_HEADS * PEER_TOPK) ** -0.5),
    }

def second_block(x, norm1_g, w_in, sb_qn_g, sb_kn_g, ml_conv_w, ml_conv_b, ml_i_b, ml_f_b,
              sg_vn_g, sg_w, sg_b, out_g, w_out, norm2_g, peer_wq, peer_keys, peer_u, peer_v):
    for l in range(DEPTH):
        xn = rms_norm_2(x, norm1_g[l]).astype(x.dtype)
        x = x + mixing_sublayer(xn, w_in[l], sb_qn_g[l], sb_kn_g[l], ml_conv_w[l], ml_conv_b[l],
                                ml_i_b[l], ml_f_b[l], sg_vn_g[l], sg_w[l], sg_b[l], out_g[l],
                                w_out[l]).astype(x.dtype)
        xn = rms_norm_2(x, norm2_g[l]).astype(x.dtype)
        x = x + peer_ffn(xn, peer_wq[l], peer_keys[l], peer_u[l], peer_v[l]).astype(x.dtype)
    return x


def setup_inputs(seed=0):
    out = dict(first_inputs(seed))
    for name, value in second_inputs(seed + 1).items():
        if name != "x":
            out[name + "_2"] = value
    return out


def reference(
    x, c, ctx, c_ctx, w_mod, b_mod, norm_mix, norm_ffn, w_in, attn_sink, pool_w, pool_scale,
    w_br_attn, w_br_pool, w_br_four, w_out, w_up, conv_w, w_down, norm_final, norm1_g_2, w_in_2,
    sb_qn_g_2, sb_kn_g_2, ml_conv_w_2, ml_conv_b_2, ml_i_b_2, ml_f_b_2, sg_vn_g_2, sg_w_2,
    sg_b_2, out_g_2, w_out_2, norm2_g_2, peer_wq_2, peer_keys_2, peer_u_2, peer_v_2,
):
    x = first_block(
        x, c, ctx, c_ctx, w_mod, b_mod, norm_mix, norm_ffn, w_in, attn_sink, pool_w, pool_scale,
        w_br_attn, w_br_pool, w_br_four, w_out, w_up, conv_w, w_down, norm_final,
    )
    return second_block(
        x, norm1_g_2, w_in_2, sb_qn_g_2, sb_kn_g_2, ml_conv_w_2, ml_conv_b_2, ml_i_b_2,
        ml_f_b_2, sg_vn_g_2, sg_w_2, sg_b_2, out_g_2, w_out_2, norm2_g_2, peer_wq_2,
        peer_keys_2, peer_u_2, peer_v_2,
    )


_drawn_inputs = setup_inputs


def setup_inputs(seed=0):
    import zlib

    import numpy as np

    out = dict(_drawn_inputs(seed))
    spreads = {}
    factors = {'norm_mix': 6.584,
     'norm_ffn': 4.757,
     'attn_sink': 8.0,
     'pool_scale': 8.0,
     'sb_qn_g_2': 8.0,
     'sb_kn_g_2': 8.0,
     'ml_conv_b_2': 5.863,
     'ml_i_b_2': 64.0,
     'sg_vn_g_2': 8.0,
     'sg_b_2': 8.0,
     'out_g_2': 2.893,
     'norm2_g_2': 8.0}
    for name, (base, spread) in spreads.items():
        noise = np.random.default_rng([zlib.crc32(name.encode()), seed]).standard_normal(out[name].shape)
        drawn = base * np.exp(spread * noise) if base else spread * noise
        out[name] = __import__('jax').numpy.asarray(drawn.astype(out[name].dtype))
    for name, factor in factors.items():
        out[name] = (out[name] * factor).astype(out[name].dtype)
    return out
```

```python
from contextlib import ExitStack, contextmanager

import concourse.bass as bass
import numpy as np
from concourse import mybir

F32 = mybir.dt.float32
U32 = mybir.dt.uint32
ALU = mybir.AluOpType
ACT = mybir.ActivationFunctionType
AX_X = mybir.AxisListType.X

P = 128
D = 1024
DC = D // P
DEPTH = 2
SEQ = 256
CTX = 256
TB = SEQ // P
EPS = 1e-6
MASKED = -1e30

HD = 64
QH, KVH = 8, 2
QW, KW = QH * HD, KVH * HD
WINDOW, GRID_W, ROPE_BASE = 128, 64, 10000.0
POOL_WINDOWS = (2, 4, 8, 16)
POOLW = len(POOL_WINDOWS) * HD
FOURW = 4 * HD
FF = 2816
FC = FF // P
NMOD = 6
NATURAL = KW + POOLW + FOURW
QC = QW // P

SBH, MLH, SGG = 6, 6, 4
SBW, MLW, SGW = SBH * HD, MLH * HD, SGG * HD
ML_CONV = 4
NATURAL2 = SBW + MLW + SGW
ZQ, ZK, ZMQ, ZMK, ZO, ZU = 0, 3, 6, 9, 12, 15
ZC = 17
YML, YSG = 3, 6
PH, NK, TOPK = 8, 128, 16
HC = 2 * PH
SLOTS = PH * TOPK

RING = 8


def offsets(*parts):
    at, out = 0, {}
    for name, width in parts:
        out[name] = (at, width)
        at += width
    return out, at


CONST, CONST_W = offsets(
    ("ident", P), ("ones", P), ("half_ones", P), ("suffix", P), ("iota", NK), ("causal", P),
    ("before", 3 * P), ("not_before", 3 * P), ("ahead", 2 * P), ("row_of_head", MLH * P),
    ("row_of_pair", MLH // 2 * P))
CONST1, CONST1_W = offsets(
    ("rope_swap", P), ("rope_cos", SEQ + CTX), ("rope_sin", SEQ + CTX), ("window", TB * 2 * SEQ),
    ("pool", TB * len(POOL_WINDOWS) * SEQ), ("dft_time", TB * 2 * SEQ), ("dft_chan", 2 * P))
SMALL1, SMALL1_W = offsets(
    ("b_mod", NMOD * DC * 2), ("norm_mix", DC * 2), ("norm_ffn", DC * 2), ("sink", QH),
    ("pool_w", 2 * HD), ("pool_scale", 2), ("conv_w", 3 * 2 * FC))
SMALL2, SMALL2_W = offsets(
    ("norm1", DC), ("norm2", DC), ("qn_g", 1), ("kn_g", 1), ("conv_w", 6 * ML_CONV), ("conv_b", 6),
    ("out_g", DC), ("if_b", 2), ("vn_g", SGW), ("sg_b", SGG * P), ("sg_w", SGG * P),
    ("w_if", DC * 2 * MLH))


@contextmanager
def stage(nc, *names):
    sems, every = [], []
    for name in names:
        base, _, n = name.partition("*")
        made = [nc.alloc_semaphore(f"{base}_{nc.next_id()}") for _ in range(int(n or 1))]
        every += made
        sems.append(made if n else made[0])
    with nc.Block(no_gpsimd_drain=True) as block:
        yield (block, *sems)
    nc.clear_and_free_semaphores(every)
    nc.all_engine_barrier(sem_only=True)


class Steps:

    def __init__(self, eng, sem, done=0):
        self.eng, self.sem, self.done = eng, sem, done

    def step(self, ins):
        ins.then_inc(self.sem, 1)
        self.done = self.done + 1
        return ins

    def settle(self):
        self.eng.wait_ge(self.sem, self.done)

    def __call__(self, ins):
        self.step(ins)
        self.settle()


def tile(dram, n):
    return dram[bass.ds(n, 1)].rearrange("a p m -> p (a m)")


def one(ap, n):
    return ap[:, bass.ds(n, 1), :].rearrange("p a m -> p (a m)")




def load_stage(k, pairs):
    with stage(k.nc, "loaded") as (block, loaded):

        @block.sync
        def _(sp):
            for out, src in pairs:
                sp.dma_start(out, src).then_inc(loaded, 16)
            sp.wait_ge(loaded, 16 * len(pairs))


def norm_stage(k, tokens, gain, shift, xT, hT):
    nc, streams = k.nc, range(tokens // SEQ)
    total = k.ps[:, 0, 0:tokens]
    rstd = k.rstd[:, 0:tokens]
    with stage(nc, "squared", "summed", "var_ready", "rooted", "scaled", "shifted") as (
            block, squared, summed, var_ready, rooted, scaled, shifted):

        @block.scalar
        def _(act):
            for c in range(DC):
                nc.scalar.activation(hT[:, c, 0:tokens], xT[:, c, 0:tokens], ACT.Square).then_inc(squared, 1)
            act.wait_ge(var_ready, 1)
            nc.scalar.activation(rstd, rstd, ACT.Sqrt).then_inc(rooted, 1)
            if shift is not None:
                for c in range(DC):
                    for s in streams:
                        h = hT[:, c, s * SEQ:(s + 1) * SEQ]
                        act.wait_ge(scaled, c * len(streams) + s + 1)
                        nc.scalar.activation(h, h, ACT.Identity, bias=shift(c, s)).then_inc(shifted, 1)

        @block.tensor
        def _(pe):
            for c in range(DC):
                pe.wait_ge(squared, c + 1)
                last = nc.tensor.matmul(total, k.const("ones"), hT[:, c, 0:tokens], start=c == 0, stop=c == DC - 1)
            last.then_inc(summed, 1)

        @block.vector
        def _(dve):
            dve.wait_ge(summed, 1)
            nc.vector.tensor_scalar(rstd, total, 1.0 / D, EPS, ALU.mult, ALU.add).then_inc(var_ready, 1)
            dve.wait_ge(rooted, 1)
            nc.vector.reciprocal(rstd, rstd).then_inc(var_ready, 1)
            dve.wait_ge(var_ready, 2)
            for c in range(DC):
                for s in streams:
                    sl = slice(s * SEQ, (s + 1) * SEQ)
                    nc.vector.scalar_tensor_tensor(hT[:, c, sl], xT[:, c, sl], gain(c, s), k.rstd[:, sl],
                                                   ALU.mult, ALU.mult).then_inc(scaled, 1)


def residual_stage(k, tokens, weights, base, chunks, src, gate, xT):
    nc, streams = k.nc, range(tokens // SEQ)
    width = chunks * P
    slots = 2 if chunks > DC else 4
    ring = k.ring.rearrange("p s m -> p (s m)")[:, 0:slots * width].rearrange("p (s m) -> p s m", s=slots)
    with stage(nc, f"weights*{slots}", "summed", "added") as (block, weights_in, summed, added):

        @block.sync
        def _(sp):
            for s in range(slots):
                sp.dma_start(ring[:, s], tile(weights, base + s)).then_inc(weights_in[s], 16)
            with sp.Fori(1, DC // slots) as i:
                for s in range(slots):
                    sp.wait_ge(summed, (i - 1) * slots + s + 1)
                    sp.dma_start(ring[:, s], tile(weights, base + i * slots + s)).then_inc(weights_in[s], 16)

        @block.tensor
        def _(pe):
            with pe.Fori(0, DC // slots) as i:
                for s in range(slots):
                    pe.wait_ge(weights_in[s], i * 16 + 16)
                    for c in range(chunks):
                        last = nc.tensor.matmul(one(k.ps, i * slots + s)[:, 0:tokens], ring[:, s, c * P:(c + 1) * P],
                                                src[:, c, 0:tokens], start=c == 0, stop=c == chunks - 1)
                    last.then_inc(summed, 1)

        @block.vector
        def _(dve):
            for n in range(DC):
                dve.wait_ge(summed, n + 1)
                for s in streams:
                    x = xT[:, n, s * SEQ:(s + 1) * SEQ]
                    add = k.ps[:, n, s * SEQ:(s + 1) * SEQ]
                    if gate is None:
                        nc.vector.tensor_tensor(x, x, add, ALU.add).then_inc(added, 1)
                    else:
                        nc.vector.scalar_tensor_tensor(x, add, gate(n, s), x, ALU.mult, ALU.add).then_inc(added, 1)




def mod_stage(k, l):
    nc, slots, tiles = k.nc, 8, NMOD * DC
    sums = k.ps[:, 0, 0:2 * tiles].rearrange("p (n c) -> p n c", c=2)
    with stage(nc, f"weights*{slots}", "silu_done", "summed", "mod_done") as (
            block, weights_in, silu_done, summed, mod_done):

        @block.sync
        def _(sp):
            for s in range(slots):
                sp.dma_start(k.ring[:, s], k.w_mod[l * tiles + s]).then_inc(weights_in[s], 16)
            with sp.Fori(1, tiles // slots) as i:
                for s in range(slots):
                    sp.wait_ge(summed, (i - 1) * slots + s + 1)
                    sp.dma_start(k.ring[:, s], tile(k.w_mod, l * tiles + i * slots + s)).then_inc(weights_in[s], 16)

        @block.scalar
        def _(act):
            nc.scalar.activation(k.cond_silu[:, :], k.cond[:, :], ACT.Silu).then_inc(silu_done, 1)

        @block.tensor
        def _(pe):
            pe.wait_ge(silu_done, 1)
            with pe.Fori(0, tiles // slots) as i:
                for s in range(slots):
                    pe.wait_ge(weights_in[s], i * 16 + 16)
                    for c in range(DC):
                        last = nc.tensor.matmul(one(sums, i * slots + s), k.ring[:, s, c * P:(c + 1) * P],
                                                k.cond_silu[:, 2 * c:2 * c + 2], start=c == 0, stop=c == DC - 1)
                    last.then_inc(summed, 1)

        @block.vector
        def _(dve):
            done = Steps(dve, mod_done)
            dve.wait_ge(summed, tiles)
            mod = k.mod.rearrange("p n c -> p (n c)")
            done(nc.vector.tensor_tensor(mod, k.ps[:, 0, 0:2 * tiles], k.small1("b_mod"), ALU.add))
            for norm, scale in (("norm_mix", 1), ("norm_ffn", 4)):
                sc = mod[:, scale * DC * 2:(scale + 1) * DC * 2]
                done(nc.vector.scalar_tensor_tensor(sc, sc, 1.0, k.small1(norm), ALU.add, ALU.mult))


def qk_stage(k, l, q_tokens):
    nc, n = k.nc, 1 + QC
    tokens = [SEQ + CTX] + [q_tokens] * QC
    raw, rot = k.ps[:, 0:2, :], k.ps[:, 2:4, :]
    with stage(nc, f"weights*{n}", "summed", "copied", "swapped", "rotated") as (
            block, weights_in, summed, copied, swapped, rotated):

        @block.sync
        def _(sp):
            for j in range(n):
                sp.dma_start(k.ring[:, j], k.w_qk[l * n + j]).then_inc(weights_in[j], 16)

        @block.tensor
        def _(pe):
            def swap(j):
                pe.wait_ge(copied, j + 1)
                if j >= 2:
                    pe.wait_ge(rotated, 3 * (j - 2) + 2)
                nc.tensor.matmul(rot[:, j % 2, 0:tokens[j]], k.const1("rope_swap"), k.qkT[:, j, 0:tokens[j]],
                                 start=True, stop=True).then_inc(swapped, 1)

            for j in range(n):
                pe.wait_ge(weights_in[j], 16)
                if j >= 2:
                    pe.wait_ge(copied, j - 1)
                for c in range(DC):
                    last = nc.tensor.matmul(raw[:, j % 2, 0:tokens[j]], k.ring[:, j, c * P:(c + 1) * P],
                                            k.hT[:, c, 0:tokens[j]], start=c == 0, stop=c == DC - 1)
                last.then_inc(summed, 1)
                if j >= 1:
                    swap(j - 1)
            swap(n - 1)

        @block.scalar
        def _(act):
            for j in range(n):
                act.wait_ge(summed, j + 1)
                nc.scalar.activation(k.qkT[:, j, 0:tokens[j]], raw[:, j % 2, 0:tokens[j]], ACT.Copy).then_inc(copied, 1)

        @block.vector
        def _(dve):
            done = Steps(dve, rotated)
            for j in range(n):
                t = slice(0, tokens[j])
                dve.wait_ge(swapped, j + 1)
                done(nc.vector.tensor_tensor(k.qkT[:, j, t], k.qkT[:, j, t], k.const1("rope_cos")[:, t], ALU.mult))
                done(nc.vector.tensor_tensor(k.rstd[:, t], rot[:, j % 2, t], k.const1("rope_sin")[:, t], ALU.mult))
                done(nc.vector.tensor_tensor(k.qkT[:, j, t], k.qkT[:, j, t], k.rstd[:, t], ALU.add))


def natural_stage(k, l, q_tokens):
    nc, half = k.nc, NATURAL // 2
    blocks = (SEQ + CTX) // P
    full = q_tokens // P
    with stage(nc, f"weights*{DC}", "summed", "copied") as (block, weights_in, summed, copied):

        @block.sync
        def _(sp):
            for c in range(DC):
                sp.dma_start(k.ring[:, c, 0:NATURAL], k.w_natural[l * DC + c]).then_inc(weights_in[c], 16)

        @block.tensor
        def _(pe):
            for c in range(DC):
                pe.wait_ge(weights_in[c], 16)
                for b in range(blocks):
                    for h in range(2 if b < full else 1):
                        cols = half if b < full else KW
                        last = nc.tensor.matmul(k.ps[:, 2 * b + h, 0:cols], k.hT[:, c, b * P:(b + 1) * P],
                                                k.ring[:, c, h * half:h * half + cols], start=c == 0, stop=c == DC - 1)
            last.then_inc(summed, 1)

        @block.scalar
        def _(act):
            act.wait_ge(summed, 1)
            for b in range(blocks):
                for h in range(2 if b < full else 1):
                    cols = half if b < full else KW
                    nc.scalar.activation(k.natural[:, b, h * half:h * half + cols], k.ps[:, 2 * b + h, 0:cols],
                                         ACT.Copy).then_inc(copied, 1)


def attention_stage(k, q_tokens):
    nc, keys = k.nc, SEQ + CTX
    units = [(b, h) for b in range(q_tokens // P) for h in range(QH)]
    scale = float(HD) ** -0.5

    def first_key(b):
        return 0 if b < TB else SEQ

    with stage(nc, "scored", "masked", "max_ready", "exp_ready", "norm_step", "probs_ready", "turned",
               "probs_turned", "weighed", "kept") as (
            block, scored, masked, max_ready, exp_ready, norm_step, probs_ready, turned, probs_turned, weighed, kept):

        @block.tensor
        def _(pe):
            def score(u):
                b, h = units[u]
                base = HD * (h // QC)
                if u >= 2:
                    pe.wait_ge(masked, u - 1)
                nc.tensor.matmul(k.ps[:, u % 2, first_key(b):keys], k.qkT[base:base + HD, 1 + h % QC, b * P:(b + 1) * P],
                                 k.qkT[base:base + HD, 0, first_key(b):keys], start=True, stop=True).then_inc(scored, 1)

            def turn(u):
                b, _ = units[u]
                pe.wait_ge(probs_ready, u + 1)
                if u >= 2:
                    pe.wait_ge(probs_turned, u - 1)
                for j in range(first_key(b) // P, keys // P):
                    last = nc.tensor.transpose(k.ps[:, 2 + u % 2, j * P:(j + 1) * P],
                                               k.probs[:, u % 2, j * P:(j + 1) * P], k.const("ident"))
                last.then_inc(turned, 1)

            def weigh(u):
                b, h = units[u]
                base = HD * (h // QC)
                pe.wait_ge(probs_turned, u + 1)
                if u >= 2:
                    pe.wait_ge(kept, u - 1)
                first = first_key(b) // P
                for j in range(first, keys // P):
                    last = nc.tensor.matmul(k.ps[base:base + HD, 4 + u % 2, 0:P], k.natural[:, j, base:base + HD],
                                            k.probsT[:, u % 2, j * P:(j + 1) * P], start=j == first, stop=j == keys // P - 1)
                last.then_inc(weighed, 1)

            score(0)
            for u in range(len(units)):
                if u + 1 < len(units):
                    score(u + 1)
                turn(u)
                if u >= 1:
                    weigh(u - 1)
            weigh(len(units) - 1)

        @block.vector
        def _(dve):
            def soften(u):
                b, h = units[u]
                cols = slice(first_key(b), keys)
                s = k.scores[:, u % 2, cols]
                m = k.stat[:, u % 2, 0:1]
                dve.wait_ge(scored, u + 1)
                if u >= 2:
                    dve.wait_ge(exp_ready, 2 * (u - 1))
                nc.vector.scalar_tensor_tensor(s, k.ps[:, u % 2, cols], scale,
                                               k.const1("window")[:, (b % TB) * 2 * SEQ:(b % TB + 1) * 2 * SEQ][:, cols],
                                               ALU.mult, ALU.add).then_inc(masked, 1)
                dve.wait_ge(masked, u + 1)
                nc.vector.reduce_max(m, s, AX_X).then_inc(max_ready, 1)
                dve.wait_ge(max_ready, 2 * u + 1)
                nc.vector.tensor_scalar(m, m, k.small1("sink")[:, h:h + 1], -1.0, ALU.max, ALU.mult).then_inc(max_ready, 1)

            def normalise(u):
                b, _ = units[u]
                cols = slice(first_key(b), keys)
                den = k.stat[:, u % 2, 3:4]
                dve.wait_ge(exp_ready, 2 * u + 2)
                nc.vector.tensor_tensor(den, k.stat[:, u % 2, 1:2], k.stat[:, u % 2, 2:3], ALU.add).then_inc(norm_step, 1)
                dve.wait_ge(norm_step, 2 * u + 1)
                nc.vector.reciprocal(den, den).then_inc(norm_step, 1)
                dve.wait_ge(norm_step, 2 * u + 2)
                if u >= 2:
                    dve.wait_ge(turned, u - 1)
                nc.vector.tensor_scalar(k.probs[:, u % 2, cols], k.exps[:, u % 2, cols], den, None,
                                        ALU.mult).then_inc(probs_ready, 1)

            def keep(u):
                b, h = units[u]
                base = HD * (h // QC)
                dve.wait_ge(weighed, u + 1)
                nc.vector.tensor_copy(k.branchT[base:base + HD, h % QC, b * P:(b + 1) * P],
                                      k.ps[base:base + HD, 4 + u % 2, 0:P]).then_inc(kept, 1)

            soften(0)
            for u in range(len(units)):
                if u + 1 < len(units):
                    soften(u + 1)
                normalise(u)
                if u >= 2:
                    keep(u - 2)
            keep(len(units) - 2)
            keep(len(units) - 1)

        @block.scalar
        def _(act):
            def exponents(u):
                b, h = units[u]
                cols = slice(first_key(b), keys)
                neg_max = k.stat[:, u % 2, 0:1]
                act.wait_ge(max_ready, 2 * u + 2)
                if u >= 2:
                    act.wait_ge(probs_ready, u - 1)
                nc.scalar.activation(k.exps[:, u % 2, cols], k.scores[:, u % 2, cols], ACT.Exp, bias=neg_max,
                                     accum_out=k.stat[:, u % 2, 1:2]).then_inc(exp_ready, 1)
                nc.scalar.activation(k.stat[:, u % 2, 2:3], k.small1("sink")[:, h:h + 1], ACT.Exp,
                                     bias=neg_max).then_inc(exp_ready, 1)

            def copy_turned(u):
                b, _ = units[u]
                cols = slice(first_key(b), keys)
                act.wait_ge(turned, u + 1)
                if u >= 2:
                    act.wait_ge(weighed, u - 1)
                nc.scalar.activation(k.probsT[:, u % 2, cols], k.ps[:, 2 + u % 2, cols], ACT.Copy).then_inc(probs_turned, 1)

            exponents(0)
            for u in range(len(units)):
                if u + 1 < len(units):
                    exponents(u + 1)
                copy_turned(u)


def pool_fourier_stage(k, q_tokens):
    nc, groups = k.nc, len(POOL_WINDOWS)
    pool = k.const1("pool").rearrange("p (b g t) -> p b g t", b=TB, g=groups)
    dft = k.const1("dft_time").rearrange("p (b t) -> p b t", b=TB)
    pool_w = k.small1("pool_w").rearrange("p (a d) -> p a d", a=2)
    streams = range(q_tokens // SEQ)
    n = 2 * len(streams)
    with stage(nc, "pooled", "pool_kept", "pool_mixed", "pool_scaled", "timed", "time_kept", "channeled", "four_kept") as (
            block, pooled, pool_kept, pool_mixed, pool_scaled, timed, time_kept, channeled, four_kept):

        @block.tensor
        def _(pe):
            for u in range(n):
                s, a = u // 2, u % 2
                if u >= 2:
                    pe.wait_ge(pool_kept, u - 1)
                for half in range(2):
                    g = 2 * a + half
                    for b in range(TB):
                        last = nc.tensor.matmul(k.ps[HD * half:HD * (half + 1), a, 0:SEQ],
                                                k.natural[:, s * TB + b, KW + g * HD:KW + (g + 1) * HD],
                                                pool[:, b, g, :], start=b == 0, stop=b == TB - 1)
                last.then_inc(pooled, 1)
                if u >= 2:
                    pe.wait_ge(time_kept, u - 1)
                for b in range(TB):
                    last = nc.tensor.matmul(k.ps[:, 2 + a, :], k.natural[:, s * TB + b, KW + POOLW + a * P:KW + POOLW + (a + 1) * P],
                                            dft[:, b, :], start=b == 0, stop=b == TB - 1)
                last.then_inc(timed, 1)
            for u in range(n):
                a = u % 2
                pe.wait_ge(pool_kept, u + 1)
                if u >= 2:
                    pe.wait_ge(pool_scaled, u - 1)
                for half in range(2):
                    rows = slice(HD * half, HD * (half + 1))
                    last = nc.tensor.matmul(k.ps[rows, 4 + a, 0:SEQ], pool_w[rows, a, :], k.pooledT[rows, u, :],
                                            start=True, stop=True)
                last.then_inc(pool_mixed, 1)
                pe.wait_ge(time_kept, u + 1)
                if u >= 2:
                    pe.wait_ge(four_kept, u - 1)
                for part in range(2):
                    last = nc.tensor.matmul(k.ps[:, 6 + a, 0:SEQ], k.const1("dft_chan")[:, part * P:(part + 1) * P],
                                            k.timedT[:, u, part * SEQ:(part + 1) * SEQ], start=part == 0, stop=part == 1)
                last.then_inc(channeled, 1)

        @block.vector
        def _(dve):
            for u in range(n):
                dve.wait_ge(pooled, u + 1)
                nc.vector.tensor_copy(k.pooledT[:, u, :], k.ps[:, u % 2, 0:SEQ]).then_inc(pool_kept, 1)
            for u in range(n):
                s, a = u // 2, u % 2
                dve.wait_ge(pool_mixed, u + 1)
                nc.vector.tensor_scalar(k.branchT[:, QC + a, s * SEQ:(s + 1) * SEQ], k.ps[:, 4 + a, 0:SEQ],
                                        k.small1("pool_scale")[:, a:a + 1], None, ALU.mult).then_inc(pool_scaled, 1)

        @block.scalar
        def _(act):
            for u in range(n):
                act.wait_ge(timed, u + 1)
                nc.scalar.activation(k.timedT[:, u, :], k.ps[:, 2 + u % 2, :], ACT.Copy).then_inc(time_kept, 1)
            for u in range(n):
                s, a = u // 2, u % 2
                act.wait_ge(channeled, u + 1)
                nc.scalar.activation(k.branchT[:, QC + 2 + a, s * SEQ:(s + 1) * SEQ], k.ps[:, 6 + a, 0:SEQ],
                                     ACT.Copy).then_inc(four_kept, 1)


def merge_stage(k, l, tokens):
    nc = k.nc
    gates, parts = 3, ((0, QC), (QC, QC + 2), (QC + 2, DC))
    t = slice(0, tokens)
    with stage(nc, f"weights*{gates + 1}", "gate_summed", "gate_ready", "branch_summed", "product",
               "merged") as (block, weights_in, gate_summed, gate_ready, branch_summed, product, merged):

        @block.sync
        def _(sp):
            for s in range(gates + 1):
                sp.dma_start(k.ring[:, s], k.w_merge[l * DC * 4 + s]).then_inc(weights_in[s], 16)
            with sp.Fori(1, DC) as n:
                for s in range(gates + 1):
                    if s < gates:
                        sp.wait_ge(gate_summed, (n - 1) * gates + s + 1)
                    else:
                        sp.wait_ge(branch_summed, n * gates)
                    sp.dma_start(k.ring[:, s], tile(k.w_merge, l * DC * 4 + n * 4 + s)).then_inc(weights_in[s], 16)

        @block.tensor
        def _(pe):
            with pe.Fori(0, DC) as n:
                for g in range(gates):
                    pe.wait_ge(weights_in[g], n * 16 + 16)
                    pe.wait_ge(gate_ready, n * gates + g + 1)
                    for c in range(DC):
                        last = nc.tensor.matmul(k.ps[:, g, t], k.ring[:, g, c * P:(c + 1) * P], k.hT[:, c, t],
                                                start=c == 0, stop=c == DC - 1)
                    last.then_inc(gate_summed, 1)
                pe.wait_ge(weights_in[gates], n * 16 + 16)
                for g, (first, end) in enumerate(parts):
                    pe.wait_ge(product, n * gates + g + 1)
                    for c in range(first, end):
                        last = nc.tensor.matmul(k.ps[:, gates + g, t], k.ring[:, gates, c * P:(c + 1) * P],
                                                k.branchT[:, c, t], start=c == first, stop=c == end - 1)
                    last.then_inc(branch_summed, 1)

        @block.scalar
        def _(act):
            for g in range(gates):
                act.sem_inc(gate_ready, 1)
            with act.Fori(0, DC) as n:
                for g in range(gates):
                    act.wait_ge(gate_summed, n * gates + g + 1)
                    act.wait_ge(product, n * gates + g + 1)
                    nc.scalar.activation(k.gate[:, g, t], k.ps[:, g, t], ACT.Sigmoid).then_inc(gate_ready, 1)

        @block.vector
        def _(dve):
            for g in range(gates):
                dve.sem_inc(product, 1)
            with dve.Fori(0, DC) as n:
                for g in range(gates):
                    dve.wait_ge(branch_summed, n * gates + g + 1)
                    dve.wait_ge(gate_ready, (n + 1) * gates + g + 1)
                    out = one(k.yT, n)[:, t] if g == 0 else k.part[:, t]
                    if g == 2:
                        dve.wait_ge(merged, n * 2 + 1)
                    nc.vector.tensor_tensor(out, k.gate[:, g, t], k.ps[:, gates + g, t], ALU.mult).then_inc(product, 1)
                    if g:
                        dve.wait_ge(product, (n + 1) * gates + g + 1)
                        y = one(k.yT, n)[:, t]
                        nc.vector.tensor_tensor(y, y, k.part[:, t], ALU.add).then_inc(merged, 1)
                        dve.wait_ge(merged, n * 2 + g)


def ffn_up_stage(k, l, tokens):
    nc, streams = k.nc, tokens // SEQ
    t = slice(0, tokens)
    turns = FC // 2
    conv_w = k.small1("conv_w").rearrange("p (w n) -> p w n", w=3)
    with stage(nc, "weights*4", "summed", "centred", "convolved", "activated", "finished") as (
            block, weights_in, summed, centred, convolved, activated, finished):

        @block.sync
        def _(sp):
            for s in range(4):
                sp.dma_start(k.ring[:, s], k.w_up[l * 2 * FC + s]).then_inc(weights_in[s], 16)
            with sp.Fori(1, turns) as i:
                for s in range(4):
                    sp.wait_ge(summed, (i - 1) * 4 + s + 1)
                    sp.dma_start(k.ring[:, s], tile(k.w_up, l * 2 * FC + i * 4 + s)).then_inc(weights_in[s], 16)

        @block.tensor
        def _(pe):
            with pe.Fori(0, turns) as i:
                for s in range(4):
                    pe.wait_ge(weights_in[s], i * 16 + 16)
                    pe.wait_ge(convolved, (i * 4 + s) * 2 + 2)
                    for c in range(DC):
                        last = nc.tensor.matmul(k.ps[:, s, t], k.ring[:, s, c * P:(c + 1) * P], k.hT[:, c, t],
                                                start=c == 0, stop=c == DC - 1)
                    last.then_inc(summed, 1)

        @block.scalar
        def _(act):
            with act.Fori(0, turns) as i:
                for s in range(4):
                    act.wait_ge(summed, i * 4 + s + 1)
                    act.wait_ge(finished, i * 2 + s // 2 + 1)
                    nc.scalar.activation(k.conv[:, s, t], k.ps[:, s, t], ACT.Copy,
                                         scale=one(conv_w, 1)[:, bass.ds(i * 4 + s, 1)]).then_inc(centred, 1)
                    if s % 2:
                        act.wait_ge(convolved, (i * 4 + s) * 2 + 10)
                        nc.scalar.activation(k.conv[:, s, t], k.conv[:, s, t], ACT.Silu).then_inc(activated, 1)

        @block.vector
        def _(dve):
            for s in range(8):
                dve.sem_inc(convolved, 1)
            for s in range(2):
                dve.sem_inc(finished, 1)
            with dve.Fori(0, turns) as i:
                for s in range(4):
                    u = k.ps[:, s, t].rearrange("p (a t) -> p a t", a=streams)
                    a = k.conv[:, s, t].rearrange("p (a t) -> p a t", a=streams)
                    dve.wait_ge(centred, i * 4 + s + 1)
                    nc.vector.scalar_tensor_tensor(a[:, :, 1:SEQ], u[:, :, 0:SEQ - 1],
                                                   one(conv_w, 0)[:, bass.ds(i * 4 + s, 1)], a[:, :, 1:SEQ],
                                                   ALU.mult, ALU.add).then_inc(convolved, 1)
                    dve.wait_ge(convolved, (i * 4 + s) * 2 + 9)
                    nc.vector.scalar_tensor_tensor(a[:, :, 0:SEQ - 1], u[:, :, 1:SEQ],
                                                   one(conv_w, 2)[:, bass.ds(i * 4 + s, 1)], a[:, :, 0:SEQ - 1],
                                                   ALU.mult, ALU.add).then_inc(convolved, 1)
                    if s % 2:
                        dve.wait_ge(activated, i * 2 + s // 2 + 1)
                        nc.vector.tensor_tensor(one(k.actT, i * 2 + s // 2)[:, t], k.conv[:, s - 1, t], k.conv[:, s, t],
                                                ALU.mult).then_inc(finished, 1)


def first_block(k):
    for l in range(DEPTH):
        tokens = SEQ if l == DEPTH - 1 else SEQ + CTX
        load_stage(k, [(k.small1_sb[:, :], k.small1_dram[l])])
        mod_stage(k, l)

        def part(m):
            return lambda c, s: k.mod[:, m * DC + c, s:s + 1]

        norm_stage(k, SEQ + CTX, part(1), part(0), k.xT, k.hT)
        qk_stage(k, l, tokens)
        natural_stage(k, l, tokens)
        attention_stage(k, tokens)
        pool_fourier_stage(k, tokens)
        merge_stage(k, l, tokens)
        residual_stage(k, tokens, k.w_out, l * DC, DC, k.yT, part(2), k.xT)
        norm_stage(k, tokens, part(4), part(3), k.xT, k.hT)
        ffn_up_stage(k, l, tokens)
        residual_stage(k, tokens, k.w_down, l * DC, FC, k.actT, part(5), k.xT)
    norm_stage(k, SEQ, lambda c, s: k.norm_final[:, c:c + 1], None, k.xT, k.x2T)




def transposed_stage(k, weights, base, tiles, dst):
    nc, slots = k.nc, 4
    turns, rest = tiles // slots, tiles % slots
    with stage(nc, f"weights*{slots}", "summed", "copied") as (block, weights_in, summed, copied):

        @block.sync
        def _(sp):
            for s in range(slots):
                sp.dma_start(k.ring[:, s], tile(weights, base + s)).then_inc(weights_in[s], 16)
            with sp.Fori(1, turns) as i:
                for s in range(slots):
                    sp.wait_ge(summed, (i - 1) * slots + s + 1)
                    sp.dma_start(k.ring[:, s], tile(weights, base + i * slots + s)).then_inc(weights_in[s], 16)
            for s in range(rest):
                sp.wait_ge(summed, (turns - 1) * slots + s + 1)
                sp.dma_start(k.ring[:, s], tile(weights, base + turns * slots + s)).then_inc(weights_in[s], 16)

        @block.tensor
        def _(pe):
            def product(i, s):
                pe.wait_ge(weights_in[s], i * 16 + 16)
                pe.wait_ge(copied, i * slots + s + 1)
                for c in range(DC):
                    last = nc.tensor.matmul(k.ps[:, s, 0:SEQ], k.ring[:, s, c * P:(c + 1) * P], k.hT[:, c, :],
                                            start=c == 0, stop=c == DC - 1)
                last.then_inc(summed, 1)

            with pe.Fori(0, turns) as i:
                for s in range(slots):
                    product(i, s)
            for s in range(rest):
                product(turns, s)

        @block.vector
        def _(dve):
            def copy(i, s):
                dve.wait_ge(summed, i * slots + s + 1)
                nc.vector.tensor_copy(one(dst, i * slots + s), k.ps[:, s, 0:SEQ]).then_inc(copied, 1)

            for s in range(slots):
                dve.sem_inc(copied, 1)
            with dve.Fori(0, turns) as i:
                for s in range(slots):
                    copy(i, s)
            for s in range(rest):
                copy(turns, s)


def natural2_stage(k, l):
    nc, half = k.nc, NATURAL2 // 2
    w_if = k.small2("w_if").rearrange("p (c n) -> p c n", c=DC)
    with stage(nc, f"weights*{DC}", "summed", "gates_summed", "copied") as (block, weights_in, summed, gates_summed, copied):

        @block.sync
        def _(sp):
            for c in range(DC):
                sp.dma_start(k.ring[:, c], tile(k.w_natural2, l * DC + c)).then_inc(weights_in[c], 16)

        @block.tensor
        def _(pe):
            for g in range(2):
                for c in range(DC):
                    last = nc.tensor.matmul(k.ps[0:MLH, 2 * TB + g, 0:SEQ], w_if[:, c, g * MLH:(g + 1) * MLH], k.hT[:, c, :],
                                            start=c == 0, stop=c == DC - 1)
            last.then_inc(gates_summed, 1)
            for c in range(DC):
                pe.wait_ge(weights_in[c], 16)
                for b in range(TB):
                    for h in range(2):
                        last = nc.tensor.matmul(k.ps[:, 2 * b + h, 0:half], k.hT[:, c, b * P:(b + 1) * P],
                                                k.ring[:, c, h * half:(h + 1) * half], start=c == 0, stop=c == DC - 1)
            last.then_inc(summed, 1)

        @block.scalar
        def _(act):
            act.wait_ge(summed, 1)
            for b in range(TB):
                for h in range(2):
                    nc.scalar.activation(k.natural2[:, b, h * half:(h + 1) * half], k.ps[:, 2 * b + h, 0:half],
                                         ACT.Copy).then_inc(copied, 1)

        @block.vector
        def _(dve):
            dve.wait_ge(gates_summed, 1)
            for g in range(2):
                nc.vector.tensor_scalar(k.gate_rows[0:MLH, g, :], k.ps[0:MLH, 2 * TB + g, 0:SEQ],
                                        k.small2("if_b")[0:MLH, g:g + 1], None, ALU.add).then_inc(copied, 1)


def head_norm_stage(k, src, chunks, gain):
    nc = k.nc
    squares, wide = k.squares[:, 0:chunks, :], 2 * SEQ
    flat = squares.rearrange("p c t -> p (c t)")
    parts = chunks * SEQ // wide
    sums = k.ps[:, 0:parts, :].rearrange("p b t -> p (b t)")
    with stage(nc, "squared", "summed", "var_ready", "rooted", "scaled") as (block, squared, summed, var_ready, rooted, scaled):

        @block.scalar
        def _(act):
            for n in range(parts):
                nc.scalar.activation(squares[:, 2 * n:2 * n + 2, :], src[:, 2 * n:2 * n + 2, :], ACT.Square).then_inc(squared, 1)
            act.wait_ge(var_ready, 1)
            nc.scalar.activation(flat, flat, ACT.Sqrt).then_inc(rooted, 1)

        @block.tensor
        def _(pe):
            for n in range(parts):
                pe.wait_ge(squared, n + 1)
                nc.tensor.matmul(k.ps[:, n, :], k.const("half_ones"), flat[:, n * wide:(n + 1) * wide],
                                 start=True, stop=True).then_inc(summed, 1)

        @block.vector
        def _(dve):
            dve.wait_ge(summed, parts)
            nc.vector.tensor_scalar(flat, sums, 1.0 / HD, EPS, ALU.mult, ALU.add).then_inc(var_ready, 1)
            dve.wait_ge(rooted, 1)
            nc.vector.reciprocal(flat, flat).then_inc(var_ready, 1)
            dve.wait_ge(var_ready, 2)
            for c in range(chunks):
                nc.vector.scalar_tensor_tensor(src[:, c, :], src[:, c, :], gain(c), squares[:, c, :],
                                               ALU.mult, ALU.mult).then_inc(scaled, 1)


def stick_breaking_stage(k):
    nc, width = k.nc, 3 * P
    half = SBH // 2 * width
    z, a, keep = k.z, k.z_abs, k.keep

    def flat(x, part):
        return x.rearrange("p h w -> p (h w)")[:, part * half:(part + 1) * half]

    with stage(nc, "scored", "score_kept", "magnitude", "log_ready", "keep_step", "suffixed", "exponent", "weights_ready",
               "weighed", "kept") as (
            block, scored, score_kept, magnitude, log_ready, keep_step, suffixed, exponent, weights_ready, weighed, kept):

        @block.tensor
        def _(pe):
            for h in range(SBH):
                base, c = HD * (h % 2), h // 2
                rows = slice(base, base + HD)
                if h >= 4:
                    pe.wait_ge(score_kept, h - 3)
                for b in range(TB):
                    last = nc.tensor.matmul(k.ps[:, h % 4, b * SEQ:b * SEQ + SEQ - b * P], k.zT[rows, ZK + c, b * P:(b + 1) * P],
                                            k.zT[rows, ZQ + c, b * P:SEQ], start=True, stop=True)
                last.then_inc(scored, 1)
            for h in range(SBH):
                pe.wait_ge(keep_step, 3 * (h // (SBH // 2)) + 3)
                if h >= 2:
                    pe.wait_ge(exponent, 2 * (h - 2) + 1)
                nc.tensor.matmul(k.ps[:, 4 + h % 2, 0:SEQ], k.const("suffix"), keep[:, h, 0:SEQ], start=True, stop=False)
                nc.tensor.matmul(k.ps[:, 4 + h % 2, P:SEQ], k.const("ones"), keep[:, h, SEQ:width], start=False, stop=True)
                nc.tensor.matmul(k.ps[:, 4 + h % 2, SEQ:width], k.const("suffix"), keep[:, h, SEQ:width],
                                 start=True, stop=True).then_inc(suffixed, 1)
            for h in range(SBH):
                base, c = HD * (h % 2), h // 2
                out = k.ps[base:base + HD, 6 + c % 2, 0:SEQ]
                pe.wait_ge(weights_ready, h + 1)
                if h >= 4:
                    pe.wait_ge(kept, h // 2 - 1)
                cols = slice(h * HD, (h + 1) * HD)
                nc.tensor.matmul(out, k.natural2[:, 0, cols], a[:, h, 0:SEQ], start=True, stop=False)
                nc.tensor.matmul(out[:, P:SEQ], k.natural2[:, 1, cols], a[:, h, SEQ:width],
                                 start=False, stop=True).then_inc(weighed, 1)

        @block.scalar
        def _(act):
            for h in range(SBH):
                act.wait_ge(scored, h + 1)
                nc.scalar.activation(z[:, h, :], k.ps[:, h % 4, 0:width], ACT.Copy,
                                     scale=float(HD) ** -0.5).then_inc(score_kept, 1)
            for part in range(2):
                act.wait_ge(score_kept, (part + 1) * SBH // 2)
                nc.scalar.activation(flat(a, part), flat(z, part), ACT.Abs).then_inc(magnitude, 1)
            for part in range(2):
                act.wait_ge(magnitude, part + 1)
                nc.scalar.activation(flat(a, part), flat(a, part), ACT.Exp, scale=-1.0).then_inc(magnitude, 1)
                act.wait_ge(magnitude, part + 3)
                nc.scalar.activation(flat(a, part), flat(a, part), ACT.Ln, bias=1.0).then_inc(log_ready, 1)
            for h in range(SBH):
                act.wait_ge(exponent, 2 * h + 2)
                nc.scalar.activation(a[:, h, :], k.arg[:, h, :], ACT.Exp).then_inc(weights_ready, 1)

        @block.vector
        def _(dve):
            for part in range(2):
                n = 3 * part
                dve.wait_ge(score_kept, (part + 1) * SBH // 2)
                nc.vector.tensor_scalar(flat(keep, part), flat(z, part), -1.0, 0.0, ALU.mult, ALU.min).then_inc(keep_step, 1)
                dve.wait_ge(keep_step, n + 1)
                dve.wait_ge(log_ready, part + 1)
                nc.vector.tensor_tensor(flat(keep, part), flat(keep, part), flat(a, part), ALU.subtract).then_inc(keep_step, 1)
                dve.wait_ge(keep_step, n + 2)
                heads = slice(part * SBH // 2, (part + 1) * SBH // 2)
                nc.vector.tensor_tensor(keep[:, heads, :], keep[:, heads, :],
                                        k.const("before").unsqueeze(1).broadcast_to([P, SBH // 2, width]),
                                        ALU.mult).then_inc(keep_step, 1)
            for h in range(SBH):
                dve.wait_ge(suffixed, h + 1)
                nc.vector.tensor_tensor(k.arg[:, h, :], z[:, h, :], k.ps[:, 4 + h % 2, 0:width], ALU.add).then_inc(exponent, 1)
                dve.wait_ge(exponent, 2 * h + 1)
                nc.vector.tensor_tensor(k.arg[:, h, :], k.arg[:, h, :], k.const("not_before"), ALU.add).then_inc(exponent, 1)
            for c in range(SBH // 2):
                dve.wait_ge(weighed, 2 * c + 2)
                nc.vector.tensor_copy(k.y2T[:, c, :], k.ps[:, 6 + c % 2, 0:SEQ]).then_inc(kept, 1)


def mlstm_prepare_stage(k):
    nc = k.nc
    h = slice(0, MLH)
    conv_w = k.small2("conv_w").rearrange("p (c w) -> p c w", c=6)
    i_row, f_row = k.gate_rows[h, 0, :], k.gate_rows[h, 1, :]
    bcum, a, M, carry, floor, w_row = (k.rows[h, n, :] for n in range(6))
    chunk = [slice(n * P, (n + 1) * P) for n in range(TB)]
    with stage(nc, "conv_step", "convolved", "conv_ready", "scan_step", "log_step", "row_step", "turned", "column_ready",
               "key_scaled") as (
            block, conv_step, convolved, conv_ready, scan_step, log_step, row_step, turned, column_ready, key_scaled):

        @block.scalar
        def _(act):
            nc.scalar.activation(k.soft[h, :], f_row, ACT.Abs).then_inc(log_step, 1)
            act.wait_ge(log_step, 1)
            nc.scalar.activation(k.soft[h, :], k.soft[h, :], ACT.Exp, scale=-1.0).then_inc(log_step, 1)
            act.wait_ge(log_step, 2)
            nc.scalar.activation(k.soft[h, :], k.soft[h, :], ACT.Ln, bias=1.0).then_inc(log_step, 1)
            act.wait_ge(scan_step, 10)
            nc.scalar.activation(floor, floor, ACT.Exp, scale=-1.0).then_inc(row_step, 1)
            nc.scalar.activation(carry[:, chunk[1]], M[:, chunk[1]], ACT.Exp, scale=-1.0, bias=k.m_carry[h, :]).then_inc(row_step, 1)
            nc.scalar.activation(w_row[:, chunk[0]], a[:, chunk[0]], ACT.Exp, bias=k.neg_last[h, :]).then_inc(row_step, 1)
            for c in range(6):
                act.wait_ge(convolved, c + 1)
                nc.scalar.activation(k.qkconv[:, c, :], k.qkconv[:, c, :], ACT.Silu).then_inc(conv_ready, 1)

        @block.vector
        def _(dve):
            scan = Steps(dve, scan_step)
            dve.wait_ge(log_step, 3)
            scan(nc.vector.tensor_scalar(f_row, f_row, 0.0, None, ALU.min))
            scan(nc.vector.tensor_tensor(f_row, f_row, k.soft[h, :], ALU.subtract))
            for n in range(TB):
                scan.step(nc.vector.tensor_tensor_scan(bcum[:, chunk[n]], k.const("ones")[h, :], f_row[:, chunk[n]], 0.0,
                                                       ALU.mult, ALU.add))
            scan.settle()
            scan(nc.vector.tensor_tensor(a, i_row, bcum, ALU.subtract))
            scan(nc.vector.tensor_tensor_scan(M[:, chunk[0]], a[:, chunk[0]], a[:, chunk[0]], 0.0, ALU.max, ALU.max))
            last = slice(P - 1, P)
            scan.step(nc.vector.tensor_tensor(k.m_carry[h, :], bcum[:, last], M[:, last], ALU.add))
            scan(nc.vector.tensor_scalar(k.neg_last[h, :], M[:, last], -1.0, None, ALU.mult))
            scan(nc.vector.tensor_tensor_scan(M[:, chunk[1]], a[:, chunk[1]], a[:, chunk[1]], k.m_carry[h, :], ALU.max, ALU.max))
            scan.step(nc.vector.tensor_tensor(floor, bcum, M, ALU.add))
            conv = Steps(dve, conv_step)
            for c in range(6):
                x, y = k.zT[:, ZMQ + c, :], k.qkconv[:, c, :]
                conv(nc.vector.tensor_scalar(y, x, conv_w[:, c, ML_CONV - 1:ML_CONV], k.small2("conv_b")[:, c:c + 1],
                                             ALU.mult, ALU.add))
                for back in range(1, ML_CONV):
                    w = conv_w[:, c, ML_CONV - 1 - back:ML_CONV - back]
                    tap = nc.vector.scalar_tensor_tensor(y[:, back:SEQ], x[:, 0:SEQ - back], w, y[:, back:SEQ], ALU.mult, ALU.add)
                    if back < ML_CONV - 1:
                        conv(tap)
                    else:
                        tap.then_inc(convolved, 1)
            dve.wait_ge(conv_ready, 6)
            nc.vector.tensor_scalar(k.qkconv[:, 3:6, :], k.qkconv[:, 3:6, :], float(HD) ** -0.5, None,
                                    ALU.mult).then_inc(key_scaled, 1)
            dve.wait_ge(turned, 1)
            nc.vector.tensor_copy(k.columns[:, :, :], k.ps[:, 0, 0:3 * MLH].rearrange("p (n h) -> p n h", n=3)).then_inc(column_ready, 1)
            dve.wait_ge(turned, 2)
            nc.vector.tensor_copy(k.floor[:, 0:2, :], k.ps[:, 1, :].rearrange("p (n t) -> p n t", n=2)).then_inc(column_ready, 1)
            nc.vector.tensor_copy(k.floor[:, 2, :], k.ps[:, 2, 0:SEQ]).then_inc(column_ready, 1)
            for c in range(MLH // 2):
                nc.vector.tensor_tensor(k.q_carry[:, c, :], k.qkconv[:, c, chunk[1]], k.ps[:, 3, c * P:(c + 1) * P],
                                        ALU.mult).then_inc(column_ready, 1)
            dve.wait_ge(turned, 3)
            dve.wait_ge(column_ready, 1)
            for n in range(MLH):
                nc.vector.tensor_scalar(k.k_keep[:, n * HD:(n + 1) * HD], k.ps[:, 4, n * HD:(n + 1) * HD],
                                        k.columns[:, 2, n:n + 1], None, ALU.mult).then_inc(column_ready, 1)

        @block.tensor
        def _(pe):
            pe.wait_ge(row_step, 3)
            for n, row in enumerate((a[:, chunk[0]], a[:, chunk[1]], w_row[:, chunk[0]])):
                last = nc.tensor.transpose(k.ps[:, 0, n * MLH:(n + 1) * MLH], row, k.const("ident")[h, 0:MLH])
            last.then_inc(turned, 1)
            pair = k.const("row_of_pair").rearrange("p (c m) -> p c m", c=MLH // 2)
            for c in range(MLH // 2):
                nc.tensor.matmul(k.ps[:, 1 + c // 2, c % 2 * SEQ:(c % 2 + 1) * SEQ], pair[h, c, :], floor, start=True, stop=True)
                last = nc.tensor.matmul(k.ps[:, 3, c * P:(c + 1) * P], pair[h, c, :], carry[:, chunk[1]], start=True, stop=True)
            last.then_inc(turned, 1)
            pe.wait_ge(key_scaled, 1)
            for c in range(MLH // 2):
                last = nc.tensor.transpose(k.ps[:, 4, c * P:(c + 1) * P], k.qkconv[:, 3 + c, 0:P], k.const("ident"))
            last.then_inc(turned, 1)


def mlstm_stage(k):
    nc = k.nc
    h6 = slice(0, MLH)
    M = k.rows[h6, 2, :]
    chunk = [slice(n * P, (n + 1) * P) for n in range(TB)]
    row = k.const("row_of_head").rearrange("p (h m) -> p h m", h=MLH)
    with stage(nc, "spread", "masked", "decayed", "scored", "probs_ready", "state_summed", "state_kept", "summed",
               "den_step", "finished") as (
            block, spread, masked, decayed, scored, probs_ready, state_summed, state_kept, summed, den_step, finished):

        @block.tensor
        def _(pe):
            for h in range(MLH):
                rows = slice(HD * (h % 2), HD * (h % 2 + 1))
                keys = k.k_keep[:, h * HD:(h + 1) * HD]
                nc.tensor.matmul(k.ps[rows, 0, h // 2 * P:h // 2 * P + HD], keys,
                                 k.natural2[:, 0, SBW + h * HD:SBW + (h + 1) * HD], start=True, stop=True)
                last = nc.tensor.matmul(k.ps[rows, 0, h // 2 * P + HD:(h // 2 + 1) * P], keys, k.const("ones")[:, 0:HD],
                                        start=True, stop=True)
            last.then_inc(state_summed, 1)
            for h in range(MLH):
                base, c = HD * (h % 2), h // 2
                rows = slice(base, base + HD)
                if h >= 2:
                    pe.wait_ge(masked, h - 1)
                nc.tensor.matmul(k.ps[:, 1 + h % 2, 0:SEQ], row[h6, h, :], M, start=True, stop=True).then_inc(spread, 1)
                if h >= 2:
                    pe.wait_ge(probs_ready, h - 1)
                for n in range(TB):
                    last = nc.tensor.matmul(k.ps[:, 3 + h % 2, chunk[n]], k.qkconv[rows, 3 + c, chunk[n]],
                                            k.qkconv[rows, c, chunk[n]], start=True, stop=True)
                last.then_inc(scored, 1)
                pe.wait_ge(probs_ready, h + 1)
                if h == 0:
                    pe.wait_ge(state_kept, 1)
                if h % 2 == 0 and c >= 1:
                    pe.wait_ge(finished, c)
                probs = k.ml_probs[:, h % 2, :]
                for bank, within, state in ((5, [k.natural2[:, n, SBW + h * HD:SBW + (h + 1) * HD] for n in range(TB)], 0),
                                            (6, [k.const("ones")[:, 0:HD]] * TB, HD)):
                    nc.tensor.matmul(k.ps[rows, bank, chunk[0]], within[0], probs[:, chunk[0]], start=True, stop=True)
                    nc.tensor.matmul(k.ps[rows, bank, chunk[1]], k.state[rows, c * P + state:c * P + state + HD],
                                     k.q_carry[rows, c, :], start=True, stop=False)
                    last = nc.tensor.matmul(k.ps[rows, bank, chunk[1]], within[1], probs[:, chunk[1]], start=False, stop=True)
                last.then_inc(summed, 1)

        @block.scalar
        def _(act):
            act.wait_ge(state_summed, 1)
            nc.scalar.activation(k.state[:, :], k.ps[:, 0, 0:MLH // 2 * P], ACT.Copy).then_inc(state_kept, 1)
            for h in range(MLH):
                act.wait_ge(masked, h + 1)
                for n in range(TB):
                    nc.scalar.activation(k.decay[:, h % 2, chunk[n]], k.ahead[:, h % 2, chunk[n]], ACT.Exp, scale=-1.0,
                                         bias=k.columns[:, n, h:h + 1]).then_inc(decayed, 1)
                if h % 2:
                    act.wait_ge(summed, h + 1)
                    nc.scalar.activation(k.den[:, :], k.ps[:, 6, 0:SEQ], ACT.Abs).then_inc(den_step, 1)

        @block.vector
        def _(dve):
            for h in range(MLH):
                dve.wait_ge(spread, h + 1)
                if h >= 2:
                    dve.wait_ge(decayed, 2 * (h - 1))
                nc.vector.tensor_tensor(k.ahead[:, h % 2, :], k.ps[:, 1 + h % 2, 0:SEQ], k.const("ahead"), ALU.add).then_inc(masked, 1)
                dve.wait_ge(scored, h + 1)
                dve.wait_ge(decayed, 2 * h + 2)
                if h >= 2:
                    dve.wait_ge(summed, h - 1)
                nc.vector.tensor_tensor(k.ml_probs[:, h % 2, :], k.decay[:, h % 2, :], k.ps[:, 3 + h % 2, 0:SEQ],
                                        ALU.mult).then_inc(probs_ready, 1)
                if h % 2:
                    c = h // 2
                    dve.wait_ge(den_step, 3 * c + 1)
                    nc.vector.tensor_tensor(k.den[:, :], k.den[:, :], k.floor[:, c, :], ALU.max).then_inc(den_step, 1)
                    dve.wait_ge(den_step, 3 * c + 2)
                    nc.vector.reciprocal(k.den[:, :], k.den[:, :]).then_inc(den_step, 1)
                    dve.wait_ge(den_step, 3 * c + 3)
                    nc.vector.tensor_tensor(k.y2T[:, YML + c, :], k.den[:, :], k.ps[:, 5, 0:SEQ], ALU.mult).then_inc(finished, 1)


def gating_stage(k):
    nc = k.nc
    first = SBW + MLW
    groups = TB * SGG
    sg_w = k.small2("sg_w").rearrange("p (g t) -> p g t", g=SGG)
    with stage(nc, "gelu_done", "squared", "var_step", "rooted", "normed", "masked", "gated", "finished") as (
            block, gelu_done, squared, var_step, rooted, normed, masked, gated, finished):

        @block.scalar
        def _(act):
            for b in range(TB):
                v = k.natural2[:, b, first:first + SGW]
                nc.scalar.activation(v, v, ACT.Gelu_apprx_tanh).then_inc(gelu_done, 1)
            u = k.zT[:, ZU:ZU + 2, :]
            nc.scalar.activation(u, u, ACT.Gelu_apprx_tanh).then_inc(gelu_done, 1)
            for b in range(TB):
                act.wait_ge(gelu_done, b + 1)
                nc.scalar.activation(k.v_square[:, b * SGW:(b + 1) * SGW], k.natural2[:, b, first:first + SGW],
                                     ACT.Square).then_inc(squared, 1)
            act.wait_ge(var_step, 2)
            nc.scalar.activation(k.v_rstd[:, :], k.v_rstd[:, :], ACT.Sqrt).then_inc(rooted, 1)

        @block.vector
        def _(dve):
            for g in range(SGG):
                nc.vector.tensor_tensor(sg_w[:, g, :], sg_w[:, g, :], k.const("causal"), ALU.mult).then_inc(masked, 1)
            dve.wait_ge(squared, TB)
            nc.vector.reduce_sum(k.v_rstd[:, :], k.v_square[:, :].rearrange("p (g d) -> p g d", g=groups), AX_X).then_inc(var_step, 1)
            dve.wait_ge(var_step, 1)
            nc.vector.tensor_scalar(k.v_rstd[:, :], k.v_rstd[:, :], 1.0 / HD, EPS, ALU.mult, ALU.add).then_inc(var_step, 1)
            dve.wait_ge(rooted, 1)
            nc.vector.reciprocal(k.v_rstd[:, :], k.v_rstd[:, :]).then_inc(var_step, 1)
            dve.wait_ge(var_step, 3)
            for b in range(TB):
                for g in range(SGG):
                    v = k.natural2[:, b, first + g * HD:first + (g + 1) * HD]
                    nc.vector.scalar_tensor_tensor(v, v, k.v_rstd[:, b * SGG + g:b * SGG + g + 1],
                                                   k.small2("vn_g")[:, g * HD:(g + 1) * HD], ALU.mult, ALU.mult).then_inc(normed, 1)
            dve.wait_ge(gelu_done, TB + 1)
            for a in range(2):
                dve.wait_ge(gated, a + 1)
                nc.vector.tensor_tensor(k.y2T[:, YSG + a, :], k.zT[:, ZU + a, :], k.ps[:, a, 0:SEQ], ALU.mult).then_inc(finished, 1)

        @block.tensor
        def _(pe):
            pe.wait_ge(normed, groups)
            pe.wait_ge(masked, SGG)
            for a in range(2):
                for g in (2 * a, 2 * a + 1):
                    rows = slice(HD * (g % 2), HD * (g % 2 + 1))
                    for b in range(TB):
                        out = k.ps[rows, a, b * P:(b + 1) * P]
                        nc.tensor.matmul(out, k.natural2[:, b, first + g * HD:first + (g + 1) * HD], sg_w[:, g, :],
                                         start=True, stop=False)
                        last = nc.tensor.matmul(out, k.const("ones")[0:1, 0:HD], k.small2("sg_b")[0:1, g * P:(g + 1) * P],
                                                start=False, stop=True)
                last.then_inc(gated, 1)


def output_gate_stage(k):
    nc = k.nc
    with stage(nc, "gate_ready", "gated") as (block, gate_ready, gated):

        @block.scalar
        def _(act):
            o = k.zT[:, ZO:ZO + 3, :]
            nc.scalar.activation(o, o, ACT.Sigmoid).then_inc(gate_ready, 1)

        @block.vector
        def _(dve):
            dve.wait_ge(gate_ready, 1)
            y = k.y2T[:, YML:YML + 3, :]
            nc.vector.tensor_tensor(y, y, k.zT[:, ZO:ZO + 3, :], ALU.mult).then_inc(gated, 1)


def choose_stage(k):
    nc = k.nc
    rows, pairs = TB * HC, TB * PH
    low = -3.0e38
    best = lambda half: slice(8 * half, 8 * half + 8)
    with stage(nc, "scored", "kept", "step", "gate_step", "turned", "slots_ready") as (
            block, scored, kept, step, gate_step, turned, slots_ready):

        @block.tensor
        def _(pe):
            for b in range(TB):
                for n in range(HC):
                    last = nc.tensor.matmul(k.ps[:, b * 4 + n // 4, n % 4 * NK:(n % 4 + 1) * NK], k.queryT[:, n, b * P:(b + 1) * P],
                                            k.keysT[:, n * NK:(n + 1) * NK], start=True, stop=True)
                    if n % 4 == 3:
                        last.then_inc(scored, 1)
            pe.wait_ge(gate_step, 5)
            for n, x in enumerate((k.key_i, k.key_j, k.gates)):
                for b in range(TB):
                    last = nc.tensor.transpose(k.ps[:, n, b * P:(b + 1) * P], x[:, b * SLOTS:(b + 1) * SLOTS], k.const("ident"))
            last.then_inc(turned, 1)

        @block.scalar
        def _(act):
            for n in range(rows // 4):
                act.wait_ge(scored, n + 1)
                nc.scalar.activation(k.key_scores[:, n * 4 * NK:(n + 1) * 4 * NK], k.ps[:, n, :], ACT.Copy).then_inc(kept, 1)
            act.wait_ge(gate_step, 1)
            nc.scalar.activation(k.gates[:, :], k.gates[:, :], ACT.Exp).then_inc(gate_step, 1)

        @block.vector
        def _(dve):
            s = Steps(dve, step)

            def top16(n, scores, spare, values, index, width):
                at = lambda x, r: x[:, r * width:(r + 1) * width]
                for r in range(n):
                    if width == NK and r % 4 == 0:
                        dve.wait_ge(kept, r // 4 + 1)
                    s.step(nc.vector.max(values[:, r, best(0)], at(scores, r)))
                s.settle()
                for r in range(n):
                    s.step(nc.vector.max_index(index[:, r, best(0)], values[:, r, best(0)], at(scores, r)))
                    s.step(nc.vector.match_replace(at(spare, r), values[:, r, best(0)], at(scores, r), low))
                s.settle()
                for r in range(n):
                    s.step(nc.vector.max(values[:, r, best(1)], at(spare, r)))
                s.settle()
                for r in range(n):
                    s.step(nc.vector.max_index(index[:, r, best(1)], values[:, r, best(1)], at(spare, r)))
                s.settle()

            top16(rows, k.key_scores, k.key_spare, k.half_val, k.half_at, NK)
            s(nc.vector.tensor_copy(k.half_key[:, :, :], k.half_at[:, :, :]))
            for n in range(pairs):
                cand = k.cand[:, n * 256:(n + 1) * 256].rearrange("p (a b) -> p a b", a=TOPK)
                s.step(nc.vector.tensor_tensor(cand, k.half_val[:, 2 * n, :].unsqueeze(2).broadcast_to([P, TOPK, TOPK]),
                                               k.half_val[:, 2 * n + 1, :].unsqueeze(1).broadcast_to([P, TOPK, TOPK]), ALU.add))
            s.settle()
            top16(pairs, k.cand, k.cand_spare, k.pair_val, k.pair_at, TOPK * TOPK)
            flat_at = k.pair_at[:, :, :].rearrange("p n k -> p (n k)")
            for key, half, op, by in ((k.key_i, 0, ALU.logical_shift_right, 4), (k.key_j, 1, ALU.bitwise_and, TOPK - 1)):
                s(nc.vector.tensor_scalar(k.place_int[:, :], flat_at, by, None, op))
                s(nc.vector.tensor_copy(k.place[:, :], k.place_int[:, :]))
                for n in range(pairs):
                    hot = k.cand[:, n * 256:(n + 1) * 256].rearrange("p (k a) -> p k a", a=TOPK)
                    s.step(nc.vector.tensor_tensor(hot, k.place[:, n * TOPK:(n + 1) * TOPK].unsqueeze(2).broadcast_to([P, TOPK, TOPK]),
                                                   k.const("iota")[:, 0:TOPK].unsqueeze(1).broadcast_to([P, TOPK, TOPK]), ALU.is_equal))
                s.settle()
                for n in range(pairs):
                    hot = k.cand[:, n * 256:(n + 1) * 256].rearrange("p (k a) -> p k a", a=TOPK)
                    s.step(nc.vector.tensor_tensor(hot, hot, k.half_key[:, 2 * n + half, :].unsqueeze(1).broadcast_to([P, TOPK, TOPK]),
                                                   ALU.mult))
                s.settle()
                s(nc.vector.reduce_sum(key[:, :], k.cand[:, :].rearrange("p (m a) -> p m a", a=TOPK), AX_X))
            gates = k.gates[:, :].rearrange("p (n k) -> p n k", k=TOPK)
            nc.vector.tensor_tensor(gates, k.pair_val[:, :, :], k.pair_val[:, :, 0:1].broadcast_to([P, pairs, TOPK]),
                                    ALU.subtract).then_inc(gate_step, 1)
            dve.wait_ge(gate_step, 2)
            nc.vector.reduce_sum(k.gate_sum[:, :], gates, AX_X).then_inc(gate_step, 1)
            dve.wait_ge(gate_step, 3)
            nc.vector.reciprocal(k.gate_sum[:, :], k.gate_sum[:, :]).then_inc(gate_step, 1)
            dve.wait_ge(gate_step, 4)
            nc.vector.tensor_tensor(gates, gates, k.gate_sum[:, :].unsqueeze(2).broadcast_to([P, pairs, TOPK]),
                                    ALU.mult).then_inc(gate_step, 1)
            dve.wait_ge(turned, 1)
            for n, x in enumerate((k.slot_i, k.slot_j, k.slot_gate)):
                nc.vector.tensor_copy(x[:, :], k.ps[:, n, 0:SEQ]).then_inc(slots_ready, 1)


def scatter_stage(k):
    nc, lot, bank = k.nc, 8, 4
    with stage(nc, "one_hot", "spread", "copied") as (block, one_hot, spread, copied):

        @block.vector
        def _(dve):
            with dve.Fori(0, SEQ // lot) as i:
                for u in range(lot):
                    t = bass.ds(i * lot + u, 1)
                    if u % bank == 0:
                        dve.wait_ge(spread, i * 2 + u // bank + 1)
                    nc.vector.tensor_scalar(k.hot_i[:, u, :], k.const("iota"), k.slot_i[:, t], k.slot_gate[:, t],
                                            ALU.is_equal, ALU.mult).then_inc(one_hot, 1)
                    nc.vector.tensor_scalar(k.hot_j[:, u, :], k.const("iota"), k.slot_j[:, t], None,
                                            ALU.is_equal).then_inc(one_hot, 1)

        @block.tensor
        def _(pe):
            for n in range(2):
                pe.sem_inc(spread, 1)
            with pe.Fori(0, SEQ // lot) as i:
                for u in range(lot):
                    if u % bank == 0:
                        pe.wait_ge(copied, i * 2 + u // bank + 1)
                    pe.wait_ge(one_hot, (i * lot + u) * 2 + 2)
                    last = nc.tensor.matmul(k.ps[:, u // bank, u % bank * NK:(u % bank + 1) * NK], k.hot_i[:, u, :],
                                            k.hot_j[:, u, :], start=True, stop=True)
                    if u % bank == bank - 1:
                        last.then_inc(spread, 1)

        @block.scalar
        def _(act):
            for n in range(2):
                act.sem_inc(copied, 1)
            with act.Fori(0, SEQ // lot) as i:
                for n in range(2):
                    act.wait_ge(spread, i * 2 + n + 3)
                    nc.scalar.activation(k.dense[:, bass.ds((i * lot + n * bank) * NK, bank * NK)], k.ps[:, n, :],
                                         ACT.Copy).then_inc(copied, 1)


def experts_stage(k, l):
    nc, steps = k.nc, NK
    dense = k.dense[:, :].rearrange("p (t j) -> p t j", j=NK)
    with stage(nc, "u_in*2", "v_in*2", "act_summed", "gelu_done", "weighted", "combined", "kept", "turned", "added") as (
            block, u_in, v_in, act_summed, gelu_done, weighted, combined, kept, turned, added):

        @block.sync
        def _(sp):
            for s in range(2):
                sp.dma_start(k.u_ring[:, s], tile(k.peer_u, l * steps + s)).then_inc(u_in[s], 16)
                sp.dma_start(k.v_ring[:, s], tile(k.peer_v, l * steps + s)).then_inc(v_in[s], 16)
            with sp.Fori(1, steps // 2) as i:
                for s in range(2):
                    sp.wait_ge(act_summed, (i - 1) * 2 + s + 1)
                    sp.dma_start(k.u_ring[:, s], tile(k.peer_u, l * steps + i * 2 + s)).then_inc(u_in[s], 16)
                    sp.wait_ge(combined, i * 2 + s + 1)
                    sp.dma_start(k.v_ring[:, s], tile(k.peer_v, l * steps + i * 2 + s)).then_inc(v_in[s], 16)

        @block.tensor
        def _(pe):
            outs = [k.ps[:, 2 + n, :] for n in range(4)]

            def activate(i, s):
                pe.wait_ge(u_in[s], i * 16 + 16)
                pe.wait_ge(gelu_done, i * 2 + s + 1)
                for c in range(DC):
                    last = nc.tensor.matmul(k.ps[:, s, 0:SEQ], k.u_ring[:, s, c * P:(c + 1) * P], k.hT[:, c, :],
                                            start=c == 0, stop=c == DC - 1)
                last.then_inc(act_summed, 1)

            def combine(i, s, stop):
                pe.wait_ge(v_in[s], i * 16 + 16)
                pe.wait_ge(weighted, i * 2 + s + 3)
                for n, out in enumerate(outs):
                    last = nc.tensor.matmul(out, k.weight[:, s, n // 2 * P:(n // 2 + 1) * P],
                                            k.v_ring[:, s, n % 2 * 512:(n % 2 + 1) * 512], start=False, stop=stop)
                last.then_inc(combined, 1)

            for s in range(2):
                pe.sem_inc(combined, 1)
            for out in outs:
                nc.tensor.matmul(out, k.zeros[:, 0:P], k.zeros[:, 0:512], start=True, stop=False)
            activate(0, 0)
            with pe.Fori(0, steps // 2 - 1) as i:
                activate(i, 1)
                combine(i, 0, False)
                activate(i + 1, 0)
                combine(i, 1, False)
            activate(steps // 2 - 1, 1)
            combine(steps // 2 - 1, 0, False)
            combine(steps // 2 - 1, 1, True)
            for c in range(DC):
                pe.wait_ge(kept, 4)
                if c >= 2:
                    pe.wait_ge(added, c - 1)
                for b in range(TB):
                    last = nc.tensor.transpose(k.ps[:, c % 2, b * P:(b + 1) * P], k.y_natural[:, b, c * P:(c + 1) * P], k.const("ident"))
                last.then_inc(turned, 1)

        @block.scalar
        def _(act):
            for s in range(2):
                act.sem_inc(gelu_done, 1)
            with act.Fori(0, steps // 2) as i:
                for s in range(2):
                    act.wait_ge(act_summed, i * 2 + s + 1)
                    act.wait_ge(weighted, i * 2 + s + 1)
                    nc.scalar.activation(k.gelu[:, s, :], k.ps[:, s, 0:SEQ], ACT.Gelu_apprx_tanh).then_inc(gelu_done, 1)
            for n in range(4):
                act.wait_ge(combined, steps + 2)
                nc.scalar.activation(k.y_natural[:, n // 2, n % 2 * 512:(n % 2 + 1) * 512], k.ps[:, 2 + n, :],
                                     ACT.Copy).then_inc(kept, 1)

        @block.vector
        def _(dve):
            for s in range(2):
                dve.sem_inc(weighted, 1)
            with dve.Fori(0, steps // 2) as i:
                for s in range(2):
                    dve.wait_ge(gelu_done, i * 2 + s + 3)
                    dve.wait_ge(combined, i * 2 + s + 1)
                    nc.vector.tensor_tensor(k.weight[:, s, :], k.gelu[:, s, :],
                                            dense[:, :, bass.ds(i * 2 + s, 1)].rearrange("p t j -> p (t j)"),
                                            ALU.mult).then_inc(weighted, 1)
            for c in range(DC):
                dve.wait_ge(turned, c + 1)
                nc.vector.tensor_tensor(k.x2T[:, c, :], k.x2T[:, c, :], k.ps[:, c % 2, 0:SEQ], ALU.add).then_inc(added, 1)


def second_block(k, scope, sb):
    nc = k.nc
    k.small2_sb = sb(scope, "small2_sb", SMALL2_W)
    k.hT = sb(scope, "h2T", DC, SEQ)
    k.slot_i, k.slot_j, k.slot_gate = (sb(scope, f"slot_{n}", SEQ) for n in ("i", "j", "gate"))
    k.hot_i, k.hot_j = sb(scope, "hot_i", 8, NK), sb(scope, "hot_j", 8, NK)
    k.u_ring, k.v_ring = sb(scope, "u_ring", 2, D), sb(scope, "v_ring", 2, D)
    k.gelu, k.weight = sb(scope, "gelu", 2, SEQ), sb(scope, "weight", 2, SEQ)
    k.zeros = sb(scope, "zeros", 512)
    k.dense = sb(scope, "dense", SEQ * NK)

    mix = Carver(k.dense)
    k.ring = mix(RING, D)
    k.zT, k.natural2 = mix(ZC, SEQ), mix(TB, NATURAL2)
    k.y2T, k.squares = mix(DC, SEQ), mix(DC, SEQ)
    k.z, k.z_abs, k.keep, k.arg = (mix(SBH, 3 * P) for _ in range(4))
    k.gate_rows, k.rows, k.soft = mix(2, SEQ), mix(6, SEQ), mix(SEQ)
    stick = Carver(k.z.rearrange("p h w -> p (h w)"))
    k.m_carry, k.neg_last, k.columns = stick(1), stick(1), stick(3, MLH)
    k.qkconv = k.squares[:, 0:6, :]
    more = Carver(k.z_abs.rearrange("p h w -> p (h w)"))
    k.floor, k.q_carry, k.k_keep = more(MLH // 2, SEQ), more(MLH // 2, P), more(MLW)
    more = Carver(k.keep.rearrange("p h w -> p (h w)"))
    k.state, k.ahead, k.decay, k.ml_probs = more(MLH // 2 * P), more(2, SEQ), more(2, SEQ), more(2, SEQ)
    more = Carver(k.arg.rearrange("p h w -> p (h w)"))
    k.den, k.v_square, k.v_rstd = more(SEQ), more(TB * SGW), more(TB * SGG)

    choose = Carver(k.dense)
    choose(RING, D)
    k.queryT, k.keysT = choose(HC, SEQ), choose(HC * NK)
    k.key_scores, k.key_spare = choose(TB * HC * NK), choose(TB * HC * NK)
    k.half_val, k.half_key = choose(TB * HC, TOPK), choose(TB * HC, TOPK)
    k.half_at = choose(TB * HC, TOPK).bitcast(U32)
    pairs = TB * PH
    k.pair_val, k.pair_at = choose(pairs, TOPK), choose(pairs, TOPK).bitcast(U32)
    k.place, k.place_int = choose(pairs * TOPK), choose(pairs * TOPK).bitcast(U32)
    k.key_i, k.key_j, k.gates, k.gate_sum = choose(TB * SLOTS), choose(TB * SLOTS), choose(TB * SLOTS), choose(pairs)
    k.cand, k.cand_spare = k.key_scores, k.key_spare
    k.y_natural = Carver(k.dense)(TB, D)

    with stage(nc, "zeroed") as (block, zeroed):

        @block.vector
        def _(dve):
            nc.vector.memset(k.zeros[:, :], 0.0).then_inc(zeroed, 1)

    with nc.Fori(0, DEPTH) as l:
        load_stage(k, [(k.small2_sb[:, :], tile(k.small2_dram, l))])
        norm_stage(k, SEQ, lambda c, s: k.small2("norm1")[:, c:c + 1], None, k.x2T, k.hT)
        transposed_stage(k, k.w_transposed2, l * ZC, ZC, k.zT)
        natural2_stage(k, l)
        head_norm_stage(k, k.zT[:, 0:6, :], 6, lambda c: k.small2("qn_g" if c < ZK else "kn_g"))
        stick_breaking_stage(k)
        mlstm_prepare_stage(k)
        mlstm_stage(k)
        gating_stage(k)
        head_norm_stage(k, k.y2T, DC, lambda c: k.small2("out_g")[:, c:c + 1])
        output_gate_stage(k)
        residual_stage(k, SEQ, k.w_out2, l * DC, DC, k.y2T, None, k.x2T)
        norm_stage(k, SEQ, lambda c, s: k.small2("norm2")[:, c:c + 1], None, k.x2T, k.hT)
        transposed_stage(k, k.w_query2, l * HC, HC, k.queryT)
        load_stage(k, [(k.keysT, tile(k.peer_keys, l))])
        choose_stage(k)
        scatter_stage(k)
        experts_stage(k, l)


def layout2(x):
    x = {name[:-2]: a for name, a in x.items() if name.endswith("_2")}
    L = DEPTH
    cuts = np.cumsum([SBW, SBW, SBW, 2 * MLW, MLW, MLW, MLH, MLH, SGW])
    q, kk, v, mqk, mv, mo, mi, mf, su, sv = np.split(x["w_in"], cuts, axis=-1)
    w_if = np.concatenate([mi, mf], -1).reshape(L, DC, P, 2 * MLH).transpose(0, 2, 1, 3)
    pair = lambda g: np.tile(g, 2)[:, None]
    small2 = np.stack([packed(SMALL2, SMALL2_W, {
        "norm1": chunked(x["norm1_g"][l]), "norm2": chunked(x["norm2_g"][l]),
        "qn_g": pair(x["sb_qn_g"][l]), "kn_g": pair(x["sb_kn_g"][l]),
        "conv_w": chunked(x["ml_conv_w"][l]).transpose(1, 2, 0), "conv_b": chunked(x["ml_conv_b"][l]),
        "out_g": chunked(x["out_g"][l]), "if_b": np.stack([x["ml_i_b"][l], x["ml_f_b"][l]], -1),
        "vn_g": np.broadcast_to(x["sg_vn_g"][l], (P, SGW)), "sg_b": x["sg_b"][l].reshape(1, -1),
        "sg_w": x["sg_w"][l].transpose(2, 0, 1), "w_if": w_if[l]}) for l in range(L)])
    experts = lambda a: a.reshape(L, NK, NK, DC, P)
    return {
        "small2_dram": small2, "w_transposed2": tiled(np.concatenate([q, kk, mqk, mo, su], -1)),
        "w_natural2": np.concatenate([v, mv, sv], -1).reshape(L * DC, P, NATURAL2),
        "w_out2": tiled(x["w_out"]), "w_query2": tiled(x["peer_wq"]),
        "peer_keys": x["peer_keys"].transpose(0, 4, 1, 2, 3).reshape(L, P, HC * NK),
        "peer_u": experts(x["peer_u"]).transpose(0, 2, 4, 3, 1).reshape(L * NK, P, D),
        "peer_v": experts(x["peer_v"]).transpose(0, 2, 1, 3, 4).reshape(L * NK, P, D),
    }




class Kit:

    def __init__(self, nc):
        self.nc = nc

    def const(self, name):
        at, width = CONST[name]
        return self.const_sb[:, at:at + width]

    def const1(self, name):
        at, width = CONST1[name]
        return self.const1_sb[:, at:at + width]

    def small1(self, name):
        at, width = SMALL1[name]
        return self.small1_sb[:, at:at + width]

    def small2(self, name):
        at, width = SMALL2[name]
        return self.small2_sb[:, at:at + width]


class Carver:

    def __init__(self, whole):
        self.whole, self.at = whole, 0

    def __call__(self, *shape):
        width = int(np.prod(shape))
        cut = self.whole[:, self.at:self.at + width]
        self.at += width
        assert self.at <= self.whole.shape[1], self.at
        if len(shape) == 2:
            return cut.rearrange("p (a b) -> p a b", a=shape[0])
        if len(shape) == 3:
            return cut.rearrange("p (a b c) -> p a b c", a=shape[0], b=shape[1])
        return cut


def program(nc, dram, out):
    k = Kit(nc)
    tokens = SEQ + CTX
    k.x_in, k.cond_in, k.norm_final_in = dram["x_in"], dram["cond_in"], dram["norm_final_in"]
    k.const_dram, k.const1_dram, k.small1_dram = dram["const_dram"], dram["const1_dram"], dram["small1_dram"]
    k.w_mod, k.w_qk, k.w_natural = dram["w_mod"], dram["w_qk"], dram["w_natural"]
    k.w_merge, k.w_out, k.w_up = dram["w_merge"], dram["w_out"], dram["w_up"]
    k.w_down, k.small2_dram, k.w_transposed2 = dram["w_down"], dram["small2_dram"], dram["w_transposed2"]
    k.w_natural2, k.w_out2, k.w_query2 = dram["w_natural2"], dram["w_out2"], dram["w_query2"]
    k.peer_keys, k.peer_u, k.peer_v = dram["peer_keys"], dram["peer_u"], dram["peer_v"]
    with ExitStack() as ctx:

        def sb(scope, name, *shape):
            return scope.enter_context(nc.sbuf_tensor(name, [P, *shape], F32))

        k.ps = ctx.enter_context(nc.psum_tensor("ps", [P, 8, 512], F32))
        k.const_sb = sb(ctx, "const_sb", CONST_W)
        k.rstd = sb(ctx, "rstd", tokens)
        k.x2T = sb(ctx, "x2T", DC, SEQ)
        with ExitStack() as scope:
            k.const1_sb = sb(scope, "const1_sb", CONST1_W)
            k.small1_sb = sb(scope, "small1_sb", SMALL1_W)
            k.cond = sb(scope, "cond", DC * 2)
            k.cond_silu = sb(scope, "cond_silu", DC * 2)
            k.norm_final = sb(scope, "norm_final_sb", DC)
            k.mod = sb(scope, "mod", NMOD * DC, 2)
            k.xT = sb(scope, "xT", DC, tokens)
            k.hT = sb(scope, "hT", DC, tokens)
            k.branchT = sb(scope, "branchT", DC, tokens)
            k.yT = sb(scope, "yT", DC, tokens)
            k.ring = sb(scope, "ring", RING, D)
            k.stat = sb(scope, "stat", 2, 4)
            work = sb(scope, "work", 14336)
            mix = Carver(work)
            k.qkT, k.natural = mix(1 + QC, tokens), mix(tokens // P, NATURAL)
            k.scores, k.exps, k.probs, k.probsT = (mix(2, tokens) for _ in range(4))
            k.pooledT, k.timedT = mix(4, SEQ), mix(4, 2 * SEQ)
            k.gate, k.part = mix(3, tokens), mix(tokens)
            ffn = Carver(work)
            k.actT, k.conv = ffn(FC, tokens), ffn(4, tokens)
            load_stage(k, [(k.xT[:, :, :], k.x_in), (k.const_sb[:, :], k.const_dram), (k.const1_sb[:, :], k.const1_dram),
                           (k.cond[:, :], k.cond_in), (k.norm_final[:, :], k.norm_final_in)])
            first_block(k)
        with ExitStack() as scope:
            second_block(k, scope, sb)
        with stage(nc, "stored") as (block, stored):

            @block.sync
            def _(sp):
                sp.dma_start(out, k.x2T[:, :, :]).then_inc(stored, 16)
                sp.wait_ge(stored, 16)


def packed(table, width, parts):
    out = np.zeros((P, width), np.float32)
    for name, part in parts.items():
        at, n = table[name]
        part = np.asarray(part, np.float32)
        part = part.reshape(part.shape[0], n)
        out[:part.shape[0], at:at + n] = part
    return out


def constants():
    i = np.arange(P)
    q, key = np.arange(SEQ)[None, :], np.arange(P)[:, None]
    before = np.concatenate([key < q, (key < np.arange(P)[None, :])], axis=1).astype(np.float32)
    causal = (i[:, None] <= i[None, :]).astype(np.float32)
    heads = np.zeros((P, MLH, P), np.float32)
    pairs = np.zeros((P, MLH // 2, P), np.float32)
    for h in range(MLH):
        heads[h, h] = 1
        pairs[h, h // 2, (h % 2) * HD:(h % 2 + 1) * HD] = 1
    return packed(CONST, CONST_W, {
        "ident": np.eye(P), "ones": np.ones((P, P)), "half_ones": np.kron(np.eye(2), np.ones((HD, HD))),
        "suffix": i[:, None] >= i[None, :], "iota": np.broadcast_to(np.arange(NK), (P, NK)), "causal": causal,
        "before": before, "not_before": (1 - before) * MASKED, "ahead": np.tile((1 - causal) * -MASKED, (1, 2)),
        "row_of_head": heads, "row_of_pair": pairs})


def constants1():
    tokens = SEQ + CTX
    freq = (ROPE_BASE ** (-np.arange(HD // 4) / (HD // 4))).astype(np.float32)
    pos = np.arange(SEQ)
    angle = np.stack([np.float32(pos // GRID_W)[:, None] * freq, np.float32(pos % GRID_W)[:, None] * freq], 1)
    cos, sin = np.ones((2, 2, 2, HD // 4, tokens)), np.zeros((2, 2, 2, HD // 4, tokens))
    cos[..., :SEQ] = np.cos(angle).transpose(1, 2, 0)[None, :, None]
    sin[..., :SEQ] = np.sin(angle).transpose(1, 2, 0)[None, :, None]
    swap = np.zeros((P, P))
    for m in range(P):
        quarter = HD // 4
        if m // quarter % 2 == 0:
            swap[m + quarter, m] = -1
        else:
            swap[m - quarter, m] = 1
    window = np.zeros((P, TB, 2 * SEQ))
    for b in range(TB):
        rel = np.arange(SEQ)[None, :] - (b * P + np.arange(P))[:, None]
        window[:, b, :SEQ] = np.where(np.abs(rel) <= WINDOW, 0, MASKED)
    pool = np.zeros((SEQ, len(POOL_WINDOWS), SEQ))
    for g, w in enumerate(POOL_WINDOWS):
        for t in range(SEQ):
            lo, hi = max(t - w // 2, 0), min(t - w // 2 + w, SEQ)
            pool[lo:hi, g, t] += 1.0 / (hi - lo)
            pool[t, g, t] -= 1
    tt = 2 * np.pi * np.outer(np.arange(SEQ), np.arange(SEQ)) / SEQ
    cc = 2 * np.pi * np.outer(np.arange(HD), np.arange(HD)) / HD
    time = np.concatenate([np.cos(tt), np.sin(tt)], 1) / np.sqrt(SEQ)
    chan = np.concatenate([np.kron(np.eye(2), np.cos(cc)), -np.kron(np.eye(2), np.sin(cc))], 1) / np.sqrt(HD)

    def by_block(a):
        return a.reshape(TB, P, -1).transpose(1, 0, 2)

    return packed(CONST1, CONST1_W, {
        "rope_swap": swap, "rope_cos": cos.reshape(P, tokens), "rope_sin": sin.reshape(P, tokens), "window": window,
        "pool": by_block(pool), "dft_time": by_block(time), "dft_chan": chan})


def chunked(a):
    return np.moveaxis(a.reshape(*a.shape[:-1], -1, P), -2, -1)


def tiled(w):
    l, rows, cols = w.shape
    a = w.reshape(l, rows // P, P, cols // P, P).transpose(0, 3, 2, 1, 4)
    return np.ascontiguousarray(a).reshape(l * cols // P, P, rows)


def layout(x):
    x = {name: np.asarray(a) for name, a in x.items()}
    L = DEPTH
    w_in = x["w_in"]
    cuts = np.cumsum([KW, KW, QW, POOLW, FOURW])
    wk, wv, wq, wu, wf, wg = np.split(w_in, cuts, axis=-1)
    heads = np.array([[c, c + QC] for c in range(QC)]).ravel()
    wq = wq.reshape(L, D, QH, HD)[:, :, heads].reshape(L, D, QW)
    br_attn = x["w_br_attn"].reshape(L, QH, HD, D)[:, heads].reshape(L, QW, D)
    branches = np.concatenate([br_attn, x["w_br_pool"], x["w_br_four"]], axis=1)
    merge = np.stack([*(a.reshape(L, DC, P, D) for a in np.split(tiled(wg).reshape(L, 3 * DC, P, D), 3, axis=1)),
                      tiled(branches).reshape(L, DC, P, D)], axis=2)
    up = tiled(x["w_up"]).reshape(L, 2, FC, P, D).transpose(0, 2, 1, 3, 4)
    conv = chunked(x["conv_w"]).reshape(L, 3, P, 2, FC).transpose(0, 2, 1, 4, 3)
    twice = lambda a: np.repeat(chunked(a)[..., None], 2, axis=-1)
    small1 = np.stack([packed(SMALL1, SMALL1_W, {
        "b_mod": twice(x["b_mod"][l]), "norm_mix": twice(x["norm_mix"][l]), "norm_ffn": twice(x["norm_ffn"][l]),
        "sink": np.broadcast_to(x["attn_sink"][l], (P, QH)),
        "pool_w": x["pool_w"][l].reshape(2, 2 * HD, HD).transpose(1, 0, 2), "pool_scale": chunked(x["pool_scale"][l]),
        "conv_w": conv[l]}) for l in range(L)])
    feed = {
        "x_in": np.concatenate([chunked(x["x"][0].T.reshape(D, SEQ).T).transpose(1, 2, 0),
                                chunked(x["ctx"][0]).transpose(1, 2, 0)], axis=-1),
        "cond_in": np.stack([chunked(x["c"][0]), chunked(x["c_ctx"])], axis=-1).reshape(P, DC * 2),
        "norm_final_in": chunked(x["norm_final"]),
        "const_dram": constants(), "const1_dram": constants1(), "small1_dram": small1,
        "w_mod": tiled(x["w_mod"]), "w_qk": tiled(np.concatenate([wk, wq], -1)),
        "w_natural": np.concatenate([wv, wu, wf], -1).reshape(L * DC, P, NATURAL),
        "w_merge": merge.reshape(L * DC * 4, P, D), "w_out": tiled(x["w_out"]), "w_up": up.reshape(-1, P, D),
        "w_down": tiled(x["w_down"]),
    }
    feed.update(layout2(x))
    return {name: np.ascontiguousarray(a, np.float32) for name, a in feed.items()}


def kernel(**inputs):
    import concourse.bacc as bacc
    from concourse.bass_utils import run_bass_kernel_spmd

    feed = layout(inputs)
    nc = bacc.Bacc("TRN2", target_bir_lowering=False, num_devices=1)
    dram = {name: nc.dram_tensor(name, a.shape, F32, kind="ExternalInput").ap() for name, a in feed.items()}
    out = nc.dram_tensor("out", (P, DC, SEQ), F32, kind="ExternalOutput").ap()
    program(nc, dram, out)
    got = run_bass_kernel_spmd(nc, [feed], core_ids=[0]).results[0]["out"]
    return np.ascontiguousarray(np.asarray(got).transpose(2, 1, 0)).reshape(1, SEQ, D)
```

```python
from contextlib import ExitStack, contextmanager

import concourse.bass as bass
import numpy as np
from concourse import mybir

F32 = mybir.dt.float32
F32R = mybir.dt.float32r
U32 = mybir.dt.uint32
ALU = mybir.AluOpType
ACT = mybir.ActivationFunctionType
AX_X = mybir.AxisListType.X

P = 128
D = 1024
DC = D // P
DEPTH = 2
SEQ = 256
CTX = 256
TB = SEQ // P
EPS = 1e-6
MASKED = -1e30

HD = 64
QH, KVH = 8, 2
QW, KW = QH * HD, KVH * HD
WINDOW, GRID_W, ROPE_BASE = 128, 64, 10000.0
POOL_WINDOWS = (2, 4, 8, 16)
POOLW = len(POOL_WINDOWS) * HD
FOURW = 4 * HD
FF = 2816
FC = FF // P
NMOD = 6
NATURAL = KW + POOLW + FOURW
QC = QW // P

SBH, MLH, SGG = 6, 6, 4
SBW, MLW, SGW = SBH * HD, MLH * HD, SGG * HD
ML_CONV = 4
NATURAL2 = SBW + MLW + SGW
ZQ, ZK, ZMQ, ZMK, ZO, ZU, ZIF = 0, 3, 6, 9, 12, 15, 17
ZC = 18
GATE_ROWS = 32
YML, YSG = 3, 6
PH, NK, TOPK = 8, 128, 16
HC = 2 * PH
SLOTS = PH * TOPK
EARLY = 28

RAW, SPLIT = 4, 2
PASSES = ((0, 0), (0, 1), (1, 0))


def offsets(*parts):
    at, out = 0, {}
    for name, width in parts:
        out[name] = (at, width)
        at += width
    return out, at


CONST, CONST_W = offsets(("ident", P), ("ones", P), ("half_ones", P), ("iota", NK))
CONST2, CONST2_W = offsets(
    ("suffix", P), ("causal", P), ("before", 3 * P), ("not_before", 3 * P), ("ahead", 2 * P), ("row_of_head", MLH * P),
    ("row_of_pair", MLH // 2 * P))
CONST1, CONST1_W = offsets(
    ("rope_swap", P), ("rope_cos", SEQ + CTX), ("rope_sin", SEQ + CTX), ("window", TB * 2 * SEQ),
    ("pool", TB * len(POOL_WINDOWS) * SEQ), ("dft_time", TB * 2 * SEQ), ("dft_chan", 2 * P))
SMALL1, SMALL1_W = offsets(
    ("b_mod", NMOD * DC * 2), ("norm_mix", DC * 2), ("norm_ffn", DC * 2), ("sink", QH),
    ("pool_w", 2 * HD), ("pool_scale", 2), ("conv_w", 3 * 2 * FC))
SMALL2, SMALL2_W = offsets(
    ("norm1", DC), ("norm2", DC), ("qn_g", 1), ("kn_g", 1), ("conv_w", 6 * ML_CONV), ("conv_b", 6),
    ("out_g", DC), ("if_b", 2), ("vn_g", SGW), ("sg_b", SGG * P), ("sg_w", SGG * P))



@contextmanager
def stage(nc, *names):
    sems, every = [], []
    for name in names:
        base, _, n = name.partition("*")
        made = [nc.alloc_semaphore(f"{base}_{nc.next_id()}") for _ in range(int(n or 1))]
        every += made
        sems.append(made if n else made[0])
    with nc.Block(no_gpsimd_drain=True) as block:
        yield (block, *sems)
    nc.clear_and_free_semaphores(every)
    nc.all_engine_barrier(sem_only=True)


class Steps:

    def __init__(self, eng, sem, done=0):
        self.eng, self.sem, self.done = eng, sem, done

    def step(self, ins):
        ins.then_inc(self.sem, 1)
        self.done = self.done + 1
        return ins

    def settle(self):
        self.eng.wait_ge(self.sem, self.done)

    def __call__(self, ins):
        self.step(ins)
        self.settle()


def tile(dram, n):
    return dram[bass.ds(n, 1)].rearrange("a p m -> p (a m)")


def one(ap, n):
    return ap[:, bass.ds(n, 1), :].rearrange("p a m -> p (a m)")


def turns(eng, n, body):
    with eng.Fori(0, n // RAW) as i:
        for s in range(RAW):
            body(i, s)
    for s in range(n % RAW):
        body(n // RAW, s)


def turns_ahead(eng, n, prepare, finish, first=False):
    full, rest = (n - SPLIT) // RAW, (n - SPLIT) % RAW

    def step(i, s):
        prepare(i + (s + SPLIT) // RAW, (s + SPLIT) % RAW)
        finish(i, s)

    def turn(i):
        for s in range(RAW):
            step(i, s)

    for s in range(SPLIT):
        prepare(0, s)
    if first:
        turn(0)
    if full > first:
        with eng.Fori(int(first), full) as i:
            turn(i)
    for s in range(rest):
        step(full, s)
    for t in range(n - SPLIT, n):
        finish(t // RAW, t % RAW)


def product(nc, out, lhsT, rhs, first, last):
    for n, (a, b) in enumerate(PASSES):
        ins = nc.tensor.matmul(out, lhsT(a), rhs(b), start=first and n == 0, stop=last and n == len(PASSES) - 1)
    return ins


WEIGHT_SEMS = (f"loaded*{RAW}", "high_ready", "low_ready", "halves_used")
HALF = DC // 2


class Weights:

    def __init__(self, k, dram, base, n, width, loaded, high_ready, low_ready, halves_used):
        self.nc, self.ring, self.split = k.nc, k.ring, k.split
        self.dram, self.base, self.n, self.width = dram, base, n, width
        self.loaded, self.high_ready, self.low_ready, self.halves_used = loaded, high_ready, low_ready, halves_used
        self.halves = [slice(0, width // 2), slice(width // 2, width)]

    def load(self, sp):
        def fetch(i, s):
            sp.dma_start(self.ring[:, s, 0:self.width], tile(self.dram, self.base + i * RAW + s)).then_inc(self.loaded[s], 16)

        def refill(i, s):
            sp.wait_ge(self.low_ready, ((i - 1) * RAW + s + 1) * 2)
            fetch(i, s)

        for s in range(RAW):
            fetch(0, s)
        if self.n // RAW > 1:
            with sp.Fori(1, self.n // RAW) as i:
                for s in range(RAW):
                    refill(i, s)
        for s in range(self.n % RAW):
            refill(self.n // RAW, s)

    def high(self, act, i, s):
        act.wait_ge(self.loaded[s], i * 16 + 16)
        for half, cols in enumerate(self.halves):
            act.wait_ge(self.halves_used, (i * RAW + s) * 2 + half + 1)
            self.nc.scalar.activation(self.split[:, s % SPLIT, 0, cols], self.ring[:, s, cols],
                                      ACT.Copy).then_inc(self.high_ready, 1)

    def low(self, eng, i, s, ops=None):
        for half, cols in enumerate(self.halves):
            eng.wait_ge(self.high_ready, (i * RAW + s) * 2 + half + 1)
            (ops or self.nc.vector).tensor_tensor(
                self.split[:, s % SPLIT, 1, cols], self.ring[:, s, cols], self.split[:, s % SPLIT, 0, cols].bitcast(F32),
                ALU.subtract).then_inc(self.low_ready, 1)

    def slots_free(self, pe):
        pe.sem_inc(self.halves_used, 2 * SPLIT)

    def used(self, i, s):
        return (i * RAW + s + 1 + SPLIT) * 2

    def part(self, s, first, width):
        return lambda p: self.split[:, s % SPLIT, p, first:first + width]

    def ready(self, pe, i, s, half):
        pe.wait_ge(self.low_ready, (i * RAW + s) * 2 + half + 1)

    def contract(self, pe, i, s, out, rhs, sums=((0, DC),)):
        for n, (first, end) in enumerate(sums):
            dst = out(n)
            for c in range(first, end):
                if c % HALF == 0:
                    self.ready(pe, i, s, c // HALF)
                last = product(self.nc, dst, self.part(s, c * P, P), rhs(c), c == first, c == end - 1)
                if c % HALF == HALF - 1:
                    last.then_inc(self.halves_used, 1)




def load_stage(k, pairs):
    with stage(k.nc, "loaded") as (block, loaded):

        @block.sync
        def _(sp):
            for out, src in pairs:
                sp.dma_start(out, src).then_inc(loaded, 16)
            sp.wait_ge(loaded, 16 * len(pairs))


def norm_stage(k, tokens, gain, shift, xT, out=None):
    nc, streams = k.nc, tokens // SEQ
    pieces = [(c, s) for c in range(DC) for s in range(streams)]
    total, rstd = k.ps[:, 0, 0:tokens], k.rstd[:, 0:tokens]
    work = k.ring.rearrange("p s m -> p (s m)")[:, 0:DC * tokens].rearrange("p (c t) -> p c t", c=DC)
    cols = [slice(s * SEQ, (s + 1) * SEQ) for s in range(streams)]
    with stage(nc, "squared", "summed", "var_ready", "rooted", "scaled", "high_ready", "low_ready") as (
            block, squared, summed, var_ready, rooted, scaled, high_ready, low_ready):

        @block.scalar
        def _(act):
            for c in range(DC):
                nc.scalar.activation(work[:, c, :], xT[:, c, 0:tokens], ACT.Square).then_inc(squared, 1)
            act.wait_ge(var_ready, 1)
            nc.scalar.activation(rstd, rstd, ACT.Sqrt).then_inc(rooted, 1)
            if out is None:
                for n, (c, s) in enumerate(pieces):
                    act.wait_ge(scaled, n + 1)
                    if shift is None:
                        nc.scalar.activation(k.hT[:, 0, c, cols[s]], work[:, c, cols[s]], ACT.Copy).then_inc(high_ready, 1)
                    else:
                        nc.scalar.activation(k.hT[:, 0, c, cols[s]], work[:, c, cols[s]], ACT.Identity,
                                             bias=shift(c, s)).then_inc(high_ready, 1)

        @block.tensor
        def _(pe):
            for c in range(DC):
                pe.wait_ge(squared, c + 1)
                last = nc.tensor.matmul(total, k.const("ones"), work[:, c, :], start=c == 0, stop=c == DC - 1)
            last.then_inc(summed, 1)

        @block.vector
        def _(dve):
            dve.wait_ge(summed, 1)
            nc.vector.tensor_scalar(rstd, total, 1.0 / D, EPS, ALU.mult, ALU.add).then_inc(var_ready, 1)
            dve.wait_ge(rooted, 1)
            nc.vector.reciprocal(rstd, rstd).then_inc(var_ready, 1)
            dve.wait_ge(var_ready, 2)
            for c, s in pieces:
                dst = work[:, c, cols[s]] if out is None else out[:, c, cols[s]]
                nc.vector.scalar_tensor_tensor(dst, xT[:, c, cols[s]], gain(c, s), k.rstd[:, cols[s]],
                                               ALU.mult, ALU.mult).then_inc(scaled, 1)
            if out is None:
                for n, (c, s) in enumerate(pieces):
                    h, high, low = work[:, c, cols[s]], k.hT[:, 0, c, cols[s]].bitcast(F32), k.hT[:, 1, c, cols[s]]
                    dve.wait_ge(high_ready, n + 1)
                    if shift is None:
                        nc.vector.tensor_tensor(low, h, high, ALU.subtract).then_inc(low_ready, 1)
                    else:
                        nc.vector.scalar_tensor_tensor(low, h, shift(c, s), high, ALU.add, ALU.subtract).then_inc(low_ready, 1)


def residual_stage(k, tokens, dram, base, chunks, src, gate, xT):
    nc, streams = k.nc, tokens // SEQ
    with stage(nc, *WEIGHT_SEMS, "chunk_high", "chunk_low", "summed", "added") as (
            block, loaded, high_ready, low_ready, halves_used, chunk_high, chunk_low, summed, added):
        weights = Weights(k, dram, base, chunks, D, loaded, high_ready, low_ready, halves_used)

        @block.sync
        def _(sp):
            weights.load(sp)

        @block.scalar
        def _(act):
            def split(i, s):
                weights.high(act, i, s)
                act.wait_ge(halves_used, (i * RAW + s + 1) * 2)
                nc.scalar.activation(k.chunk[:, s % SPLIT, 0, 0:tokens], one(src, i * RAW + s)[:, 0:tokens],
                                     ACT.Copy).then_inc(chunk_high, 1)

            turns(act, chunks, split)

        @block.vector
        def _(dve):
            def split(i, s):
                weights.low(dve, i, s)
                dve.wait_ge(chunk_high, i * RAW + s + 1)
                nc.vector.tensor_tensor(k.chunk[:, s % SPLIT, 1, 0:tokens], one(src, i * RAW + s)[:, 0:tokens],
                                        k.chunk[:, s % SPLIT, 0, 0:tokens].bitcast(F32), ALU.subtract).then_inc(chunk_low, 1)

            turns(dve, chunks, split)
            for n in range(DC):
                dve.wait_ge(summed, n + 1)
                for s in range(streams):
                    x, add = xT[:, n, s * SEQ:(s + 1) * SEQ], k.ps[:, n, s * SEQ:(s + 1) * SEQ]
                    if gate is None:
                        nc.vector.tensor_tensor(x, x, add, ALU.add).then_inc(added, 1)
                    else:
                        nc.vector.scalar_tensor_tensor(x, add, gate(n, s), x, ALU.mult, ALU.add).then_inc(added, 1)

        @block.tensor
        def _(pe):
            def add_tile(i, s, first=False, last=False):
                pe.wait_ge(chunk_low, i * RAW + s + 1)
                for n in range(DC):
                    if n % HALF == 0:
                        weights.ready(pe, i, s, n // HALF)
                    ins = product(nc, k.ps[:, n, 0:tokens], weights.part(s, n * P, P),
                                  lambda p: k.chunk[:, s % SPLIT, p, 0:tokens], first, last)
                    if last:
                        ins.then_inc(summed, 1)
                    elif n % HALF == HALF - 1:
                        ins.then_inc(halves_used, 1)

            weights.slots_free(pe)
            full = (chunks - 1) // RAW
            for s in range(RAW):
                add_tile(0, s, first=s == 0)
            if full > 1:
                with pe.Fori(1, full) as i:
                    for s in range(RAW):
                        add_tile(i, s)
            for t in range(full * RAW, chunks):
                add_tile(t // RAW, t % RAW, last=t == chunks - 1)




def mod_stage(k, l, needed, others):
    nc, tiles = k.nc, NMOD * DC
    sums = k.ps[:, 4, 0:2 * tiles]
    with stage(nc, f"loaded*{RAW}", "needed_in", "others_in", "silu_done", "tiles_used", "rows_summed", "rows_kept",
               "turned", "mod_done") as (
            block, loaded, needed_in, others_in, silu_done, tiles_used, rows_summed, rows_kept, turned, mod_done):

        @block.sync
        def _(sp):
            for s in range(RAW):
                sp.dma_start(k.ring[:, s], tile(k.w_mod, l * tiles + s)).then_inc(loaded[s], 16)
            with sp.Fori(1, tiles // RAW) as i:
                for s in range(RAW):
                    sp.wait_ge(tiles_used, (i - 1) * RAW + s + 1)
                    sp.dma_start(k.ring[:, s], tile(k.w_mod, l * tiles + i * RAW + s)).then_inc(loaded[s], 16)

        @block.scalar
        def _(act):
            for out, src in needed:
                act.dma_start(out, src).then_inc(needed_in, 16)
            act.wait_ge(needed_in, 16 * len(needed))
            nc.scalar.activation(k.cond_silu[:, :], k.cond[:, :], ACT.Silu).then_inc(silu_done, 1)
            for out, src in others:
                act.dma_start(out, src).then_inc(others_in, 16)
            if others:
                act.wait_ge(others_in, 16 * len(others))

        @block.tensor
        def _(pe):
            pe.wait_ge(needed_in, 16 * len(needed))

            def turn(g):
                pe.wait_ge(rows_kept, 2 * g + 2)
                for n in range(DC):
                    last = nc.tensor.transpose(sums[:, 2 * (g * DC + n):2 * (g * DC + n) + 2],
                                               k.mod_rows[0:2, g % 2, n * P:(n + 1) * P], k.const("ident")[0:2, 0:2])
                last.then_inc(turned, 1)

            pe.wait_ge(silu_done, 1)
            for g in range(NMOD):
                if g >= 2:
                    pe.wait_ge(rows_kept, 2 * (g - 2) + 2)
                for c in range(DC):
                    t = g * DC + c
                    pe.wait_ge(loaded[t % RAW], 16 * (t // RAW) + 16)
                    for half in range(2):
                        last = nc.tensor.matmul(k.ps[0:2, g % 2 * 2 + half, :], k.cond_silu[:, 2 * c:2 * c + 2],
                                                k.ring[:, t % RAW, half * 512:(half + 1) * 512],
                                                start=c == 0, stop=c == DC - 1)
                    last.then_inc(tiles_used, 1)
                if g >= 1:
                    turn(g - 1)
            turn(NMOD - 1)

        @block.vector
        def _(dve):
            done = Steps(dve, mod_done)
            for g in range(NMOD):
                dve.wait_ge(tiles_used, (g + 1) * DC)
                if g >= 2:
                    dve.wait_ge(turned, g - 1)
                for half in range(2):
                    nc.vector.tensor_copy(k.mod_rows[0:2, g % 2, half * 512:(half + 1) * 512],
                                          k.ps[0:2, g % 2 * 2 + half, :]).then_inc(rows_kept, 1)
            dve.wait_ge(turned, NMOD)
            dve.wait_ge(needed_in, 16 * len(needed))
            mod = k.mod.rearrange("p n c -> p (n c)")
            done(nc.vector.tensor_tensor(mod, sums, k.small1("b_mod"), ALU.add))
            for norm, scale in (("norm_mix", 1), ("norm_ffn", 4)):
                sc = mod[:, scale * DC * 2:(scale + 1) * DC * 2]
                done(nc.vector.scalar_tensor_tensor(sc, sc, 1.0, k.small1(norm), ALU.add, ALU.mult))


def qk_stage(k, l, q_tokens):
    nc, n = k.nc, 1 + QC
    tokens = [SEQ + CTX] + [q_tokens] * QC
    raw, rot = k.ps[:, 0:2, :], k.ps[:, 2:4, :]
    at = lambda t: (t // RAW, t % RAW)
    with stage(nc, *WEIGHT_SEMS, "copied", "swapped", "rotated") as (
            block, loaded, high_ready, low_ready, halves_used, copied, swapped, rotated):
        weights = Weights(k, k.w_qk, l * n, n, D, loaded, high_ready, low_ready, halves_used)

        @block.sync
        def _(sp):
            weights.load(sp)

        @block.tensor
        def _(pe):
            def swap(j):
                pe.wait_ge(copied, j + 1)
                if j >= 2:
                    pe.wait_ge(rotated, 3 * (j - 2) + 2)
                nc.tensor.matmul(rot[:, j % 2, 0:tokens[j]], k.const1("rope_swap"), k.qkT[:, j, 0:tokens[j]],
                                 start=True, stop=True).then_inc(swapped, 1)

            weights.slots_free(pe)
            for j in range(n):
                if j >= 2:
                    pe.wait_ge(copied, j - 1)
                weights.contract(pe, *at(j), lambda n: raw[:, j % 2, 0:tokens[j]],
                                 lambda c: lambda p: k.hT[:, p, c, 0:tokens[j]])
                if j >= 1:
                    swap(j - 1)
            swap(n - 1)

        @block.scalar
        def _(act):
            for j in range(-SPLIT, n):
                if j + SPLIT < n:
                    weights.high(act, *at(j + SPLIT))
                if j >= 0:
                    act.wait_ge(halves_used, weights.used(*at(j)))
                    nc.scalar.activation(k.qkT[:, j, 0:tokens[j]], raw[:, j % 2, 0:tokens[j]], ACT.Copy).then_inc(copied, 1)

        @block.vector
        def _(dve):
            done = Steps(dve, rotated)
            for j in range(-SPLIT, n):
                if j + SPLIT < n:
                    weights.low(dve, *at(j + SPLIT))
                if j < 0:
                    continue
                t = slice(0, tokens[j])
                dve.wait_ge(swapped, j + 1)
                done(nc.vector.tensor_tensor(k.qkT[:, j, t], k.qkT[:, j, t], k.const1("rope_cos")[:, t], ALU.mult))
                done(nc.vector.tensor_tensor(k.rstd[:, t], rot[:, j % 2, t], k.const1("rope_sin")[:, t], ALU.mult))
                done(nc.vector.tensor_tensor(k.qkT[:, j, t], k.qkT[:, j, t], k.rstd[:, t], ALU.add))


def natural_stage(k, l, q_tokens):
    nc, half = k.nc, NATURAL // 2
    full = q_tokens // P
    blocks = (SEQ + CTX) // P
    parts = [(b, h, half if b < full else KW) for h in range(2) for b in range(full if h else blocks)]
    first_of = (0, blocks)
    with stage(nc, *WEIGHT_SEMS, "summed", "copied") as (
            block, loaded, high_ready, low_ready, halves_used, summed, copied):
        weights = Weights(k, k.w_natural, l * DC, DC, NATURAL, loaded, high_ready, low_ready, halves_used)

        @block.sync
        def _(sp):
            weights.load(sp)

        @block.tensor
        def _(pe):
            weights.slots_free(pe)
            for c in range(DC):
                for n, (b, h, cols) in enumerate(parts):
                    if n in (0, first_of[1]):
                        weights.ready(pe, c // RAW, c % RAW, h)
                    last = product(nc, k.ps[:, 2 * b + h, 0:cols], lambda p: k.hT[:, p, c, b * P:(b + 1) * P],
                                   weights.part(c % RAW, h * half, cols), c == 0, c == DC - 1)
                    if c == DC - 1:
                        last.then_inc(summed, 1)
                    elif n + 1 in (first_of[1], len(parts)):
                        last.then_inc(halves_used, 1)

        @block.scalar
        def _(act):
            turns(act, DC, lambda i, s: weights.high(act, i, s))
            for n, (b, h, cols) in enumerate(parts):
                if n % 2 == 0:
                    act.wait_ge(summed, n + 1)
                    nc.scalar.activation(k.natural[:, b, h * half:h * half + cols], k.ps[:, 2 * b + h, 0:cols],
                                         ACT.Copy).then_inc(copied, 1)

        @block.vector
        def _(dve):
            turns(dve, DC, lambda i, s: weights.low(dve, i, s))
            for n, (b, h, cols) in enumerate(parts):
                if n % 2 == 1:
                    dve.wait_ge(summed, n + 1)
                    nc.vector.tensor_copy(k.natural[:, b, h * half:h * half + cols], k.ps[:, 2 * b + h, 0:cols]).then_inc(copied, 1)


def attention_stage(k, q_tokens):
    nc, keys = k.nc, SEQ + CTX
    units = [(b, h) for b in range(q_tokens // P) for h in range(QH)]
    scale = float(HD) ** -0.5

    def first_key(b):
        return 0 if b < TB else SEQ

    with stage(nc, "scored", "masked", "max_ready", "exp_ready", "norm_step", "probs_ready", "turned",
               "probs_turned", "weighed", "kept_high", "kept") as (
            block, scored, masked, max_ready, exp_ready, norm_step, probs_ready, turned, probs_turned, weighed,
            kept_high, kept):

        def output(u):
            b, h = units[u]
            base = HD * (h // QC)
            return k.ps[base:base + HD, 4 + u % 4, 0:P], slice(base, base + HD), h % QC, slice(b * P, (b + 1) * P)

        @block.tensor
        def _(pe):
            def score(u):
                b, h = units[u]
                base = HD * (h // QC)
                if u >= 2:
                    pe.wait_ge(masked, u - 1)
                nc.tensor.matmul(k.ps[:, u % 2, first_key(b):keys], k.qkT[base:base + HD, 1 + h % QC, b * P:(b + 1) * P],
                                 k.qkT[base:base + HD, 0, first_key(b):keys], start=True, stop=True).then_inc(scored, 1)

            def turn(u):
                b, _ = units[u]
                pe.wait_ge(probs_ready, u + 1)
                if u >= 2:
                    pe.wait_ge(probs_turned, u - 1)
                for j in range(first_key(b) // P, keys // P):
                    last = nc.tensor.transpose(k.ps[:, 2 + u % 2, j * P:(j + 1) * P],
                                               k.probs[:, u % 2, j * P:(j + 1) * P], k.const("ident"))
                last.then_inc(turned, 1)

            def weigh(u):
                b, _ = units[u]
                out, rows, _, _ = output(u)
                pe.wait_ge(probs_turned, u + 1)
                if u >= 4:
                    pe.wait_ge(kept, u - 3)
                first = first_key(b) // P
                for j in range(first, keys // P):
                    last = nc.tensor.matmul(out, k.natural[:, j, rows],
                                            k.probsT[:, u % 2, j * P:(j + 1) * P], start=j == first, stop=j == keys // P - 1)
                last.then_inc(weighed, 1)

            score(0)
            score(1)
            for u in range(len(units)):
                if u + 2 < len(units):
                    score(u + 2)
                turn(u)
                if u >= 1:
                    weigh(u - 1)
            weigh(len(units) - 1)

        @block.vector
        def _(dve):
            def soften(u):
                b, h = units[u]
                cols = slice(first_key(b), keys)
                s = k.scores[:, u % 2, cols]
                m = k.stat[:, u % 2, 0:1]
                dve.wait_ge(scored, u + 1)
                if u >= 2:
                    dve.wait_ge(exp_ready, 2 * (u - 1))
                nc.vector.scalar_tensor_tensor(s, k.ps[:, u % 2, cols], scale,
                                               k.const1("window")[:, (b % TB) * 2 * SEQ:(b % TB + 1) * 2 * SEQ][:, cols],
                                               ALU.mult, ALU.add).then_inc(masked, 1)
                dve.wait_ge(masked, u + 1)
                nc.vector.reduce_max(m, s, AX_X).then_inc(max_ready, 1)
                dve.wait_ge(max_ready, 2 * u + 1)
                nc.vector.tensor_scalar(m, m, k.small1("sink")[:, h:h + 1], -1.0, ALU.max, ALU.mult).then_inc(max_ready, 1)

            def normalise(u):
                b, _ = units[u]
                cols = slice(first_key(b), keys)
                den = k.stat[:, u % 2, 3:4]
                dve.wait_ge(exp_ready, 2 * u + 2)
                nc.vector.tensor_tensor(den, k.stat[:, u % 2, 1:2], k.stat[:, u % 2, 2:3], ALU.add).then_inc(norm_step, 1)
                dve.wait_ge(norm_step, 2 * u + 1)
                nc.vector.reciprocal(den, den).then_inc(norm_step, 1)
                dve.wait_ge(norm_step, 2 * u + 2)
                if u >= 2:
                    dve.wait_ge(turned, u - 1)
                nc.vector.tensor_scalar(k.probs[:, u % 2, cols], k.exps[:, u % 2, cols], den, None,
                                        ALU.mult).then_inc(probs_ready, 1)

            def keep(u):
                summed, rows, c, cols = output(u)
                dve.wait_ge(kept_high, u + 1)
                nc.vector.tensor_tensor(k.branchT[rows, 1, c, cols], summed, k.branchT[rows, 0, c, cols].bitcast(F32),
                                        ALU.subtract).then_inc(kept, 1)

            soften(0)
            for u in range(len(units)):
                if u + 1 < len(units):
                    soften(u + 1)
                normalise(u)
                if u >= 3:
                    keep(u - 3)
            for u in range(len(units) - 3, len(units)):
                keep(u)

        @block.scalar
        def _(act):
            def exponents(u):
                b, h = units[u]
                cols = slice(first_key(b), keys)
                neg_max = k.stat[:, u % 2, 0:1]
                act.wait_ge(max_ready, 2 * u + 2)
                if u >= 2:
                    act.wait_ge(probs_ready, u - 1)
                nc.scalar.activation(k.exps[:, u % 2, cols], k.scores[:, u % 2, cols], ACT.Exp, bias=neg_max,
                                     accum_out=k.stat[:, u % 2, 1:2]).then_inc(exp_ready, 1)
                nc.scalar.activation(k.stat[:, u % 2, 2:3], k.small1("sink")[:, h:h + 1], ACT.Exp,
                                     bias=neg_max).then_inc(exp_ready, 1)

            def copy_turned(u):
                b, _ = units[u]
                cols = slice(first_key(b), keys)
                act.wait_ge(turned, u + 1)
                if u >= 2:
                    act.wait_ge(weighed, u - 1)
                nc.scalar.activation(k.probsT[:, u % 2, cols], k.ps[:, 2 + u % 2, cols], ACT.Copy).then_inc(probs_turned, 1)

            def keep_high(u):
                summed, rows, c, cols = output(u)
                act.wait_ge(weighed, u + 1)
                nc.scalar.activation(k.branchT[rows, 0, c, cols], summed, ACT.Copy).then_inc(kept_high, 1)

            exponents(0)
            for u in range(len(units)):
                if u + 1 < len(units):
                    exponents(u + 1)
                copy_turned(u)
                if u >= 2:
                    keep_high(u - 2)
            for u in range(len(units) - 2, len(units)):
                keep_high(u)


def pool_fourier_stage(k, q_tokens):
    nc, groups = k.nc, len(POOL_WINDOWS)
    pool = k.const1("pool").rearrange("p (b g t) -> p b g t", b=TB, g=groups)
    dft = k.const1("dft_time").rearrange("p (b t) -> p b t", b=TB)
    pool_w = k.small1("pool_w").rearrange("p (a d) -> p a d", a=2)
    streams = range(q_tokens // SEQ)
    n = 2 * len(streams)
    with stage(nc, "pooled", "pool_kept", "pool_mixed", "pool_high", "pool_scaled", "timed", "time_kept", "channeled",
               "four_high", "four_kept") as (
            block, pooled, pool_kept, pool_mixed, pool_high, pool_scaled, timed, time_kept, channeled,
            four_high, four_kept):

        @block.tensor
        def _(pe):
            for u in range(n):
                s, a = u // 2, u % 2
                if u >= 2:
                    pe.wait_ge(pool_kept, u - 1)
                for half in range(2):
                    g = 2 * a + half
                    for b in range(TB):
                        last = nc.tensor.matmul(k.ps[HD * half:HD * (half + 1), a, 0:SEQ],
                                                k.natural[:, s * TB + b, KW + g * HD:KW + (g + 1) * HD],
                                                pool[:, b, g, :], start=b == 0, stop=b == TB - 1)
                last.then_inc(pooled, 1)
                if u >= 2:
                    pe.wait_ge(time_kept, u - 1)
                for b in range(TB):
                    last = nc.tensor.matmul(k.ps[:, 2 + a, :], k.natural[:, s * TB + b, KW + POOLW + a * P:KW + POOLW + (a + 1) * P],
                                            dft[:, b, :], start=b == 0, stop=b == TB - 1)
                last.then_inc(timed, 1)
            for u in range(n):
                a = u % 2
                pe.wait_ge(pool_kept, u + 1)
                if u >= 2:
                    pe.wait_ge(pool_scaled, u - 1)
                for half in range(2):
                    rows = slice(HD * half, HD * (half + 1))
                    last = nc.tensor.matmul(k.ps[rows, 4 + a, 0:SEQ], pool_w[rows, a, :], k.pooledT[rows, u, :],
                                            start=True, stop=True)
                last.then_inc(pool_mixed, 1)
                pe.wait_ge(time_kept, u + 1)
                if u >= 2:
                    pe.wait_ge(four_kept, u - 1)
                for part in range(2):
                    last = nc.tensor.matmul(k.ps[:, 6 + a, 0:SEQ], k.const1("dft_chan")[:, part * P:(part + 1) * P],
                                            k.timedT[:, u, part * SEQ:(part + 1) * SEQ], start=part == 0, stop=part == 1)
                last.then_inc(channeled, 1)

        @block.vector
        def _(dve):
            for u in range(n):
                dve.wait_ge(pooled, u + 1)
                nc.vector.tensor_copy(k.pooledT[:, u, :], k.ps[:, u % 2, 0:SEQ]).then_inc(pool_kept, 1)
            for u in range(n):
                s, a = u // 2, u % 2
                dve.wait_ge(pool_mixed, u + 1)
                high, low = (k.branchT[:, p, QC + a, s * SEQ:(s + 1) * SEQ] for p in range(2))
                scale = k.small1("pool_scale")[:, a:a + 1]
                nc.vector.tensor_scalar(high, k.ps[:, 4 + a, 0:SEQ], scale, None, ALU.mult).then_inc(pool_high, 1)
                dve.wait_ge(pool_high, u + 1)
                nc.vector.scalar_tensor_tensor(low, k.ps[:, 4 + a, 0:SEQ], scale, high.bitcast(F32),
                                               ALU.mult, ALU.subtract).then_inc(pool_scaled, 1)
                high, low = (k.branchT[:, p, QC + 2 + a, s * SEQ:(s + 1) * SEQ] for p in range(2))
                dve.wait_ge(four_high, u + 1)
                nc.vector.tensor_tensor(low, k.ps[:, 6 + a, 0:SEQ], high.bitcast(F32), ALU.subtract).then_inc(four_kept, 1)

        @block.scalar
        def _(act):
            for u in range(n):
                act.wait_ge(timed, u + 1)
                nc.scalar.activation(k.timedT[:, u, :], k.ps[:, 2 + u % 2, :], ACT.Copy).then_inc(time_kept, 1)
            for u in range(n):
                s, a = u // 2, u % 2
                act.wait_ge(channeled, u + 1)
                nc.scalar.activation(k.branchT[:, 0, QC + 2 + a, s * SEQ:(s + 1) * SEQ], k.ps[:, 6 + a, 0:SEQ],
                                     ACT.Copy).then_inc(four_high, 1)


def merge_stage(k, l, tokens):
    nc = k.nc
    gates, parts = 3, ((0, QC), (QC, QC + 2), (QC + 2, DC))
    t = slice(0, tokens)
    n_tiles = (gates + 1) * DC
    with stage(nc, *WEIGHT_SEMS, "gate_ready", "products", "merged") as (
            block, loaded, high_ready, low_ready, halves_used, gate_ready, products, merged):
        weights = Weights(k, k.w_merge, l * n_tiles, n_tiles, D, loaded, high_ready, low_ready, halves_used)

        @block.sync
        def _(sp):
            weights.load(sp)

        @block.tensor
        def _(pe):
            def use(n, s):
                def branch(g):
                    pe.wait_ge(products, n * gates + g + 1)
                    return k.ps[:, gates + g, t]

                if s < gates:
                    pe.wait_ge(gate_ready, n * gates + s + 1)
                    weights.contract(pe, n, s, lambda n: k.ps[:, s, t], lambda c: lambda p: k.hT[:, p, c, t])
                else:
                    weights.contract(pe, n, s, branch, lambda c: lambda p: k.branchT[:, p, c, t], parts)

            weights.slots_free(pe)
            turns(pe, n_tiles, use)

        @block.scalar
        def _(act):
            def keep_gate(n, s):
                if s < gates:
                    act.wait_ge(halves_used, weights.used(n, s))
                    act.wait_ge(products, n * gates + s + 1)
                    nc.scalar.activation(k.gate[:, s, t], k.ps[:, s, t], ACT.Sigmoid).then_inc(gate_ready, 1)

            act.sem_inc(gate_ready, gates)
            turns_ahead(act, n_tiles, lambda i, s: weights.high(act, i, s), keep_gate)

        @block.vector
        def _(dve):
            def merge(n, s):
                if s < gates:
                    return
                y = one(k.yT, n)[:, t]
                dve.wait_ge(halves_used, weights.used(n, s))
                for g in range(gates):
                    dve.wait_ge(gate_ready, (n + 1) * gates + g + 1)
                    if g:
                        dve.wait_ge(merged, n * 2 + g - 1)
                    nc.vector.tensor_tensor(y if g == 0 else k.part[:, t], k.gate[:, g, t], k.ps[:, gates + g, t],
                                            ALU.mult).then_inc(products, 1)
                    if g:
                        dve.wait_ge(products, (n + 1) * gates + g + 1)
                        nc.vector.tensor_tensor(y, y, k.part[:, t], ALU.add).then_inc(merged, 1)

            dve.sem_inc(products, gates)
            turns_ahead(dve, n_tiles, lambda i, s: weights.low(dve, i, s), merge)


def ffn_up_stage(k, l, tokens):
    nc, streams = k.nc, tokens // SEQ
    t, n_tiles = slice(0, tokens), 2 * FC
    first_tile = lambda i: isinstance(i, int) and i == 0
    tap = [one(k.small1("conv_w").rearrange("p (w n) -> p w n", w=3), w) for w in range(3)]
    with stage(nc, *WEIGHT_SEMS, "centred", "convolved", "activated", "finished") as (
            block, loaded, high_ready, low_ready, halves_used, centred, convolved, activated, finished):
        weights = Weights(k, k.w_up, l * n_tiles, n_tiles, D, loaded, high_ready, low_ready, halves_used)

        @block.sync
        def _(sp):
            weights.load(sp)

        @block.tensor
        def _(pe):
            def use(i, s):
                pe.wait_ge(convolved, (i * RAW + s) * 2 + 2)
                weights.contract(pe, i, s, lambda n: k.ps[:, s, t], lambda c: lambda p: k.hT[:, p, c, t])

            weights.slots_free(pe)
            turns(pe, n_tiles, use)

        @block.scalar
        def _(act):
            def centre(i, s):
                act.wait_ge(halves_used, weights.used(i, s))
                act.wait_ge(finished, i * 2 + s // 2 + 1)
                nc.scalar.activation(k.conv[:, s, t], k.ps[:, s, t], ACT.Copy,
                                     scale=tap[1][:, bass.ds(i * RAW + s, 1)]).then_inc(centred, 1)

            def activate(i, s):
                act.wait_ge(convolved, (i * RAW + s) * 2 + 10)
                nc.scalar.activation(k.conv[:, s, t], k.conv[:, s, t], ACT.Silu).then_inc(activated, 1)

            def finish(i, s):
                centre(i, s)
                if s == 2:
                    activate(i, 1)
                elif s == 0 and not first_tile(i):
                    activate(i - 1, RAW - 1)

            turns_ahead(act, n_tiles, lambda i, s: weights.high(act, i, s), finish, first=True)
            activate(n_tiles // RAW - 1, RAW - 1)

        @block.vector
        def _(dve):
            def convolve(i, s):
                u = k.ps[:, s, t].rearrange("p (a t) -> p a t", a=streams)
                a = k.conv[:, s, t].rearrange("p (a t) -> p a t", a=streams)
                dve.wait_ge(centred, i * RAW + s + 1)
                nc.vector.scalar_tensor_tensor(a[:, :, 1:SEQ], u[:, :, 0:SEQ - 1], tap[0][:, bass.ds(i * RAW + s, 1)],
                                               a[:, :, 1:SEQ], ALU.mult, ALU.add).then_inc(convolved, 1)
                dve.wait_ge(convolved, (i * RAW + s) * 2 + 9)
                nc.vector.scalar_tensor_tensor(a[:, :, 0:SEQ - 1], u[:, :, 1:SEQ], tap[2][:, bass.ds(i * RAW + s, 1)],
                                               a[:, :, 0:SEQ - 1], ALU.mult, ALU.add).then_inc(convolved, 1)

            def gate(i, s):
                dve.wait_ge(activated, i * 2 + s // 2 + 1)
                nc.vector.tensor_tensor(one(k.actT, i * 2 + s // 2)[:, t], k.conv[:, s - 1, t], k.conv[:, s, t],
                                        ALU.mult).then_inc(finished, 1)

            def finish(i, s):
                convolve(i, s)
                if s == 2:
                    gate(i, 1)
                elif s == 0 and not first_tile(i):
                    gate(i - 1, RAW - 1)

            dve.sem_inc(convolved, 8)
            dve.sem_inc(finished, 2)
            turns_ahead(dve, n_tiles, lambda i, s: weights.low(dve, i, s), finish, first=True)
            gate(n_tiles // RAW - 1, RAW - 1)


def first_block(k, sb):
    first_loads = [(k.xT[:, :, :], k.x_in), (k.const1_sb[:, :], k.const1_dram), (k.norm_final[:, :], k.norm_final_in)]
    for l in range(DEPTH):
        tokens = SEQ if l == DEPTH - 1 else SEQ + CTX
        every = SEQ + CTX
        with ExitStack() as scope:
            k.mod_rows = sb(scope, f"mod_rows_{l}", 2, D)
            needed = [(k.cond[:, :], k.cond_in), (k.const_sb[:, :], k.const_dram)] if l == 0 else []
            mod_stage(k, l, [(k.small1_sb[:, :], k.small1_dram[l]), *needed], first_loads if l == 0 else [])

        def part(m):
            return lambda c, s: k.mod[:, m * DC + c, s:s + 1]

        norm_stage(k, every, part(1), part(0), k.xT)
        with ExitStack() as scope:
            k.yT = sb(scope, f"yT_{l}", DC, every)
            with ExitStack() as mixers:
                k.branchT = sb(mixers, f"branchT_{l}", 2, DC, every, dtype=F32R)
                k.qkT, k.natural = sb(mixers, f"qkT_{l}", 1 + QC, every), sb(mixers, f"natural_{l}", every // P, NATURAL)
                work = sb(mixers, f"mixer_work_{l}", 4 * 2 * every)
                attend, pool, merge = Carver(work), Carver(work), Carver(work)
                k.scores, k.exps, k.probs, k.probsT = (attend(2, every) for _ in range(4))
                k.pooledT, k.timedT = pool(4, SEQ), pool(4, 2 * SEQ)
                k.gate, k.part = merge(3, every), merge(every)
                qk_stage(k, l, tokens)
                natural_stage(k, l, tokens)
                attention_stage(k, tokens)
                pool_fourier_stage(k, tokens)
                merge_stage(k, l, tokens)
            with ExitStack() as chunks:
                k.chunk = sb(chunks, f"y_chunk_{l}", SPLIT, 2, every, dtype=F32R)
                residual_stage(k, tokens, k.w_out, l * DC, DC, k.yT, part(2), k.xT)
        norm_stage(k, tokens, part(4), part(3), k.xT)
        with ExitStack() as scope:
            k.actT = sb(scope, f"actT_{l}", FC, every)
            k.conv = sb(scope, f"conv_{l}", RAW, every)
            k.chunk = sb(scope, f"act_chunk_{l}", SPLIT, 2, every, dtype=F32R)
            ffn_up_stage(k, l, tokens)
            residual_stage(k, tokens, k.w_down, l * FC, FC, k.actT, part(5), k.xT)
    norm_stage(k, SEQ, lambda c, s: k.norm_final[:, c:c + 1], None, k.xT, k.x2T)




def transposed_stage(k, dram, base, tiles, dst):
    nc = k.nc
    with stage(nc, *WEIGHT_SEMS, "copied") as (block, loaded, high_ready, low_ready, halves_used, copied):
        weights = Weights(k, dram, base, tiles, D, loaded, high_ready, low_ready, halves_used)

        @block.sync
        def _(sp):
            weights.load(sp)

        @block.scalar
        def _(act):
            turns(act, tiles, lambda i, s: weights.high(act, i, s))

        @block.tensor
        def _(pe):
            def use(i, s):
                pe.wait_ge(copied, i * RAW + s + 1)
                weights.contract(pe, i, s, lambda n: k.ps[:, s, 0:SEQ], lambda c: lambda p: k.hT[:, p, c, :])

            weights.slots_free(pe)
            turns(pe, tiles, use)

        @block.vector
        def _(dve):
            def copy(i, s):
                dve.wait_ge(halves_used, weights.used(i, s))
                nc.vector.tensor_copy(one(dst, i * RAW + s), k.ps[:, s, 0:SEQ]).then_inc(copied, 1)

            dve.sem_inc(copied, RAW)
            turns_ahead(dve, tiles, lambda i, s: weights.low(dve, i, s), copy)


def natural2_stage(k, l):
    nc, half = k.nc, NATURAL2 // 2
    parts = [(b, h) for h in range(2) for b in range(TB)]
    with stage(nc, *WEIGHT_SEMS, "summed", "copied", "gate_step") as (
            block, loaded, high_ready, low_ready, halves_used, summed, copied, gate_step):
        weights = Weights(k, k.w_natural2, l * DC, DC, NATURAL2, loaded, high_ready, low_ready, halves_used)

        @block.sync
        def _(sp):
            weights.load(sp)

        @block.tensor
        def _(pe):
            weights.slots_free(pe)
            for c in range(DC):
                for b, h in parts:
                    if b == 0:
                        weights.ready(pe, c // RAW, c % RAW, h)
                    last = product(nc, k.ps[:, 2 * b + h, 0:half], lambda p: k.hT[:, p, c, b * P:(b + 1) * P],
                                   weights.part(c % RAW, h * half, half), c == 0, c == DC - 1)
                    if c == DC - 1:
                        last.then_inc(summed, 1)
                    elif b == TB - 1:
                        last.then_inc(halves_used, 1)

        @block.scalar
        def _(act):
            turns(act, DC, lambda i, s: weights.high(act, i, s))
            for n, (b, h) in enumerate(parts):
                if n % 2 == 0:
                    act.wait_ge(summed, n + 1)
                    nc.scalar.activation(k.natural2[:, b, h * half:(h + 1) * half], k.ps[:, 2 * b + h, 0:half],
                                         ACT.Copy).then_inc(copied, 1)

        @block.vector
        def _(dve):
            gate = Steps(dve, gate_step)
            turns(dve, DC, lambda i, s: weights.low(dve, i, s))
            for g in range(2):
                row = k.gate_rows[0:MLH, g, :]
                gate(nc.vector.tensor_copy(row, k.zT[g * GATE_ROWS:g * GATE_ROWS + MLH, ZIF, :]))
                gate(nc.vector.tensor_scalar(row, row, k.small2("if_b")[0:MLH, g:g + 1], None, ALU.add))
            for n, (b, h) in enumerate(parts):
                if n % 2 == 1:
                    dve.wait_ge(summed, n + 1)
                    nc.vector.tensor_copy(k.natural2[:, b, h * half:(h + 1) * half], k.ps[:, 2 * b + h, 0:half]).then_inc(copied, 1)


def head_norm_stage(k, src, chunks, gain):
    nc = k.nc
    squares, wide = k.squares[:, 0:chunks, :], 2 * SEQ
    flat = squares.rearrange("p c t -> p (c t)")
    parts = chunks * SEQ // wide
    sums = k.ps[:, 0:parts, :].rearrange("p b t -> p (b t)")
    with stage(nc, "squared", "summed", "var_ready", "rooted", "scaled") as (block, squared, summed, var_ready, rooted, scaled):

        @block.scalar
        def _(act):
            for n in range(parts):
                nc.scalar.activation(squares[:, 2 * n:2 * n + 2, :], src[:, 2 * n:2 * n + 2, :], ACT.Square).then_inc(squared, 1)
            act.wait_ge(var_ready, 1)
            nc.scalar.activation(flat, flat, ACT.Sqrt).then_inc(rooted, 1)

        @block.tensor
        def _(pe):
            for n in range(parts):
                pe.wait_ge(squared, n + 1)
                nc.tensor.matmul(k.ps[:, n, :], k.const("half_ones"), flat[:, n * wide:(n + 1) * wide],
                                 start=True, stop=True).then_inc(summed, 1)

        @block.vector
        def _(dve):
            dve.wait_ge(summed, parts)
            nc.vector.tensor_scalar(flat, sums, 1.0 / HD, EPS, ALU.mult, ALU.add).then_inc(var_ready, 1)
            dve.wait_ge(rooted, 1)
            nc.vector.reciprocal(flat, flat).then_inc(var_ready, 1)
            dve.wait_ge(var_ready, 2)
            for c in range(chunks):
                nc.vector.scalar_tensor_tensor(src[:, c, :], src[:, c, :], gain(c), squares[:, c, :],
                                               ALU.mult, ALU.mult).then_inc(scaled, 1)


def stick_breaking_stage(k):
    nc, width = k.nc, 3 * P
    half = SBH // 2 * width
    z, a, keep = k.z, k.z_abs, k.keep

    def flat(x, part):
        return x.rearrange("p h w -> p (h w)")[:, part * half:(part + 1) * half]

    with stage(nc, "scored", "score_kept", "magnitude", "log_ready", "keep_step", "suffixed", "exponent", "weights_ready",
               "weighed", "kept") as (
            block, scored, score_kept, magnitude, log_ready, keep_step, suffixed, exponent, weights_ready, weighed, kept):

        @block.tensor
        def _(pe):
            for h in range(SBH):
                base, c = HD * (h % 2), h // 2
                rows = slice(base, base + HD)
                if h >= 4:
                    pe.wait_ge(score_kept, h - 3)
                for b in range(TB):
                    last = nc.tensor.matmul(k.ps[:, h % 4, b * SEQ:b * SEQ + SEQ - b * P], k.zT[rows, ZK + c, b * P:(b + 1) * P],
                                            k.zT[rows, ZQ + c, b * P:SEQ], start=True, stop=True)
                last.then_inc(scored, 1)
            for h in range(SBH):
                pe.wait_ge(keep_step, 3 * (h // (SBH // 2)) + 3)
                if h >= 2:
                    pe.wait_ge(exponent, 2 * (h - 2) + 1)
                nc.tensor.matmul(k.ps[:, 4 + h % 2, 0:SEQ], k.const2("suffix"), keep[:, h, 0:SEQ], start=True, stop=False)
                nc.tensor.matmul(k.ps[:, 4 + h % 2, P:SEQ], k.const("ones"), keep[:, h, SEQ:width], start=False, stop=True)
                nc.tensor.matmul(k.ps[:, 4 + h % 2, SEQ:width], k.const2("suffix"), keep[:, h, SEQ:width],
                                 start=True, stop=True).then_inc(suffixed, 1)
            for h in range(SBH):
                base, c = HD * (h % 2), h // 2
                out = k.ps[base:base + HD, 6 + c % 2, 0:SEQ]
                pe.wait_ge(weights_ready, h + 1)
                if h >= 4:
                    pe.wait_ge(kept, h // 2 - 1)
                cols = slice(h * HD, (h + 1) * HD)
                nc.tensor.matmul(out, k.natural2[:, 0, cols], a[:, h, 0:SEQ], start=True, stop=False)
                nc.tensor.matmul(out[:, P:SEQ], k.natural2[:, 1, cols], a[:, h, SEQ:width],
                                 start=False, stop=True).then_inc(weighed, 1)

        @block.scalar
        def _(act):
            for h in range(SBH):
                act.wait_ge(scored, h + 1)
                nc.scalar.activation(z[:, h, :], k.ps[:, h % 4, 0:width], ACT.Copy,
                                     scale=float(HD) ** -0.5).then_inc(score_kept, 1)
            for part in range(2):
                act.wait_ge(score_kept, (part + 1) * SBH // 2)
                nc.scalar.activation(flat(a, part), flat(z, part), ACT.Abs).then_inc(magnitude, 1)
            for part in range(2):
                act.wait_ge(magnitude, part + 1)
                nc.scalar.activation(flat(a, part), flat(a, part), ACT.Exp, scale=-1.0).then_inc(magnitude, 1)
                act.wait_ge(magnitude, part + 3)
                nc.scalar.activation(flat(a, part), flat(a, part), ACT.Ln, bias=1.0).then_inc(log_ready, 1)
            for h in range(SBH):
                act.wait_ge(exponent, 2 * h + 2)
                nc.scalar.activation(a[:, h, :], k.arg[:, h, :], ACT.Exp).then_inc(weights_ready, 1)

        @block.vector
        def _(dve):
            for part in range(2):
                n = 3 * part
                dve.wait_ge(score_kept, (part + 1) * SBH // 2)
                nc.vector.tensor_scalar(flat(keep, part), flat(z, part), -1.0, 0.0, ALU.mult, ALU.min).then_inc(keep_step, 1)
                dve.wait_ge(keep_step, n + 1)
                dve.wait_ge(log_ready, part + 1)
                nc.vector.tensor_tensor(flat(keep, part), flat(keep, part), flat(a, part), ALU.subtract).then_inc(keep_step, 1)
                dve.wait_ge(keep_step, n + 2)
                heads = slice(part * SBH // 2, (part + 1) * SBH // 2)
                nc.vector.tensor_tensor(keep[:, heads, :], keep[:, heads, :],
                                        k.const2("before").unsqueeze(1).broadcast_to([P, SBH // 2, width]),
                                        ALU.mult).then_inc(keep_step, 1)
            for h in range(SBH):
                dve.wait_ge(suffixed, h + 1)
                nc.vector.tensor_tensor(k.arg[:, h, :], z[:, h, :], k.ps[:, 4 + h % 2, 0:width], ALU.add).then_inc(exponent, 1)
                dve.wait_ge(exponent, 2 * h + 1)
                nc.vector.tensor_tensor(k.arg[:, h, :], k.arg[:, h, :], k.const2("not_before"), ALU.add).then_inc(exponent, 1)
            for c in range(SBH // 2):
                dve.wait_ge(weighed, 2 * c + 2)
                nc.vector.tensor_copy(k.y2T[:, c, :], k.ps[:, 6 + c % 2, 0:SEQ]).then_inc(kept, 1)


def mlstm_prepare_stage(k):
    nc = k.nc
    h = slice(0, MLH)
    conv_w = k.small2("conv_w").rearrange("p (c w) -> p c w", c=6)
    i_row, f_row = k.gate_rows[h, 0, :], k.gate_rows[h, 1, :]
    bcum, a, M, carry, floor, w_row = (k.rows[h, n, :] for n in range(6))
    chunk = [slice(n * P, (n + 1) * P) for n in range(TB)]
    with stage(nc, "conv_step", "convolved", "conv_ready", "scan_step", "log_step", "row_step", "turned", "column_ready",
               "key_scaled") as (
            block, conv_step, convolved, conv_ready, scan_step, log_step, row_step, turned, column_ready, key_scaled):

        @block.scalar
        def _(act):
            nc.scalar.activation(k.soft[h, :], f_row, ACT.Abs).then_inc(log_step, 1)
            act.wait_ge(log_step, 1)
            nc.scalar.activation(k.soft[h, :], k.soft[h, :], ACT.Exp, scale=-1.0).then_inc(log_step, 1)
            act.wait_ge(log_step, 2)
            nc.scalar.activation(k.soft[h, :], k.soft[h, :], ACT.Ln, bias=1.0).then_inc(log_step, 1)
            act.wait_ge(scan_step, 10)
            nc.scalar.activation(floor, floor, ACT.Exp, scale=-1.0).then_inc(row_step, 1)
            nc.scalar.activation(carry[:, chunk[1]], M[:, chunk[1]], ACT.Exp, scale=-1.0, bias=k.m_carry[h, :]).then_inc(row_step, 1)
            nc.scalar.activation(w_row[:, chunk[0]], a[:, chunk[0]], ACT.Exp, bias=k.neg_last[h, :]).then_inc(row_step, 1)
            for c in range(6):
                act.wait_ge(convolved, c + 1)
                nc.scalar.activation(k.qkconv[:, c, :], k.qkconv[:, c, :], ACT.Silu).then_inc(conv_ready, 1)

        @block.vector
        def _(dve):
            scan = Steps(dve, scan_step)
            dve.wait_ge(log_step, 3)
            scan(nc.vector.tensor_scalar(f_row, f_row, 0.0, None, ALU.min))
            scan(nc.vector.tensor_tensor(f_row, f_row, k.soft[h, :], ALU.subtract))
            for n in range(TB):
                scan.step(nc.vector.tensor_tensor_scan(bcum[:, chunk[n]], k.const("ones")[h, :], f_row[:, chunk[n]], 0.0,
                                                       ALU.mult, ALU.add))
            scan.settle()
            scan(nc.vector.tensor_tensor(a, i_row, bcum, ALU.subtract))
            scan(nc.vector.tensor_tensor_scan(M[:, chunk[0]], a[:, chunk[0]], a[:, chunk[0]], 0.0, ALU.max, ALU.max))
            last = slice(P - 1, P)
            scan.step(nc.vector.tensor_tensor(k.m_carry[h, :], bcum[:, last], M[:, last], ALU.add))
            scan(nc.vector.tensor_scalar(k.neg_last[h, :], M[:, last], -1.0, None, ALU.mult))
            scan(nc.vector.tensor_tensor_scan(M[:, chunk[1]], a[:, chunk[1]], a[:, chunk[1]], k.m_carry[h, :], ALU.max, ALU.max))
            scan.step(nc.vector.tensor_tensor(floor, bcum, M, ALU.add))
            conv = Steps(dve, conv_step)
            for c in range(6):
                x, y = k.zT[:, ZMQ + c, :], k.qkconv[:, c, :]
                conv(nc.vector.tensor_scalar(y, x, conv_w[:, c, ML_CONV - 1:ML_CONV], k.small2("conv_b")[:, c:c + 1],
                                             ALU.mult, ALU.add))
                for back in range(1, ML_CONV):
                    w = conv_w[:, c, ML_CONV - 1 - back:ML_CONV - back]
                    tap = nc.vector.scalar_tensor_tensor(y[:, back:SEQ], x[:, 0:SEQ - back], w, y[:, back:SEQ], ALU.mult, ALU.add)
                    if back < ML_CONV - 1:
                        conv(tap)
                    else:
                        tap.then_inc(convolved, 1)
            dve.wait_ge(conv_ready, 6)
            nc.vector.tensor_scalar(k.qkconv[:, 3:6, :], k.qkconv[:, 3:6, :], float(HD) ** -0.5, None,
                                    ALU.mult).then_inc(key_scaled, 1)
            dve.wait_ge(turned, 1)
            nc.vector.tensor_copy(k.columns[:, :, :], k.ps[:, 0, 0:3 * MLH].rearrange("p (n h) -> p n h", n=3)).then_inc(column_ready, 1)
            dve.wait_ge(turned, 2)
            nc.vector.tensor_copy(k.floor[:, 0:2, :], k.ps[:, 1, :].rearrange("p (n t) -> p n t", n=2)).then_inc(column_ready, 1)
            nc.vector.tensor_copy(k.floor[:, 2, :], k.ps[:, 2, 0:SEQ]).then_inc(column_ready, 1)
            for c in range(MLH // 2):
                nc.vector.tensor_tensor(k.q_carry[:, c, :], k.qkconv[:, c, chunk[1]], k.ps[:, 3, c * P:(c + 1) * P],
                                        ALU.mult).then_inc(column_ready, 1)
            dve.wait_ge(turned, 3)
            dve.wait_ge(column_ready, 1)
            for n in range(MLH):
                nc.vector.tensor_scalar(k.k_keep[:, n * HD:(n + 1) * HD], k.ps[:, 4, n * HD:(n + 1) * HD],
                                        k.columns[:, 2, n:n + 1], None, ALU.mult).then_inc(column_ready, 1)

        @block.tensor
        def _(pe):
            pe.wait_ge(row_step, 3)
            for n, row in enumerate((a[:, chunk[0]], a[:, chunk[1]], w_row[:, chunk[0]])):
                last = nc.tensor.transpose(k.ps[:, 0, n * MLH:(n + 1) * MLH], row, k.const("ident")[h, 0:MLH])
            last.then_inc(turned, 1)
            pair = k.const2("row_of_pair").rearrange("p (c m) -> p c m", c=MLH // 2)
            for c in range(MLH // 2):
                nc.tensor.matmul(k.ps[:, 1 + c // 2, c % 2 * SEQ:(c % 2 + 1) * SEQ], pair[h, c, :], floor, start=True, stop=True)
                last = nc.tensor.matmul(k.ps[:, 3, c * P:(c + 1) * P], pair[h, c, :], carry[:, chunk[1]], start=True, stop=True)
            last.then_inc(turned, 1)
            pe.wait_ge(key_scaled, 1)
            for c in range(MLH // 2):
                last = nc.tensor.transpose(k.ps[:, 4, c * P:(c + 1) * P], k.qkconv[:, 3 + c, 0:P], k.const("ident"))
            last.then_inc(turned, 1)


def mlstm_stage(k):
    nc = k.nc
    h6 = slice(0, MLH)
    M = k.rows[h6, 2, :]
    chunk = [slice(n * P, (n + 1) * P) for n in range(TB)]
    row = k.const2("row_of_head").rearrange("p (h m) -> p h m", h=MLH)
    with stage(nc, "spread", "masked", "decayed", "scored", "probs_ready", "state_summed", "state_kept", "summed",
               "den_step", "finished") as (
            block, spread, masked, decayed, scored, probs_ready, state_summed, state_kept, summed, den_step, finished):

        @block.tensor
        def _(pe):
            for h in range(MLH):
                rows = slice(HD * (h % 2), HD * (h % 2 + 1))
                keys = k.k_keep[:, h * HD:(h + 1) * HD]
                nc.tensor.matmul(k.ps[rows, 0, h // 2 * P:h // 2 * P + HD], keys,
                                 k.natural2[:, 0, SBW + h * HD:SBW + (h + 1) * HD], start=True, stop=True)
                last = nc.tensor.matmul(k.ps[rows, 0, h // 2 * P + HD:(h // 2 + 1) * P], keys, k.const("ones")[:, 0:HD],
                                        start=True, stop=True)
            last.then_inc(state_summed, 1)
            for h in range(MLH):
                base, c = HD * (h % 2), h // 2
                rows = slice(base, base + HD)
                if h >= 2:
                    pe.wait_ge(masked, h - 1)
                nc.tensor.matmul(k.ps[:, 1 + h % 2, 0:SEQ], row[h6, h, :], M, start=True, stop=True).then_inc(spread, 1)
                if h >= 2:
                    pe.wait_ge(probs_ready, h - 1)
                for n in range(TB):
                    last = nc.tensor.matmul(k.ps[:, 3 + h % 2, chunk[n]], k.qkconv[rows, 3 + c, chunk[n]],
                                            k.qkconv[rows, c, chunk[n]], start=True, stop=True)
                last.then_inc(scored, 1)
                pe.wait_ge(probs_ready, h + 1)
                if h == 0:
                    pe.wait_ge(state_kept, 1)
                if h % 2 == 0 and c >= 1:
                    pe.wait_ge(finished, c)
                probs = k.ml_probs[:, h % 2, :]
                for bank, within, state in ((5, [k.natural2[:, n, SBW + h * HD:SBW + (h + 1) * HD] for n in range(TB)], 0),
                                            (6, [k.const("ones")[:, 0:HD]] * TB, HD)):
                    nc.tensor.matmul(k.ps[rows, bank, chunk[0]], within[0], probs[:, chunk[0]], start=True, stop=True)
                    nc.tensor.matmul(k.ps[rows, bank, chunk[1]], k.state[rows, c * P + state:c * P + state + HD],
                                     k.q_carry[rows, c, :], start=True, stop=False)
                    last = nc.tensor.matmul(k.ps[rows, bank, chunk[1]], within[1], probs[:, chunk[1]], start=False, stop=True)
                last.then_inc(summed, 1)

        @block.scalar
        def _(act):
            act.wait_ge(state_summed, 1)
            nc.scalar.activation(k.state[:, :], k.ps[:, 0, 0:MLH // 2 * P], ACT.Copy).then_inc(state_kept, 1)
            for h in range(MLH):
                act.wait_ge(masked, h + 1)
                for n in range(TB):
                    nc.scalar.activation(k.decay[:, h % 2, chunk[n]], k.ahead[:, h % 2, chunk[n]], ACT.Exp, scale=-1.0,
                                         bias=k.columns[:, n, h:h + 1]).then_inc(decayed, 1)
                if h % 2:
                    act.wait_ge(summed, h + 1)
                    nc.scalar.activation(k.den[:, :], k.ps[:, 6, 0:SEQ], ACT.Abs).then_inc(den_step, 1)

        @block.vector
        def _(dve):
            for h in range(MLH):
                dve.wait_ge(spread, h + 1)
                if h >= 2:
                    dve.wait_ge(decayed, 2 * (h - 1))
                nc.vector.tensor_tensor(k.ahead[:, h % 2, :], k.ps[:, 1 + h % 2, 0:SEQ], k.const2("ahead"), ALU.add).then_inc(masked, 1)
                dve.wait_ge(scored, h + 1)
                dve.wait_ge(decayed, 2 * h + 2)
                if h >= 2:
                    dve.wait_ge(summed, h - 1)
                nc.vector.tensor_tensor(k.ml_probs[:, h % 2, :], k.decay[:, h % 2, :], k.ps[:, 3 + h % 2, 0:SEQ],
                                        ALU.mult).then_inc(probs_ready, 1)
                if h % 2:
                    c = h // 2
                    dve.wait_ge(den_step, 3 * c + 1)
                    nc.vector.tensor_tensor(k.den[:, :], k.den[:, :], k.floor[:, c, :], ALU.max).then_inc(den_step, 1)
                    dve.wait_ge(den_step, 3 * c + 2)
                    nc.vector.reciprocal(k.den[:, :], k.den[:, :]).then_inc(den_step, 1)
                    dve.wait_ge(den_step, 3 * c + 3)
                    nc.vector.tensor_tensor(k.y2T[:, YML + c, :], k.den[:, :], k.ps[:, 5, 0:SEQ], ALU.mult).then_inc(finished, 1)


def gating_stage(k):
    nc = k.nc
    first = SBW + MLW
    groups = TB * SGG
    sg_w = k.small2("sg_w").rearrange("p (g t) -> p g t", g=SGG)
    with stage(nc, "gelu_done", "squared", "var_step", "rooted", "normed", "masked", "gated", "finished") as (
            block, gelu_done, squared, var_step, rooted, normed, masked, gated, finished):

        @block.scalar
        def _(act):
            for b in range(TB):
                v = k.natural2[:, b, first:first + SGW]
                nc.scalar.activation(v, v, ACT.Gelu_apprx_tanh).then_inc(gelu_done, 1)
            u = k.zT[:, ZU:ZU + 2, :]
            nc.scalar.activation(u, u, ACT.Gelu_apprx_tanh).then_inc(gelu_done, 1)
            for b in range(TB):
                act.wait_ge(gelu_done, b + 1)
                nc.scalar.activation(k.v_square[:, b * SGW:(b + 1) * SGW], k.natural2[:, b, first:first + SGW],
                                     ACT.Square).then_inc(squared, 1)
            act.wait_ge(var_step, 2)
            nc.scalar.activation(k.v_rstd[:, :], k.v_rstd[:, :], ACT.Sqrt).then_inc(rooted, 1)

        @block.vector
        def _(dve):
            for g in range(SGG):
                nc.vector.tensor_tensor(sg_w[:, g, :], sg_w[:, g, :], k.const2("causal"), ALU.mult).then_inc(masked, 1)
            dve.wait_ge(squared, TB)
            nc.vector.reduce_sum(k.v_rstd[:, :], k.v_square[:, :].rearrange("p (g d) -> p g d", g=groups), AX_X).then_inc(var_step, 1)
            dve.wait_ge(var_step, 1)
            nc.vector.tensor_scalar(k.v_rstd[:, :], k.v_rstd[:, :], 1.0 / HD, EPS, ALU.mult, ALU.add).then_inc(var_step, 1)
            dve.wait_ge(rooted, 1)
            nc.vector.reciprocal(k.v_rstd[:, :], k.v_rstd[:, :]).then_inc(var_step, 1)
            dve.wait_ge(var_step, 3)
            for b in range(TB):
                for g in range(SGG):
                    v = k.natural2[:, b, first + g * HD:first + (g + 1) * HD]
                    nc.vector.scalar_tensor_tensor(v, v, k.v_rstd[:, b * SGG + g:b * SGG + g + 1],
                                                   k.small2("vn_g")[:, g * HD:(g + 1) * HD], ALU.mult, ALU.mult).then_inc(normed, 1)
            dve.wait_ge(gelu_done, TB + 1)
            for a in range(2):
                dve.wait_ge(gated, a + 1)
                nc.vector.tensor_tensor(k.y2T[:, YSG + a, :], k.zT[:, ZU + a, :], k.ps[:, a, 0:SEQ], ALU.mult).then_inc(finished, 1)

        @block.tensor
        def _(pe):
            pe.wait_ge(normed, groups)
            pe.wait_ge(masked, SGG)
            for a in range(2):
                for g in (2 * a, 2 * a + 1):
                    rows = slice(HD * (g % 2), HD * (g % 2 + 1))
                    for b in range(TB):
                        out = k.ps[rows, a, b * P:(b + 1) * P]
                        nc.tensor.matmul(out, k.natural2[:, b, first + g * HD:first + (g + 1) * HD], sg_w[:, g, :],
                                         start=True, stop=False)
                        last = nc.tensor.matmul(out, k.const("ones")[0:1, 0:HD], k.small2("sg_b")[0:1, g * P:(g + 1) * P],
                                                start=False, stop=True)
                last.then_inc(gated, 1)


def output_gate_stage(k):
    nc = k.nc
    with stage(nc, "gate_ready", "gated") as (block, gate_ready, gated):

        @block.scalar
        def _(act):
            o = k.zT[:, ZO:ZO + 3, :]
            nc.scalar.activation(o, o, ACT.Sigmoid).then_inc(gate_ready, 1)

        @block.vector
        def _(dve):
            dve.wait_ge(gate_ready, 1)
            y = k.y2T[:, YML:YML + 3, :]
            nc.vector.tensor_tensor(y, y, k.zT[:, ZO:ZO + 3, :], ALU.mult).then_inc(gated, 1)


def choose_stage(k, l):
    nc, pairs = k.nc, TB * PH
    n_tiles, low = HC + EARLY, -3.0e38
    last_turn = n_tiles // RAW - 1
    best = lambda half: slice(8 * half, 8 * half + 8)
    with stage(nc, *WEIGHT_SEMS, "keys_in", "kept", "scored", "scores_used", "row_step", "step", "gate_step", "turned",
               "slots_ready") as (
            block, loaded, high_ready, low_ready, halves_used, keys_in, kept, scored, scores_used, row_step,
            step, gate_step, turned, slots_ready):
        weights = Weights(k, k.w_choose, l * n_tiles, n_tiles, D, loaded, high_ready, low_ready, halves_used)

        @block.sync
        def _(sp):
            sp.dma_start(k.keysT, tile(k.peer_keys, l)).then_inc(keys_in, 16)
            weights.load(sp)

        @block.gpsimd
        def _(pool):
            turns(pool, n_tiles, lambda i, s: weights.low(pool, i, s, nc.gpsimd))

        @block.tensor
        def _(pe):
            def use(i, s):
                pe.wait_ge(kept, i * RAW + s + 1)
                weights.contract(pe, i, s, lambda n: k.ps[:, s, 0:SEQ], lambda c: lambda p: k.hT[:, p, c, :])

            def score(i, s):
                pe.wait_ge(kept, i * RAW + s + 1 + RAW)
                pe.wait_ge(scores_used, i * RAW + s + 1)
                for b in range(TB):
                    last = nc.tensor.matmul(k.ps[:, RAW + s, b * NK:(b + 1) * NK], k.queryT[:, s, b * P:(b + 1) * P],
                                            k.keysT[:, bass.ds((i * RAW + s) * NK, NK)], start=True, stop=True)
                last.then_inc(scored, 1)

            weights.slots_free(pe)
            pe.wait_ge(keys_in, 16)
            for s in range(RAW):
                use(0, s)
                if s:
                    score(0, s - 1)
            with pe.Fori(1, HC // RAW) as i:
                for s in range(RAW):
                    use(i, s)
                    score(i + (s - 1) // RAW, (s - 1) % RAW)
            score(HC // RAW - 1, RAW - 1)
            with pe.Fori(HC // RAW, last_turn + 1) as i:
                for s in range(RAW):
                    use(i, s)
            pe.wait_ge(kept, n_tiles + RAW)
            pe.wait_ge(gate_step, 5)
            for n, x in enumerate((k.key_i, k.key_j, k.gates)):
                for b in range(TB):
                    last = nc.tensor.transpose(k.ps[:, n, b * P:(b + 1) * P], x[:, b * SLOTS:(b + 1) * SLOTS], k.const("ident"))
            last.then_inc(turned, 1)

        @block.scalar
        def _(act):
            def high(i, s):
                weights.high(act, i + (s + SPLIT) // RAW, (s + SPLIT) % RAW)

            def keep_query(i, s):
                act.wait_ge(halves_used, weights.used(i, s))
                act.wait_ge(scored, i * RAW + s + 1)
                nc.scalar.activation(k.queryT[:, s, :], k.ps[:, s, 0:SEQ], ACT.Copy).then_inc(kept, 1)

            def keep_early(i, s):
                act.wait_ge(halves_used, weights.used(i, s))
                nc.scalar.activation(one(k.early, i * RAW + s - HC), k.ps[:, s, 0:SEQ], ACT.Gelu_apprx_tanh).then_inc(kept, 1)

            act.sem_inc(kept, RAW)
            act.sem_inc(scored, RAW)
            for s in range(SPLIT):
                weights.high(act, 0, s)
            with act.Fori(0, HC // RAW) as i:
                for s in range(RAW):
                    high(i, s)
                    keep_query(i, s)
            with act.Fori(HC // RAW, last_turn) as i:
                for s in range(RAW):
                    high(i, s)
                    keep_early(i, s)
            for s in range(RAW):
                if s + SPLIT < RAW:
                    high(last_turn, s)
                keep_early(last_turn, s)
            act.wait_ge(gate_step, 1)
            nc.scalar.activation(k.gates[:, :], k.gates[:, :], ACT.Exp).then_inc(gate_step, 1)

        @block.vector
        def _(dve):
            def best_keys(n):
                scores = lambda b: k.ps[:, RAW + n % RAW, b * NK:(b + 1) * NK]
                spare = lambda b: k.key_spare[:, n % 2, b * NK:(b + 1) * NK]
                value = lambda b, half: k.half_val[:, b * HC + n, best(half)]
                at = lambda b, half: k.half_at[:, b * HC + n, best(half)]
                dve.wait_ge(scored, n + 1 + RAW)
                for b in range(TB):
                    rows.step(nc.vector.max(value(b, 0), scores(b)))
                rows.settle()
                for b in range(TB):
                    rows.step(nc.vector.max_index(at(b, 0), value(b, 0), scores(b)))
                    rows.step(nc.vector.match_replace(spare(b), value(b, 0), scores(b), low))
                rows.settle()
                dve.sem_inc(scores_used, 1)
                for b in range(TB):
                    rows.step(nc.vector.max(value(b, 1), spare(b)))
                rows.settle()
                for b in range(TB):
                    rows.step(nc.vector.max_index(at(b, 1), value(b, 1), spare(b)))

            rows = Steps(dve, row_step)
            dve.sem_inc(scores_used, RAW)
            for n in range(HC):
                best_keys(n)
            rows.settle()
            s = Steps(dve, step)

            def top16(n, scores, spare, values, index, width):
                at = lambda x, r: x[:, r * width:(r + 1) * width]
                for r in range(n):
                    s.step(nc.vector.max(values[:, r, best(0)], at(scores, r)))
                s.settle()
                for r in range(n):
                    s.step(nc.vector.max_index(index[:, r, best(0)], values[:, r, best(0)], at(scores, r)))
                    s.step(nc.vector.match_replace(at(spare, r), values[:, r, best(0)], at(scores, r), low))
                s.settle()
                for r in range(n):
                    s.step(nc.vector.max(values[:, r, best(1)], at(spare, r)))
                s.settle()
                for r in range(n):
                    s.step(nc.vector.max_index(index[:, r, best(1)], values[:, r, best(1)], at(spare, r)))
                s.settle()

            s(nc.vector.tensor_copy(k.half_key[:, :, :], k.half_at[:, :, :]))
            for n in range(pairs):
                cand = k.cand[:, n * 256:(n + 1) * 256].rearrange("p (a b) -> p a b", a=TOPK)
                s.step(nc.vector.tensor_tensor(cand, k.half_val[:, 2 * n, :].unsqueeze(2).broadcast_to([P, TOPK, TOPK]),
                                               k.half_val[:, 2 * n + 1, :].unsqueeze(1).broadcast_to([P, TOPK, TOPK]), ALU.add))
            s.settle()
            top16(pairs, k.cand, k.cand_spare, k.pair_val, k.pair_at, TOPK * TOPK)
            flat_at = k.pair_at[:, :, :].rearrange("p n k -> p (n k)")
            for key, half, op, by in ((k.key_i, 0, ALU.logical_shift_right, 4), (k.key_j, 1, ALU.bitwise_and, TOPK - 1)):
                s(nc.vector.tensor_scalar(k.place_int[:, :], flat_at, by, None, op))
                s(nc.vector.tensor_copy(k.place[:, :], k.place_int[:, :]))
                for n in range(pairs):
                    hot = k.cand[:, n * 256:(n + 1) * 256].rearrange("p (k a) -> p k a", a=TOPK)
                    s.step(nc.vector.tensor_tensor(hot, k.place[:, n * TOPK:(n + 1) * TOPK].unsqueeze(2).broadcast_to([P, TOPK, TOPK]),
                                                   k.const("iota")[:, 0:TOPK].unsqueeze(1).broadcast_to([P, TOPK, TOPK]), ALU.is_equal))
                s.settle()
                for n in range(pairs):
                    hot = k.cand[:, n * 256:(n + 1) * 256].rearrange("p (k a) -> p k a", a=TOPK)
                    s.step(nc.vector.tensor_tensor(hot, hot, k.half_key[:, 2 * n + half, :].unsqueeze(1).broadcast_to([P, TOPK, TOPK]),
                                                   ALU.mult))
                s.settle()
                s(nc.vector.reduce_sum(key[:, :], k.cand[:, :].rearrange("p (m a) -> p m a", a=TOPK), AX_X))
            gates = k.gates[:, :].rearrange("p (n k) -> p n k", k=TOPK)
            nc.vector.tensor_tensor(gates, k.pair_val[:, :, :], k.pair_val[:, :, 0:1].broadcast_to([P, pairs, TOPK]),
                                    ALU.subtract).then_inc(gate_step, 1)
            dve.wait_ge(gate_step, 2)
            nc.vector.reduce_sum(k.gate_sum[:, :], gates, AX_X).then_inc(gate_step, 1)
            dve.wait_ge(gate_step, 3)
            nc.vector.reciprocal(k.gate_sum[:, :], k.gate_sum[:, :]).then_inc(gate_step, 1)
            dve.wait_ge(gate_step, 4)
            nc.vector.tensor_tensor(gates, gates, k.gate_sum[:, :].unsqueeze(2).broadcast_to([P, pairs, TOPK]),
                                    ALU.mult).then_inc(gate_step, 1)
            dve.wait_ge(turned, 1)
            for n, x in enumerate((k.slot_i, k.slot_j, k.slot_gate)):
                nc.vector.tensor_copy(x[:, :], k.ps[:, n, 0:SEQ]).then_inc(slots_ready, 1)


def scatter_stage(k):
    nc, lot, lots, late = k.nc, 4, 4, NK - EARLY
    turns_all = SEQ // (lots * lot)
    iota = k.const("iota").unsqueeze(1).broadcast_to([P, lot, NK])
    token = lambda i, n: (i * lots + n) * lot

    def lagged(eng, make, keep, lag):
        for n in range(lots):
            make(0, n)
            if n >= lag:
                keep(0, n - lag)
        with eng.Fori(1, turns_all) as i:
            for n in range(lots):
                make(i, n)
                keep(i + (n - lag) // lots, (n - lag) % lots)
        for n in range(lots - lag, lots):
            keep(turns_all - 1, n)

    with stage(nc, "one_hot", "gated", "spread", "copied", "weighted") as (block, one_hot, gated, spread, copied, weighted):

        @block.vector
        def _(dve):
            def one_hots(i, n):
                dve.wait_ge(spread, i * lots + n + 1)
                for hot, slot, many in ((k.hot_i, k.slot_i, lot - 1), (k.hot_j, k.slot_j, lot)):
                    keys = slot[:, bass.ds(token(i, n), many)].unsqueeze(2).broadcast_to([P, many, NK])
                    nc.vector.tensor_tensor(hot[:, n * lot:n * lot + many, :], iota[:, 0:many, :], keys,
                                            ALU.is_equal).then_inc(one_hot, 1)
                t = bass.ds(token(i, n) + lot - 1, 1)
                nc.vector.tensor_scalar(k.hot_i[:, n * lot + lot - 1, :], k.const("iota"), k.slot_i[:, t], k.slot_gate[:, t],
                                        ALU.is_equal, ALU.mult).then_inc(one_hot, 1)

            def weigh_early(i, n):
                early = k.early[:, :, bass.ds(token(i, n), lot)]
                dve.wait_ge(copied, i * lots + n + 1)
                nc.vector.tensor_tensor(early, early, k.ps[:, n, :].rearrange("p (t j) -> p j t", t=lot)[:, 0:EARLY, :],
                                        ALU.mult).then_inc(weighted, 1)

            dve.sem_inc(weighted, lots)
            lagged(dve, one_hots, weigh_early, 2)

        @block.tensor
        def _(pe):
            pe.sem_inc(spread, lots)
            with pe.Fori(0, turns_all) as i:
                for n in range(lots):
                    pe.wait_ge(weighted, i * lots + n + 1)
                    pe.wait_ge(one_hot, (i * lots + n) * 3 + 3)
                    for u in range(lot):
                        if u < lot - 1:
                            pe.wait_ge(gated, (i * lots + n) * (lot - 1) + u + 1)
                        last = nc.tensor.matmul(k.ps[:, n, u * NK:(u + 1) * NK], k.hot_i[:, n * lot + u, :],
                                                k.hot_j[:, n * lot + u, :], start=True, stop=True)
                    last.then_inc(spread, 1)

        @block.scalar
        def _(act):
            def gate(i, n):
                act.wait_ge(one_hot, (i * lots + n) * 3 + 1)
                for u in range(lot - 1):
                    hot = k.hot_i[:, n * lot + u, :]
                    nc.scalar.activation(hot, hot, ACT.Copy,
                                         scale=k.slot_gate[:, bass.ds(token(i, n) + u, 1)]).then_inc(gated, 1)

            def keep(i, n):
                act.wait_ge(spread, i * lots + n + 1 + lots)
                nc.scalar.activation(
                    k.dense[:, bass.ds(token(i, n) * late, lot * late)].rearrange("p (t j) -> p t j", t=lot),
                    k.ps[:, n, :].rearrange("p (t j) -> p t j", t=lot)[:, :, EARLY:NK], ACT.Copy).then_inc(copied, 1)

            lagged(act, gate, keep, 1)


def experts_stage(k, l):
    nc, n_tiles = k.nc, EARLY + 2 * (NK - EARLY)
    first_turn, last_turn = EARLY // RAW, n_tiles // RAW - 1
    dense = k.dense[:, :].rearrange("p (t j) -> p t j", j=NK - EARLY)
    outs = [k.ps[:, 2 + n, :] for n in range(4)]

    def turn_loop(eng, body):
        def turn(i, first=False, last=False):
            j = 2 * (i - first_turn) + EARLY
            tiles = [(True, j, 0) if first else (False, j - 1, 1), (True, j + 1, 1), (False, j, 0),
                     (False, j + 1, 1) if last else (True, j + 2, 0)]
            for s, (is_u, j, buf) in enumerate(tiles):
                body(i, s, is_u, j, buf, first, last)

        turn(first_turn, first=True)
        with eng.Fori(first_turn + 1, last_turn) as i:
            turn(i)
        turn(last_turn, last=True)

    def prepare_ahead(prepare, i, s, last):
        if not last or s + SPLIT < RAW:
            prepare(i + (s + SPLIT) // RAW, (s + SPLIT) % RAW)

    with stage(nc, *WEIGHT_SEMS, "gelu_done", "weight_step", "weighted", "kept", "turned", "added") as (
            block, loaded, high_ready, low_ready, halves_used, gelu_done, weight_step, weighted, kept, turned, added):
        weights = Weights(k, k.peer_uv, l * n_tiles, n_tiles, D, loaded, high_ready, low_ready, halves_used)

        @block.sync
        def _(sp):
            weights.load(sp)

        @block.tensor
        def _(pe):
            def activate(i, s, j, buf):
                pe.wait_ge(gelu_done, j - EARLY + 1)
                weights.contract(pe, i, s, lambda n: k.ps[:, buf, 0:SEQ], lambda c: lambda p: k.hT[:, p, c, :])

            def combine(i, s, j, buf, first, last):
                pe.wait_ge(weighted, j + 3)
                for half in range(2):
                    weights.ready(pe, i, s, half)
                    for b in range(TB):
                        ins = product(nc, outs[2 * b + half], lambda p: k.weight[:, buf, p, b * P:(b + 1) * P],
                                      weights.part(s, half * 512, 512), first, last)
                    ins.then_inc(halves_used, 1)

            def use(i, s, is_u, j, buf, first, last):
                if is_u:
                    activate(i, s, j, buf)
                else:
                    combine(i, s, j, buf, False, last and s == RAW - 1)

            weights.slots_free(pe)
            for s in range(RAW):
                combine(0, s, s, s % 2, s == 0, False)
            with pe.Fori(1, first_turn) as i:
                for s in range(RAW):
                    combine(i, s, i * RAW + s, s % 2, False, False)
            turn_loop(pe, use)
            pe.wait_ge(kept, len(outs))
            for c in range(DC):
                if c >= 2:
                    pe.wait_ge(added, c - 1)
                for b in range(TB):
                    ins = nc.tensor.transpose(k.ps[:, c % 2, b * P:(b + 1) * P], k.y_natural[:, b, c * P:(c + 1) * P],
                                              k.const("ident"))
                ins.then_inc(turned, 1)

        @block.scalar
        def _(act):
            def activate(i, s, is_u, j, buf, first, last):
                prepare_ahead(lambda i, s: weights.high(act, i, s), i, s, last)
                if is_u:
                    act.wait_ge(halves_used, weights.used(i, s))
                    act.wait_ge(weighted, j + 1)
                    nc.scalar.activation(k.gelu[:, buf, :], k.ps[:, buf, 0:SEQ], ACT.Gelu_apprx_tanh).then_inc(gelu_done, 1)

            act.sem_inc(gelu_done, 2)
            for s in range(SPLIT):
                weights.high(act, 0, s)
            with act.Fori(0, first_turn) as i:
                for s in range(RAW):
                    prepare_ahead(lambda i, s: weights.high(act, i, s), i, s, False)
            turn_loop(act, activate)
            act.wait_ge(halves_used, weights.used(last_turn, RAW - 1))
            for n, out in enumerate(outs):
                nc.scalar.activation(k.y_natural[:, n // 2, n % 2 * 512:(n % 2 + 1) * 512], out, ACT.Copy).then_inc(kept, 1)

        @block.vector
        def _(dve):
            def split_early(i, s):
                j = i * RAW + s
                w, high, low = one(k.early, j), k.weight[:, s % 2, 0, :], k.weight[:, s % 2, 1, :]
                dve.wait_ge(halves_used, (j + SPLIT) * 2 - 2)
                nc.vector.tensor_copy(high, w).then_inc(weight_step, 1)
                dve.wait_ge(weight_step, j + 1)
                nc.vector.tensor_tensor(low, w, high.bitcast(F32), ALU.subtract).then_inc(weighted, 1)

            def weigh(i, s, is_u, j, buf, first, last):
                prepare_ahead(lambda i, s: weights.low(dve, i, s), i, s, last)
                if not is_u:
                    return
                high, low = k.weight[:, buf, 0, :], k.weight[:, buf, 1, :]
                dve.wait_ge(gelu_done, j - EARLY + 3)
                dve.wait_ge(weighted, j + 2)
                if first and s < 2:
                    dve.wait_ge(halves_used, weights.used(first_turn - 1, RAW - 2 + s))
                else:
                    dve.wait_ge(halves_used, weights.used(first_turn, 2) + (j - EARLY - 2) * 4)
                nc.vector.tensor_tensor(k.gated[:, :], k.gelu[:, buf, :], dense[:, :, bass.ds(j - EARLY, 1)].rearrange("p t j -> p (t j)"),
                                        ALU.mult).then_inc(weight_step, 1)
                dve.wait_ge(weight_step, j * 2 - EARLY + 1)
                nc.vector.tensor_copy(high, k.gated[:, :]).then_inc(weight_step, 1)
                dve.wait_ge(weight_step, j * 2 - EARLY + 2)
                nc.vector.tensor_tensor(low, k.gated[:, :], high.bitcast(F32), ALU.subtract).then_inc(weighted, 1)

            dve.sem_inc(weighted, 2)
            def prepare_early(i, s):
                weights.low(dve, i, s)
                split_early(i, s)

            for s in range(SPLIT):
                prepare_early(0, s)
            with dve.Fori(0, first_turn - 1) as i:
                for s in range(RAW):
                    prepare_ahead(prepare_early, i, s, False)
            for s in range(RAW):
                prepare_ahead(prepare_early if s + SPLIT < RAW else lambda i, s: weights.low(dve, i, s), first_turn - 1, s, False)
            turn_loop(dve, weigh)
            for c in range(DC):
                dve.wait_ge(turned, c + 1)
                nc.vector.tensor_tensor(k.x2T[:, c, :], k.x2T[:, c, :], k.ps[:, c % 2, 0:SEQ], ALU.add).then_inc(added, 1)


def second_block(k, scope, sb):
    nc = k.nc
    k.hT = sb(scope, "h2T", 2, DC, SEQ, dtype=F32R)
    k.chunk = sb(scope, "chunk2", SPLIT, 2, SEQ, dtype=F32R)
    k.weight = k.chunk
    k.slot_i, k.slot_j, k.slot_gate = (sb(scope, f"slot_{n}", SEQ) for n in ("i", "j", "gate"))
    k.gelu, k.gated = sb(scope, "gelu", 2, SEQ), sb(scope, "gated", SEQ)
    hot = Carver(k.ring.rearrange("p s m -> p (s m)"))
    k.hot_i, k.hot_j = hot(16, NK), hot(16, NK)
    gates = sb(scope, "gates", SEQ * NK)
    k.early = gates[:, 0:EARLY * SEQ].rearrange("p (j t) -> p j t", j=EARLY)
    k.dense = gates[:, EARLY * SEQ:]

    mix = Carver(gates)
    k.const2_sb, k.small2_sb = mix(CONST2_W), mix(SMALL2_W)
    k.zT, k.natural2 = mix(ZC, SEQ), mix(TB, NATURAL2)
    k.y2T, k.squares = mix(DC, SEQ), mix(DC, SEQ)
    k.z, k.z_abs, k.keep, k.arg = (mix(SBH, 3 * P) for _ in range(4))
    k.gate_rows, k.rows, k.soft = mix(2, SEQ), mix(6, SEQ), mix(SEQ)
    stick = Carver(k.z.rearrange("p h w -> p (h w)"))
    k.m_carry, k.neg_last, k.columns = stick(1), stick(1), stick(3, MLH)
    k.qkconv = k.squares[:, 0:6, :]
    more = Carver(k.z_abs.rearrange("p h w -> p (h w)"))
    k.floor, k.q_carry, k.k_keep = more(MLH // 2, SEQ), more(MLH // 2, P), more(MLW)
    more = Carver(k.keep.rearrange("p h w -> p (h w)"))
    k.state, k.ahead, k.decay, k.ml_probs = more(MLH // 2 * P), more(2, SEQ), more(2, SEQ), more(2, SEQ)
    more = Carver(k.arg.rearrange("p h w -> p (h w)"))
    k.den, k.v_square, k.v_rstd = more(SEQ), more(TB * SGW), more(TB * SGG)

    choose = Carver(k.dense)
    k.queryT, k.keysT = choose(RAW, SEQ), choose(HC * NK)
    k.key_spare = choose(2, TB * NK)
    k.half_val, k.half_key = choose(TB * HC, TOPK), choose(TB * HC, TOPK)
    k.half_at = choose(TB * HC, TOPK).bitcast(U32)
    pairs = TB * PH
    k.pair_val, k.pair_at = choose(pairs, TOPK), choose(pairs, TOPK).bitcast(U32)
    k.place, k.place_int = choose(pairs * TOPK), choose(pairs * TOPK).bitcast(U32)
    k.key_i, k.key_j, k.gates, k.gate_sum = choose(TB * SLOTS), choose(TB * SLOTS), choose(TB * SLOTS), choose(pairs)
    k.cand, k.cand_spare = choose(pairs * TOPK * TOPK), choose(pairs * TOPK * TOPK)
    k.y_natural = Carver(k.dense)(TB, D)

    with nc.Fori(0, DEPTH) as l:
        load_stage(k, [(k.const2_sb, k.const2_dram), (k.small2_sb, tile(k.small2_dram, l))])
        norm_stage(k, SEQ, lambda c, s: k.small2("norm1")[:, c:c + 1], None, k.x2T)
        transposed_stage(k, k.w_transposed2, l * ZC, ZC, k.zT)
        natural2_stage(k, l)
        head_norm_stage(k, k.zT[:, 0:6, :], 6, lambda c: k.small2("qn_g" if c < ZK else "kn_g"))
        stick_breaking_stage(k)
        mlstm_prepare_stage(k)
        mlstm_stage(k)
        gating_stage(k)
        head_norm_stage(k, k.y2T, DC, lambda c: k.small2("out_g")[:, c:c + 1])
        output_gate_stage(k)
        residual_stage(k, SEQ, k.w_out2, l * DC, DC, k.y2T, None, k.x2T)
        norm_stage(k, SEQ, lambda c, s: k.small2("norm2")[:, c:c + 1], None, k.x2T)
        choose_stage(k, l)
        scatter_stage(k)
        experts_stage(k, l)


def layout2(x):
    x = {name[:-2]: a for name, a in x.items() if name.endswith("_2")}
    L = DEPTH
    cuts = np.cumsum([SBW, SBW, SBW, 2 * MLW, MLW, MLW, MLH, MLH, SGW])
    q, kk, v, mqk, mv, mo, mi, mf, su, sv = np.split(x["w_in"], cuts, axis=-1)
    w_if = np.zeros((L, D, P), np.float32)
    w_if[..., 0:MLH], w_if[..., GATE_ROWS:GATE_ROWS + MLH] = mi, mf
    pair = lambda g: np.tile(g, 2)[:, None]
    small2 = np.stack([packed(SMALL2, SMALL2_W, {
        "norm1": chunked(x["norm1_g"][l]), "norm2": chunked(x["norm2_g"][l]),
        "qn_g": pair(x["sb_qn_g"][l]), "kn_g": pair(x["sb_kn_g"][l]),
        "conv_w": chunked(x["ml_conv_w"][l]).transpose(1, 2, 0), "conv_b": chunked(x["ml_conv_b"][l]),
        "out_g": chunked(x["out_g"][l]), "if_b": np.stack([x["ml_i_b"][l], x["ml_f_b"][l]], -1),
        "vn_g": np.broadcast_to(x["sg_vn_g"][l], (P, SGW)), "sg_b": x["sg_b"][l].reshape(1, -1),
        "sg_w": x["sg_w"][l].transpose(2, 0, 1)}) for l in range(L)])
    pu = x["peer_u"].reshape(L, NK, NK, DC, P).transpose(0, 2, 4, 3, 1).reshape(L, NK, P, D)
    pv = x["peer_v"].reshape(L, NK, NK, D).transpose(0, 2, 1, 3)
    query = tiled(x["peer_wq"]).reshape(L, HC, P, D)
    uv = np.empty((L, EARLY + 2 * (NK - EARLY), P, D), np.float32)
    uv[:, :EARLY], late = pv[:, :EARLY], uv[:, EARLY:]
    late[:, 0], late[:, 1:-1:2], late[:, 2:-1:2], late[:, -1] = pu[:, EARLY], pu[:, EARLY + 1:], pv[:, EARLY:-1], pv[:, -1]
    return {
        "small2_dram": small2, "w_transposed2": tiled(np.concatenate([q, kk, mqk, mo, su, w_if], -1)),
        "w_natural2": np.concatenate([v, mv, sv], -1).reshape(L * DC, P, NATURAL2),
        "w_out2": x["w_out"].reshape(L * DC, P, D), "w_choose": np.concatenate([query, pu[:, :EARLY]], axis=1).reshape(-1, P, D),
        "peer_keys": x["peer_keys"].transpose(0, 4, 1, 2, 3).reshape(L, P, HC * NK),
        "peer_uv": uv.reshape(-1, P, D),
    }




class Kit:

    def __init__(self, nc):
        self.nc = nc

    def const(self, name):
        at, width = CONST[name]
        return self.const_sb[:, at:at + width]

    def const2(self, name):
        at, width = CONST2[name]
        return self.const2_sb[:, at:at + width]

    def const1(self, name):
        at, width = CONST1[name]
        return self.const1_sb[:, at:at + width]

    def small1(self, name):
        at, width = SMALL1[name]
        return self.small1_sb[:, at:at + width]

    def small2(self, name):
        at, width = SMALL2[name]
        return self.small2_sb[:, at:at + width]


class Carver:

    def __init__(self, whole):
        self.whole, self.at = whole, 0

    def __call__(self, *shape):
        width = int(np.prod(shape))
        cut = self.whole[:, self.at:self.at + width]
        self.at += width
        assert self.at <= self.whole.shape[1], self.at
        if len(shape) == 2:
            return cut.rearrange("p (a b) -> p a b", a=shape[0])
        if len(shape) == 3:
            return cut.rearrange("p (a b c) -> p a b c", a=shape[0], b=shape[1])
        return cut


def program(nc, dram, out):
    k = Kit(nc)
    tokens = SEQ + CTX
    k.x_in, k.cond_in, k.norm_final_in = dram["x_in"], dram["cond_in"], dram["norm_final_in"]
    k.const_dram, k.const1_dram, k.const2_dram = dram["const_dram"], dram["const1_dram"], dram["const2_dram"]
    k.small1_dram, k.small2_dram = dram["small1_dram"], dram["small2_dram"]
    k.w_mod, k.w_qk, k.w_natural = dram["w_mod"], dram["w_qk"], dram["w_natural"]
    k.w_merge, k.w_out, k.w_up, k.w_down = dram["w_merge"], dram["w_out"], dram["w_up"], dram["w_down"]
    k.w_transposed2, k.w_natural2 = dram["w_transposed2"], dram["w_natural2"]
    k.w_out2, k.w_choose = dram["w_out2"], dram["w_choose"]
    k.peer_keys, k.peer_uv = dram["peer_keys"], dram["peer_uv"]
    with ExitStack() as ctx:

        def sb(scope, name, *shape, dtype=F32):
            return scope.enter_context(nc.sbuf_tensor(name, [P, *shape], dtype))

        k.ps = ctx.enter_context(nc.psum_tensor("ps", [P, 8, 512], F32))
        k.const_sb = sb(ctx, "const_sb", CONST_W)
        k.rstd = sb(ctx, "rstd", tokens)
        k.x2T = sb(ctx, "x2T", DC, SEQ)
        k.ring = sb(ctx, "ring", RAW, D)
        k.split = sb(ctx, "split", SPLIT, 2, D, dtype=F32R)
        with ExitStack() as scope:
            k.const1_sb = sb(scope, "const1_sb", CONST1_W)
            k.small1_sb = sb(scope, "small1_sb", SMALL1_W)
            k.cond = sb(scope, "cond", DC * 2)
            k.cond_silu = sb(scope, "cond_silu", DC * 2)
            k.norm_final = sb(scope, "norm_final_sb", DC)
            k.mod = sb(scope, "mod", NMOD * DC, 2)
            k.xT = sb(scope, "xT", DC, tokens)
            k.hT = sb(scope, "hT", 2, DC, tokens, dtype=F32R)
            k.stat = sb(scope, "stat", 2, 4)
            first_block(k, sb)
        with ExitStack() as scope:
            second_block(k, scope, sb)
        with stage(nc, "stored") as (block, stored):

            @block.sync
            def _(sp):
                sp.dma_start(out, k.x2T[:, :, :]).then_inc(stored, 16)
                sp.wait_ge(stored, 16)


def packed(table, width, parts):
    out = np.zeros((P, width), np.float32)
    for name, part in parts.items():
        at, n = table[name]
        part = np.asarray(part, np.float32)
        part = part.reshape(part.shape[0], n)
        out[:part.shape[0], at:at + n] = part
    return out


def constants():
    i = np.arange(P)
    q, key = np.arange(SEQ)[None, :], np.arange(P)[:, None]
    before = np.concatenate([key < q, (key < np.arange(P)[None, :])], axis=1).astype(np.float32)
    causal = (i[:, None] <= i[None, :]).astype(np.float32)
    heads = np.zeros((P, MLH, P), np.float32)
    pairs = np.zeros((P, MLH // 2, P), np.float32)
    for h in range(MLH):
        heads[h, h] = 1
        pairs[h, h // 2, (h % 2) * HD:(h % 2 + 1) * HD] = 1
    return packed(CONST, CONST_W, {
        "ident": np.eye(P), "ones": np.ones((P, P)), "half_ones": np.kron(np.eye(2), np.ones((HD, HD))),
        "iota": np.broadcast_to(np.arange(NK), (P, NK))}), packed(CONST2, CONST2_W, {
        "suffix": i[:, None] >= i[None, :], "causal": causal,
        "before": before, "not_before": (1 - before) * MASKED, "ahead": np.tile((1 - causal) * -MASKED, (1, 2)),
        "row_of_head": heads, "row_of_pair": pairs})


def constants1():
    tokens = SEQ + CTX
    freq = (ROPE_BASE ** (-np.arange(HD // 4) / (HD // 4))).astype(np.float32)
    pos = np.arange(SEQ)
    angle = np.stack([np.float32(pos // GRID_W)[:, None] * freq, np.float32(pos % GRID_W)[:, None] * freq], 1)
    cos, sin = np.ones((2, 2, 2, HD // 4, tokens)), np.zeros((2, 2, 2, HD // 4, tokens))
    cos[..., :SEQ] = np.cos(angle).transpose(1, 2, 0)[None, :, None]
    sin[..., :SEQ] = np.sin(angle).transpose(1, 2, 0)[None, :, None]
    swap = np.zeros((P, P))
    for m in range(P):
        quarter = HD // 4
        if m // quarter % 2 == 0:
            swap[m + quarter, m] = -1
        else:
            swap[m - quarter, m] = 1
    window = np.zeros((P, TB, 2 * SEQ))
    for b in range(TB):
        rel = np.arange(SEQ)[None, :] - (b * P + np.arange(P))[:, None]
        window[:, b, :SEQ] = np.where(np.abs(rel) <= WINDOW, 0, MASKED)
    pool = np.zeros((SEQ, len(POOL_WINDOWS), SEQ))
    for g, w in enumerate(POOL_WINDOWS):
        for t in range(SEQ):
            lo, hi = max(t - w // 2, 0), min(t - w // 2 + w, SEQ)
            pool[lo:hi, g, t] += 1.0 / (hi - lo)
            pool[t, g, t] -= 1
    tt = 2 * np.pi * np.outer(np.arange(SEQ), np.arange(SEQ)) / SEQ
    cc = 2 * np.pi * np.outer(np.arange(HD), np.arange(HD)) / HD
    time = np.concatenate([np.cos(tt), np.sin(tt)], 1) / np.sqrt(SEQ)
    chan = np.concatenate([np.kron(np.eye(2), np.cos(cc)), -np.kron(np.eye(2), np.sin(cc))], 1) / np.sqrt(HD)

    def by_block(a):
        return a.reshape(TB, P, -1).transpose(1, 0, 2)

    return packed(CONST1, CONST1_W, {
        "rope_swap": swap, "rope_cos": cos.reshape(P, tokens), "rope_sin": sin.reshape(P, tokens), "window": window,
        "pool": by_block(pool), "dft_time": by_block(time), "dft_chan": chan})


def chunked(a):
    return np.moveaxis(a.reshape(*a.shape[:-1], -1, P), -2, -1)


def tiled(w):
    l, rows, cols = w.shape
    a = w.reshape(l, rows // P, P, cols // P, P).transpose(0, 3, 2, 1, 4)
    return np.ascontiguousarray(a).reshape(l * cols // P, P, rows)


def layout(x):
    x = {name: np.asarray(a) for name, a in x.items()}
    L = DEPTH
    w_in = x["w_in"]
    cuts = np.cumsum([KW, KW, QW, POOLW, FOURW])
    wk, wv, wq, wu, wf, wg = np.split(w_in, cuts, axis=-1)
    heads = np.array([[c, c + QC] for c in range(QC)]).ravel()
    wq = wq.reshape(L, D, QH, HD)[:, :, heads].reshape(L, D, QW)
    br_attn = x["w_br_attn"].reshape(L, QH, HD, D)[:, heads].reshape(L, QW, D)
    branches = np.concatenate([br_attn, x["w_br_pool"], x["w_br_four"]], axis=1)
    merge = np.stack([*(a.reshape(L, DC, P, D) for a in np.split(tiled(wg).reshape(L, 3 * DC, P, D), 3, axis=1)),
                      tiled(branches).reshape(L, DC, P, D)], axis=2)
    up = tiled(x["w_up"]).reshape(L, 2, FC, P, D).transpose(0, 2, 1, 3, 4)
    conv = chunked(x["conv_w"]).reshape(L, 3, P, 2, FC).transpose(0, 2, 1, 4, 3)
    twice = lambda a: np.repeat(chunked(a)[..., None], 2, axis=-1)
    small1 = np.stack([packed(SMALL1, SMALL1_W, {
        "b_mod": twice(x["b_mod"][l]), "norm_mix": twice(x["norm_mix"][l]), "norm_ffn": twice(x["norm_ffn"][l]),
        "sink": np.broadcast_to(x["attn_sink"][l], (P, QH)),
        "pool_w": x["pool_w"][l].reshape(2, 2 * HD, HD).transpose(1, 0, 2), "pool_scale": chunked(x["pool_scale"][l]),
        "conv_w": conv[l]}) for l in range(L)])
    const, const2 = constants()
    feed = {
        "x_in": np.concatenate([chunked(x["x"][0].T.reshape(D, SEQ).T).transpose(1, 2, 0),
                                chunked(x["ctx"][0]).transpose(1, 2, 0)], axis=-1),
        "cond_in": np.stack([chunked(x["c"][0]), chunked(x["c_ctx"])], axis=-1).reshape(P, DC * 2),
        "norm_final_in": chunked(x["norm_final"]),
        "const_dram": const, "const2_dram": const2, "const1_dram": constants1(), "small1_dram": small1,
        "w_mod": x["w_mod"].reshape(L, DC, P, NMOD, D).transpose(0, 3, 1, 2, 4).reshape(L * NMOD * DC, P, D),
        "w_qk": tiled(np.concatenate([wk, wq], -1)),
        "w_natural": np.concatenate([wv, wu, wf], -1).reshape(L * DC, P, NATURAL),
        "w_merge": merge.reshape(L * DC * 4, P, D), "w_out": x["w_out"].reshape(L * DC, P, D), "w_up": up.reshape(-1, P, D),
        "w_down": x["w_down"].reshape(L * FC, P, D),
    }
    feed.update(layout2(x))
    return {name: np.ascontiguousarray(a, np.float32) for name, a in feed.items()}


def kernel(**inputs):
    import concourse.bacc as bacc
    from concourse.bass_utils import run_bass_kernel_spmd

    feed = layout(inputs)
    nc = bacc.Bacc("TRN2", target_bir_lowering=False, num_devices=1)
    dram = {name: nc.dram_tensor(name, a.shape, F32, kind="ExternalInput").ap() for name, a in feed.items()}
    out = nc.dram_tensor("out", (P, DC, SEQ), F32, kind="ExternalOutput").ap()
    program(nc, dram, out)
    got = run_bass_kernel_spmd(nc, [feed], core_ids=[0]).results[0]["out"]
    return np.ascontiguousarray(np.asarray(got).transpose(2, 1, 0)).reshape(1, SEQ, D)
```

```python
from contextlib import ExitStack, contextmanager

import concourse.bass as bass
import numpy as np
from concourse import mybir

F32 = mybir.dt.float32
F32R = mybir.dt.float32r
U32 = mybir.dt.uint32
ALU = mybir.AluOpType
ACT = mybir.ActivationFunctionType
AX_X = mybir.AxisListType.X

P = 128
D = 1024
DC = D // P
DEPTH = 2
SEQ = 256
CTX = 256
TB = SEQ // P
EPS = 1e-6
MASKED = -1e30

HD = 64
QH, KVH = 8, 2
QW, KW = QH * HD, KVH * HD
WINDOW, GRID_W, ROPE_BASE = 128, 64, 10000.0
POOL_WINDOWS = (2, 4, 8, 16)
POOLW = len(POOL_WINDOWS) * HD
FOURW = 4 * HD
FF = 2816
FC = FF // P
NMOD = 6
NATURAL = KW + POOLW + FOURW
QC = QW // P

SBH, MLH, SGG = 6, 6, 4
SBW, MLW, SGW = SBH * HD, MLH * HD, SGG * HD
ML_CONV = 4
NATURAL2 = SBW + MLW + SGW
ZQ, ZK, ZMQ, ZMK, ZO, ZU, ZIF = 0, 3, 6, 9, 12, 15, 17
ZC = 18
GATE_ROWS = 32
YML, YSG = 3, 6
PH, NK, TOPK = 8, 128, 16
HC = 2 * PH
SLOTS = PH * TOPK
EARLY = 28

RAW, SPLIT = 4, 2
PASSES = ((0, 0), (0, 1), (1, 0))


def offsets(*parts):
    at, out = 0, {}
    for name, width in parts:
        out[name] = (at, width)
        at += width
    return out, at


CONST, CONST_W = offsets(("ident", P), ("ones", P), ("iota", NK))
CONST2, CONST2_W = offsets(
    ("suffix", P), ("causal", P), ("before", 3 * P), ("not_before", 3 * P), ("ahead", 2 * P), ("row_of_head", MLH * P),
    ("row_of_pair", DC * P), ("head_of_row", DC * 2 * DC))
CONST1, CONST1_W = offsets(
    ("rope_swap", P), ("rope_cos", SEQ + CTX), ("rope_sin", SEQ + CTX), ("window", TB * 2 * SEQ),
    ("pool", TB * len(POOL_WINDOWS) * SEQ), ("dft_time", TB * 2 * SEQ), ("dft_chan", 2 * P))
SMALL1, SMALL1_W = offsets(
    ("b_mod", NMOD * DC * 2), ("norm_mix", DC * 2), ("norm_ffn", DC * 2), ("sink", QH),
    ("pool_w", 2 * HD), ("pool_scale", 2), ("conv_w", 3 * 2 * FC))
SMALL2, SMALL2_W = offsets(
    ("norm1", DC), ("norm2", DC), ("qn_g", 1), ("kn_g", 1), ("conv_w", 6 * ML_CONV), ("conv_b", 6),
    ("out_g", DC), ("if_b", 2), ("vn_g", SGW), ("sg_b", SGG * P), ("sg_w", SGG * P))



@contextmanager
def stage(nc, *names, weights=None):
    sems, every = [], list(weights.loaded) if weights else []
    for name in names:
        sems.append(nc.alloc_semaphore(f"{name}_{nc.next_id()}"))
    with nc.Block(no_gpsimd_drain=True) as block:
        yield (block, *sems)
    nc.clear_and_free_semaphores(every + sems)
    nc.all_engine_barrier(sem_only=True)


class Steps:

    def __init__(self, eng, sem, done=0):
        self.eng, self.sem, self.done = eng, sem, done

    def step(self, ins):
        ins.then_inc(self.sem, 1)
        self.done = self.done + 1
        return ins

    def settle(self):
        self.eng.wait_ge(self.sem, self.done)

    def __call__(self, ins):
        self.step(ins)
        self.settle()


def tile(dram, n):
    return dram[bass.ds(n, 1)].rearrange("a p m -> p (a m)")


def one(ap, n):
    return ap[:, bass.ds(n, 1), :].rearrange("p a m -> p (a m)")


def turns(eng, n, body):
    with eng.Fori(0, n // RAW) as i:
        for s in range(RAW):
            body(i, s)
    for s in range(n % RAW):
        body(n // RAW, s)


def turns_ahead(eng, n, prepare, finish, first=False):
    full, rest = (n - SPLIT) // RAW, (n - SPLIT) % RAW

    def step(i, s):
        prepare(i + (s + SPLIT) // RAW, (s + SPLIT) % RAW)
        finish(i, s)

    def turn(i):
        for s in range(RAW):
            step(i, s)

    for s in range(SPLIT):
        prepare(0, s)
    if first:
        turn(0)
    if full > first:
        with eng.Fori(int(first), full) as i:
            turn(i)
    for s in range(rest):
        step(full, s)
    for t in range(n - SPLIT, n):
        finish(t // RAW, t % RAW)


def product(nc, out, lhsT, rhs, first, last):
    for n, (a, b) in enumerate(PASSES):
        ins = nc.tensor.matmul(out, lhsT(a), rhs(b), start=first and n == 0, stop=last and n == len(PASSES) - 1)
    return ins


WEIGHT_SEMS = ("high_ready", "low_ready", "halves_used")
HALF = DC // 2


class Weights:

    def __init__(self, k, dram, base, n, width=D):
        self.nc, self.ring, self.split = k.nc, k.ring, k.split
        self.dram, self.base, self.n, self.width = dram, base, n, width
        self.loaded = [k.nc.alloc_semaphore(f"loaded_{k.nc.next_id()}") for _ in range(RAW)]
        self.begun = False
        self.halves = [slice(0, width // 2), slice(width // 2, width)]

    def signals(self, high_ready, low_ready, halves_used):
        self.high_ready, self.low_ready, self.halves_used = high_ready, low_ready, halves_used

    def fetch(self, sp, i, s):
        sp.dma_start(self.ring[:, s, 0:self.width], tile(self.dram, self.base + i * RAW + s)).then_inc(self.loaded[s], 16)

    def begin(self, sp, before=None):
        for s in range(RAW):
            if before:
                last = (before.n - 1 - s) // RAW
                sp.wait_ge(before.low_ready, (last * RAW + s + 1) * 2)
            self.fetch(sp, 0, s)
        self.begun = True

    def load(self, sp, ahead=None):
        def refill(i, s):
            sp.wait_ge(self.low_ready, ((i - 1) * RAW + s + 1) * 2)
            self.fetch(sp, i, s)

        if not self.begun:
            self.begin(sp)
        if self.n // RAW > 1:
            with sp.Fori(1, self.n // RAW) as i:
                for s in range(RAW):
                    refill(i, s)
        for s in range(self.n % RAW):
            refill(self.n // RAW, s)
        if ahead:
            ahead.begin(sp, self)

    def high(self, act, i, s):
        act.wait_ge(self.loaded[s], i * 16 + 16)
        for half, cols in enumerate(self.halves):
            act.wait_ge(self.halves_used, (i * RAW + s) * 2 + half + 1)
            self.nc.scalar.activation(self.split[:, s % SPLIT, 0, cols], self.ring[:, s, cols],
                                      ACT.Copy).then_inc(self.high_ready, 1)

    def low(self, eng, i, s, ops=None):
        for half, cols in enumerate(self.halves):
            eng.wait_ge(self.high_ready, (i * RAW + s) * 2 + half + 1)
            (ops or self.nc.vector).tensor_tensor(
                self.split[:, s % SPLIT, 1, cols], self.ring[:, s, cols], self.split[:, s % SPLIT, 0, cols].bitcast(F32),
                ALU.subtract).then_inc(self.low_ready, 1)

    def slots_free(self, pe):
        pe.sem_inc(self.halves_used, 2 * SPLIT)

    def used(self, i, s):
        return (i * RAW + s + 1 + SPLIT) * 2

    def part(self, s, first, width):
        return lambda p: self.split[:, s % SPLIT, p, first:first + width]

    def ready(self, pe, i, s, half):
        pe.wait_ge(self.low_ready, (i * RAW + s) * 2 + half + 1)

    def contract(self, pe, i, s, out, rhs, sums=((0, DC),)):
        for n, (first, end) in enumerate(sums):
            dst = out(n)
            for c in range(first, end):
                if c % HALF == 0:
                    self.ready(pe, i, s, c // HALF)
                last = product(self.nc, dst, self.part(s, c * P, P), rhs(c), c == first, c == end - 1)
                if c % HALF == HALF - 1:
                    last.then_inc(self.halves_used, 1)




def norm_stage(k, tokens, gain, shift, xT, out=None, loads=(), ahead=None):
    nc, streams = k.nc, tokens // SEQ
    pieces = [(c, s) for c in range(DC) for s in range(streams)]
    blocks = tokens // P
    total, root, rstd = k.ps[:, 2:2 + blocks, 0], k.rstd[:, 0:blocks], k.ps[:, 1, 0:tokens]
    work = k.norm_work
    cols = [slice(s * SEQ, (s + 1) * SEQ) for s in range(streams)]
    with stage(nc, "squared", "added", "summed", "var_ready", "rooted", "spread", "scaled", "shifted", "high_ready",
               "low_ready", "loads_in") as (
            block, squared, added, summed, var_ready, rooted, spread, scaled, shifted, high_ready, low_ready, loads_in):

        @block.sync
        def _(sp):
            for dst, src in loads:
                sp.dma_start(dst, src).then_inc(loads_in, 16)
            if ahead:
                ahead.begin(sp)
            if loads:
                sp.wait_ge(loads_in, 16 * len(loads))

        @block.scalar
        def _(act):
            for c in range(DC):
                nc.scalar.activation(work[:, c, 0:tokens], xT[:, c, 0:tokens], ACT.Square).then_inc(squared, 1)
            act.wait_ge(var_ready, 1)
            nc.scalar.activation(root, root, ACT.Sqrt).then_inc(rooted, 1)
            if out is None:
                for n, (c, s) in enumerate(pieces):
                    act.wait_ge(scaled, n + 1)
                    h = work[:, c, cols[s]]
                    if shift is not None and n % 2:
                        nc.scalar.activation(h, h, ACT.Identity, bias=shift(c, s)).then_inc(shifted, 1)
                        act.wait_ge(shifted, n // 2 + 1)
                    if shift is None or n % 2:
                        nc.scalar.activation(k.hT[:, 0, c, cols[s]], h, ACT.Copy).then_inc(high_ready, 1)
                    else:
                        nc.scalar.activation(k.hT[:, 0, c, cols[s]], work[:, c, cols[s]], ACT.Identity,
                                             bias=shift(c, s)).then_inc(high_ready, 1)

        @block.gpsimd
        def _(pool):
            if out is None:
                for n, (c, s) in enumerate(pieces):
                    if n % 2:
                        pool.wait_ge(high_ready, n + 1)
                        nc.gpsimd.tensor_tensor(k.hT[:, 1, c, cols[s]], work[:, c, cols[s]], k.hT[:, 0, c, cols[s]].bitcast(F32),
                                                ALU.subtract).then_inc(low_ready, 1)

        @block.tensor
        def _(pe):
            pe.wait_ge(added, DC - 1)
            for n in range(blocks):
                last = nc.tensor.matmul(k.ps[:, 2 + n, 0:1], work[:, 0, n * P:(n + 1) * P], k.const("ones")[:, 0:1],
                                        start=True, stop=True)
            last.then_inc(summed, 1)
            pe.wait_ge(var_ready, 2)
            for n in range(blocks):
                last = nc.tensor.matmul(rstd[:, n * P:(n + 1) * P], root[:, n:n + 1].broadcast_to([P, P]), k.const("ident"),
                                        start=True, stop=True)
            last.then_inc(spread, 1)

        @block.vector
        def _(dve):
            for c in range(1, DC):
                dve.wait_ge(squared, c + 1)
                if c >= 2:
                    dve.wait_ge(added, c - 1)
                nc.vector.tensor_tensor(work[:, 0, 0:tokens], work[:, 0, 0:tokens], work[:, c, 0:tokens], ALU.add).then_inc(added, 1)
            dve.wait_ge(summed, 1)
            nc.vector.tensor_scalar(root, total, 1.0 / D, EPS, ALU.mult, ALU.add).then_inc(var_ready, 1)
            dve.wait_ge(rooted, 1)
            nc.vector.reciprocal(root, root).then_inc(var_ready, 1)
            dve.wait_ge(spread, 1)
            if loads:
                dve.wait_ge(loads_in, 16 * len(loads))
            for c, s in pieces:
                dst = work[:, c, cols[s]] if out is None else out[:, c, cols[s]]
                nc.vector.scalar_tensor_tensor(dst, xT[:, c, cols[s]], gain(c, s), rstd[:, cols[s]],
                                               ALU.mult, ALU.mult).then_inc(scaled, 1)
            if out is None:
                for n, (c, s) in enumerate(pieces):
                    if n % 2:
                        continue
                    h, high, low = work[:, c, cols[s]], k.hT[:, 0, c, cols[s]].bitcast(F32), k.hT[:, 1, c, cols[s]]
                    dve.wait_ge(high_ready, n + 1)
                    if shift is None:
                        nc.vector.tensor_tensor(low, h, high, ALU.subtract).then_inc(low_ready, 1)
                    else:
                        nc.vector.scalar_tensor_tensor(low, h, shift(c, s), high, ALU.add, ALU.subtract).then_inc(low_ready, 1)


def residual_stage(k, tokens, weights, chunks, src, gate, xT, ahead=None):
    nc, streams = k.nc, tokens // SEQ
    with stage(nc, *WEIGHT_SEMS, "chunk_high", "chunk_low", "summed", "added", weights=weights) as (
            block, high_ready, low_ready, halves_used, chunk_high, chunk_low, summed, added):
        weights.signals(high_ready, low_ready, halves_used)

        @block.sync
        def _(sp):
            weights.load(sp, ahead)

        @block.scalar
        def _(act):
            def split(i, s):
                weights.high(act, i, s)
                act.wait_ge(halves_used, (i * RAW + s + 1) * 2)
                nc.scalar.activation(k.chunk[:, s % SPLIT, 0, 0:tokens], one(src, i * RAW + s)[:, 0:tokens],
                                     ACT.Copy).then_inc(chunk_high, 1)

            turns(act, chunks, split)

        @block.vector
        def _(dve):
            def split(i, s):
                weights.low(dve, i, s)
                dve.wait_ge(chunk_high, i * RAW + s + 1)
                nc.vector.tensor_tensor(k.chunk[:, s % SPLIT, 1, 0:tokens], one(src, i * RAW + s)[:, 0:tokens],
                                        k.chunk[:, s % SPLIT, 0, 0:tokens].bitcast(F32), ALU.subtract).then_inc(chunk_low, 1)

            turns(dve, chunks, split)
            for n in range(DC):
                dve.wait_ge(summed, n + 1)
                for s in range(streams):
                    x, add = xT[:, n, s * SEQ:(s + 1) * SEQ], k.ps[:, n, s * SEQ:(s + 1) * SEQ]
                    if gate is None:
                        nc.vector.tensor_tensor(x, x, add, ALU.add).then_inc(added, 1)
                    else:
                        nc.vector.scalar_tensor_tensor(x, add, gate(n, s), x, ALU.mult, ALU.add).then_inc(added, 1)

        @block.tensor
        def _(pe):
            def add_tile(i, s, first=False, last=False):
                pe.wait_ge(chunk_low, i * RAW + s + 1)
                for n in range(DC):
                    if n % HALF == 0:
                        weights.ready(pe, i, s, n // HALF)
                    ins = product(nc, k.ps[:, n, 0:tokens], weights.part(s, n * P, P),
                                  lambda p: k.chunk[:, s % SPLIT, p, 0:tokens], first, last)
                    if last:
                        ins.then_inc(summed, 1)
                    elif n % HALF == HALF - 1:
                        ins.then_inc(halves_used, 1)

            weights.slots_free(pe)
            full = (chunks - 1) // RAW
            for s in range(RAW):
                add_tile(0, s, first=s == 0)
            if full > 1:
                with pe.Fori(1, full) as i:
                    for s in range(RAW):
                        add_tile(i, s)
            for t in range(full * RAW, chunks):
                add_tile(t // RAW, t % RAW, last=t == chunks - 1)




def mod_stage(k, weights, needed, others, ahead):
    nc, tiles, rows = k.nc, NMOD * DC, 4
    sums = k.ps[:, 4, 0:rows * tiles].rearrange("p (n r) -> p n r", r=rows)
    cond = k.cond_silu[:, :].rearrange("p (c s) -> p c s", s=2)
    at = lambda t: (t // RAW, t % RAW)
    with stage(nc, *WEIGHT_SEMS, "needed_in", "others_in", "silu_done", "cleared", "cond_high", "cond_low", "rows_kept",
               "turned", "mod_done", weights=weights) as (
            block, high_ready, low_ready, halves_used, needed_in, others_in, silu_done, cleared, cond_high, cond_low,
            rows_kept, turned, mod_done):
        weights.signals(high_ready, low_ready, halves_used)

        @block.sync
        def _(sp):
            weights.load(sp, ahead)

        @block.scalar
        def _(act):
            for out, src in needed:
                act.dma_start(out, src).then_inc(needed_in, 16)
            act.wait_ge(needed_in, 16 * len(needed))
            nc.scalar.activation(k.cond_silu[:, :], k.cond[:, :], ACT.Silu).then_inc(silu_done, 1)
            act.wait_ge(silu_done, 1)
            act.wait_ge(cleared, 1)
            nc.scalar.activation(k.cond_split[:, :, 0:2], cond, ACT.Copy).then_inc(cond_high, 1)
            for out, src in others:
                act.dma_start(out, src).then_inc(others_in, 16)
            turns(act, tiles, lambda i, s: weights.high(act, i, s))
            if others:
                act.wait_ge(others_in, 16 * len(others))

        @block.tensor
        def _(pe):
            def turn(g):
                pe.wait_ge(rows_kept, 2 * g + 2)
                for n in range(DC):
                    last = nc.tensor.transpose(sums[:, g * DC + n, :], k.mod_rows[0:rows, g % 2, n * P:(n + 1) * P],
                                               k.const("ident")[0:rows, 0:rows])
                last.then_inc(turned, 1)

            weights.slots_free(pe)
            pe.wait_ge(needed_in, 16 * len(needed))
            pe.wait_ge(cond_low, 1)
            for g in range(NMOD):
                if g >= 2:
                    pe.wait_ge(rows_kept, 2 * (g - 2) + 2)
                for c in range(DC):
                    i, s = at(g * DC + c)
                    for half in range(2):
                        weights.ready(pe, i, s, half)
                        for p in range(2):
                            last = nc.tensor.matmul(k.ps[:, g % 2 * 2 + half, :], k.cond_split[:, c, :],
                                                    weights.part(s, half * 512, 512)(p),
                                                    start=c == 0 and p == 0, stop=c == DC - 1 and p == 1)
                        last.then_inc(halves_used, 1)
                if g >= 1:
                    turn(g - 1)
            turn(NMOD - 1)

        @block.vector
        def _(dve):
            def keep_rows(g):
                dve.wait_ge(halves_used, weights.used(*at((g + 1) * DC - 1)))
                if g >= 2:
                    dve.wait_ge(turned, g - 1)
                for half in range(2):
                    nc.vector.tensor_copy(k.mod_rows[0:rows, g % 2, half * 512:(half + 1) * 512],
                                          k.ps[0:rows, g % 2 * 2 + half, :]).then_inc(rows_kept, 1)

            nc.vector.memset(k.cond_split[:, :, :].bitcast(U32), 0).then_inc(cleared, 1)
            dve.wait_ge(cond_high, 1)
            nc.vector.tensor_tensor(k.cond_split[:, :, 2:4], cond, k.cond_split[:, :, 0:2].bitcast(F32),
                                    ALU.subtract).then_inc(cond_low, 1)
            for t in range(tiles + SPLIT):
                if t < tiles:
                    weights.low(dve, *at(t))
                if t >= SPLIT and (t - SPLIT) % DC == DC - 1:
                    keep_rows((t - SPLIT) // DC)
            done = Steps(dve, mod_done)
            dve.wait_ge(turned, NMOD)
            dve.wait_ge(needed_in, 16 * len(needed))
            mod = k.mod.rearrange("p n c -> p (n c)")
            done(nc.vector.tensor_tensor(k.mod[:, :, :], sums[:, :, 0:2], k.small1("b_mod").rearrange("p (n c) -> p n c", c=2),
                                         ALU.add))
            done(nc.vector.tensor_tensor(k.mod[:, :, :], sums[:, :, 2:4], k.mod[:, :, :], ALU.add))
            for norm, scale in (("norm_mix", 1), ("norm_ffn", 4)):
                sc = mod[:, scale * DC * 2:(scale + 1) * DC * 2]
                done(nc.vector.scalar_tensor_tensor(sc, sc, 1.0, k.small1(norm), ALU.add, ALU.mult))


def qk_stage(k, weights, q_tokens, ahead):
    nc, n = k.nc, 1 + QC
    tokens = [SEQ + CTX] + [q_tokens] * QC
    raw, rot = k.ps[:, 0:2, :], k.ps[:, 2:4, :]
    at = lambda t: (t // RAW, t % RAW)
    with stage(nc, *WEIGHT_SEMS, "copied", "swapped", "rotated", "split_high", "split_low", weights=weights) as (
            block, high_ready, low_ready, halves_used, copied, swapped, rotated, split_high, split_low):
        weights.signals(high_ready, low_ready, halves_used)

        @block.sync
        def _(sp):
            weights.load(sp, ahead)

        @block.tensor
        def _(pe):
            def swap(j):
                pe.wait_ge(copied, j + 1)
                if j >= 2:
                    pe.wait_ge(rotated, 3 * (j - 2) + 2)
                nc.tensor.matmul(rot[:, j % 2, 0:tokens[j]], k.const1("rope_swap"), k.qkT[:, j, 0:tokens[j]],
                                 start=True, stop=True).then_inc(swapped, 1)

            weights.slots_free(pe)
            for j in range(n):
                if j >= 2:
                    pe.wait_ge(copied, j - 1)
                weights.contract(pe, *at(j), lambda n: raw[:, j % 2, 0:tokens[j]],
                                 lambda c: lambda p: k.hT[:, p, c, 0:tokens[j]])
                if j >= 1:
                    swap(j - 1)
            swap(n - 1)

        @block.scalar
        def _(act):
            def keep_high(j):
                act.wait_ge(rotated, 3 * j + 3)
                nc.scalar.activation(k.qk_split[:, 0, j, 0:tokens[j]], k.qkT[:, j, 0:tokens[j]], ACT.Copy).then_inc(split_high, 1)

            for j in range(-SPLIT, n):
                if j + SPLIT < n:
                    weights.high(act, *at(j + SPLIT))
                if j >= 0:
                    act.wait_ge(halves_used, weights.used(*at(j)))
                    nc.scalar.activation(k.qkT[:, j, 0:tokens[j]], raw[:, j % 2, 0:tokens[j]], ACT.Copy).then_inc(copied, 1)
                if j >= 1:
                    keep_high(j - 1)
            keep_high(n - 1)

        @block.vector
        def _(dve):
            def keep_low(j):
                t = slice(0, tokens[j])
                dve.wait_ge(split_high, j + 1)
                nc.vector.tensor_tensor(k.qk_split[:, 1, j, t], k.qkT[:, j, t], k.qk_split[:, 0, j, t].bitcast(F32),
                                        ALU.subtract).then_inc(split_low, 1)

            done = Steps(dve, rotated)
            for j in range(-SPLIT, n):
                if j + SPLIT < n:
                    weights.low(dve, *at(j + SPLIT))
                if j < 0:
                    continue
                t = slice(0, tokens[j])
                dve.wait_ge(swapped, j + 1)
                done(nc.vector.tensor_tensor(k.qkT[:, j, t], k.qkT[:, j, t], k.const1("rope_cos")[:, t], ALU.mult))
                done(nc.vector.tensor_tensor(k.rstd[:, t], rot[:, j % 2, t], k.const1("rope_sin")[:, t], ALU.mult))
                done(nc.vector.tensor_tensor(k.qkT[:, j, t], k.qkT[:, j, t], k.rstd[:, t], ALU.add))
                if j >= 1:
                    keep_low(j - 1)
            keep_low(n - 1)


def natural_stage(k, weights, q_tokens, ahead):
    nc, half = k.nc, NATURAL // 2
    full = q_tokens // P
    blocks = (SEQ + CTX) // P
    parts = [(b, h, half if b < full else KW) for h in range(2) for b in range(full if h else blocks)]
    first_of = (0, blocks)
    with stage(nc, *WEIGHT_SEMS, "summed", "copied", weights=weights) as (
            block, high_ready, low_ready, halves_used, summed, copied):
        weights.signals(high_ready, low_ready, halves_used)

        @block.sync
        def _(sp):
            weights.load(sp, ahead)

        @block.tensor
        def _(pe):
            weights.slots_free(pe)
            for c in range(DC):
                for n, (b, h, cols) in enumerate(parts):
                    if n in (0, first_of[1]):
                        weights.ready(pe, c // RAW, c % RAW, h)
                    last = product(nc, k.ps[:, 2 * b + h, 0:cols], lambda p: k.hT[:, p, c, b * P:(b + 1) * P],
                                   weights.part(c % RAW, h * half, cols), c == 0, c == DC - 1)
                    if c == DC - 1:
                        last.then_inc(summed, 1)
                    elif n + 1 in (first_of[1], len(parts)):
                        last.then_inc(halves_used, 1)

        @block.scalar
        def _(act):
            turns(act, DC, lambda i, s: weights.high(act, i, s))
            for n, (b, h, cols) in enumerate(parts):
                if n % 2 == 0:
                    act.wait_ge(summed, n + 1)
                    nc.scalar.activation(k.natural[:, b, h * half:h * half + cols], k.ps[:, 2 * b + h, 0:cols],
                                         ACT.Copy).then_inc(copied, 1)

        @block.vector
        def _(dve):
            turns(dve, DC, lambda i, s: weights.low(dve, i, s))
            for n, (b, h, cols) in enumerate(parts):
                if n % 2 == 1:
                    dve.wait_ge(summed, n + 1)
                    nc.vector.tensor_copy(k.natural[:, b, h * half:h * half + cols], k.ps[:, 2 * b + h, 0:cols]).then_inc(copied, 1)


def attention_stage(k, q_tokens):
    nc, keys = k.nc, SEQ + CTX
    units = [(b, h) for b in range(q_tokens // P) for h in range(QH)]
    scale = float(HD) ** -0.5

    def first_key(b):
        return 0 if b < TB else SEQ

    with stage(nc, "scored", "masked", "max_ready", "exp_ready", "norm_step", "probs_ready", "turned",
               "probs_turned", "weighed", "kept_high", "kept") as (
            block, scored, masked, max_ready, exp_ready, norm_step, probs_ready, turned, probs_turned, weighed,
            kept_high, kept):

        def output(u):
            b, h = units[u]
            base = HD * (h // QC)
            return k.ps[base:base + HD, 4 + u % 4, 0:P], slice(base, base + HD), h % QC, slice(b * P, (b + 1) * P)

        @block.tensor
        def _(pe):
            def score(u):
                b, h = units[u]
                base = HD * (h // QC)
                if u >= 2:
                    pe.wait_ge(masked, u - 1)
                product(nc, k.ps[:, u % 2, first_key(b):keys],
                        lambda p: k.qk_split[base:base + HD, p, 1 + h % QC, b * P:(b + 1) * P],
                        lambda p: k.qk_split[base:base + HD, p, 0, first_key(b):keys], True, True).then_inc(scored, 1)

            def turn(u):
                b, _ = units[u]
                pe.wait_ge(probs_ready, u + 1)
                if u >= 2:
                    pe.wait_ge(probs_turned, u - 1)
                for j in range(first_key(b) // P, keys // P):
                    last = nc.tensor.transpose(k.ps[:, 2 + u % 2, j * P:(j + 1) * P],
                                               k.probs[:, u % 2, j * P:(j + 1) * P], k.const("ident"))
                last.then_inc(turned, 1)

            def weigh(u):
                b, _ = units[u]
                out, rows, _, _ = output(u)
                pe.wait_ge(probs_turned, u + 1)
                if u >= 4:
                    pe.wait_ge(kept, u - 3)
                first = first_key(b) // P
                for j in range(first, keys // P):
                    last = nc.tensor.matmul(out, k.natural[:, j, rows],
                                            k.probsT[:, u % 2, j * P:(j + 1) * P], start=j == first, stop=j == keys // P - 1)
                last.then_inc(weighed, 1)

            score(0)
            score(1)
            for u in range(len(units)):
                if u + 2 < len(units):
                    score(u + 2)
                turn(u)
                if u >= 1:
                    weigh(u - 1)
            weigh(len(units) - 1)

        @block.vector
        def _(dve):
            def mask_scores(u):
                b, h = units[u]
                cols = slice(first_key(b), keys)
                s = k.scores[:, u % 2, cols]
                dve.wait_ge(scored, u + 1)
                if u >= 2:
                    dve.wait_ge(exp_ready, 2 * (u - 1))
                nc.vector.scalar_tensor_tensor(s, k.ps[:, u % 2, cols], scale,
                                               k.const1("window")[:, (b % TB) * 2 * SEQ:(b % TB + 1) * 2 * SEQ][:, cols],
                                               ALU.mult, ALU.add).then_inc(masked, 1)
                dve.wait_ge(masked, u + 1)
                nc.vector.reduce_max(k.stat[:, u % 2, 0:1], s, AX_X).then_inc(max_ready, 1)

            def shift(u):
                m = k.stat[:, u % 2, 0:1]
                dve.wait_ge(max_ready, 2 * u + 1)
                nc.vector.tensor_scalar(m, m, k.small1("sink")[:, units[u][1]:units[u][1] + 1], -1.0,
                                        ALU.max, ALU.mult).then_inc(max_ready, 1)

            def sum_up(u):
                dve.wait_ge(exp_ready, 2 * u + 2)
                nc.vector.tensor_tensor(k.stat[:, u % 2, 3:4], k.stat[:, u % 2, 1:2], k.stat[:, u % 2, 2:3],
                                        ALU.add).then_inc(norm_step, 1)

            def invert(u):
                den = k.stat[:, u % 2, 3:4]
                dve.wait_ge(norm_step, 2 * u + 1)
                nc.vector.reciprocal(den, den).then_inc(norm_step, 1)

            def normalise(u):
                cols = slice(first_key(units[u][0]), keys)
                dve.wait_ge(norm_step, 2 * u + 2)
                if u >= 2:
                    dve.wait_ge(turned, u - 1)
                nc.vector.tensor_scalar(k.probs[:, u % 2, cols], k.exps[:, u % 2, cols], k.stat[:, u % 2, 3:4], None,
                                        ALU.mult).then_inc(probs_ready, 1)

            def keep(u):
                summed, rows, c, cols = output(u)
                dve.wait_ge(kept_high, u + 1)
                nc.vector.tensor_tensor(k.branchT[rows, 1, c, cols], summed, k.branchT[rows, 0, c, cols].bitcast(F32),
                                        ALU.subtract).then_inc(kept, 1)

            mask_scores(0)
            shift(0)
            for u in range(len(units)):
                more = u + 1 < len(units)
                if more:
                    mask_scores(u + 1)
                sum_up(u)
                if more:
                    shift(u + 1)
                invert(u)
                if u >= 3:
                    keep(u - 3)
                normalise(u)
            for u in range(len(units) - 3, len(units)):
                keep(u)

        @block.scalar
        def _(act):
            def exponents(u):
                b, h = units[u]
                cols = slice(first_key(b), keys)
                neg_max = k.stat[:, u % 2, 0:1]
                act.wait_ge(max_ready, 2 * u + 2)
                if u >= 2:
                    act.wait_ge(probs_ready, u - 1)
                nc.scalar.activation(k.exps[:, u % 2, cols], k.scores[:, u % 2, cols], ACT.Exp, bias=neg_max,
                                     accum_out=k.stat[:, u % 2, 1:2]).then_inc(exp_ready, 1)
                nc.scalar.activation(k.stat[:, u % 2, 2:3], k.small1("sink")[:, h:h + 1], ACT.Exp,
                                     bias=neg_max).then_inc(exp_ready, 1)

            def copy_turned(u):
                b, _ = units[u]
                cols = slice(first_key(b), keys)
                act.wait_ge(turned, u + 1)
                if u >= 2:
                    act.wait_ge(weighed, u - 1)
                nc.scalar.activation(k.probsT[:, u % 2, cols], k.ps[:, 2 + u % 2, cols], ACT.Copy).then_inc(probs_turned, 1)

            def keep_high(u):
                summed, rows, c, cols = output(u)
                act.wait_ge(weighed, u + 1)
                nc.scalar.activation(k.branchT[rows, 0, c, cols], summed, ACT.Copy).then_inc(kept_high, 1)

            exponents(0)
            for u in range(len(units)):
                if u + 1 < len(units):
                    exponents(u + 1)
                copy_turned(u)
                if u >= 2:
                    keep_high(u - 2)
            for u in range(len(units) - 2, len(units)):
                keep_high(u)


def pool_fourier_stage(k, q_tokens):
    nc, groups = k.nc, len(POOL_WINDOWS)
    pool = k.const1("pool").rearrange("p (b g t) -> p b g t", b=TB, g=groups)
    dft = k.const1("dft_time").rearrange("p (b t) -> p b t", b=TB)
    pool_w = k.small1("pool_w").rearrange("p (a d) -> p a d", a=2)
    streams = range(q_tokens // SEQ)
    n = 2 * len(streams)
    with stage(nc, "pooled", "pool_kept", "pool_mixed", "pool_high", "pool_scaled", "timed", "time_kept", "channeled",
               "four_high", "four_kept") as (
            block, pooled, pool_kept, pool_mixed, pool_high, pool_scaled, timed, time_kept, channeled,
            four_high, four_kept):

        @block.tensor
        def _(pe):
            for u in range(n):
                s, a = u // 2, u % 2
                if u >= 2:
                    pe.wait_ge(pool_kept, u - 1)
                for half in range(2):
                    g = 2 * a + half
                    for b in range(TB):
                        last = nc.tensor.matmul(k.ps[HD * half:HD * (half + 1), a, 0:SEQ],
                                                k.natural[:, s * TB + b, KW + g * HD:KW + (g + 1) * HD],
                                                pool[:, b, g, :], start=b == 0, stop=b == TB - 1)
                last.then_inc(pooled, 1)
                if u >= 2:
                    pe.wait_ge(time_kept, u - 1)
                for b in range(TB):
                    last = nc.tensor.matmul(k.ps[:, 2 + a, :], k.natural[:, s * TB + b, KW + POOLW + a * P:KW + POOLW + (a + 1) * P],
                                            dft[:, b, :], start=b == 0, stop=b == TB - 1)
                last.then_inc(timed, 1)
            for u in range(n):
                a = u % 2
                pe.wait_ge(pool_kept, u + 1)
                if u >= 2:
                    pe.wait_ge(pool_scaled, u - 1)
                for half in range(2):
                    rows = slice(HD * half, HD * (half + 1))
                    last = nc.tensor.matmul(k.ps[rows, 4 + a, 0:SEQ], pool_w[rows, a, :], k.pooledT[rows, u, :],
                                            start=True, stop=True)
                last.then_inc(pool_mixed, 1)
                pe.wait_ge(time_kept, u + 1)
                if u >= 2:
                    pe.wait_ge(four_kept, u - 1)
                for part in range(2):
                    last = nc.tensor.matmul(k.ps[:, 6 + a, 0:SEQ], k.const1("dft_chan")[:, part * P:(part + 1) * P],
                                            k.timedT[:, u, part * SEQ:(part + 1) * SEQ], start=part == 0, stop=part == 1)
                last.then_inc(channeled, 1)

        @block.vector
        def _(dve):
            for u in range(n):
                dve.wait_ge(pooled, u + 1)
                nc.vector.tensor_copy(k.pooledT[:, u, :], k.ps[:, u % 2, 0:SEQ]).then_inc(pool_kept, 1)
            for u in range(n):
                s, a = u // 2, u % 2
                dve.wait_ge(pool_mixed, u + 1)
                high, low = (k.branchT[:, p, QC + a, s * SEQ:(s + 1) * SEQ] for p in range(2))
                scale = k.small1("pool_scale")[:, a:a + 1]
                nc.vector.tensor_scalar(high, k.ps[:, 4 + a, 0:SEQ], scale, None, ALU.mult).then_inc(pool_high, 1)
                dve.wait_ge(pool_high, u + 1)
                nc.vector.scalar_tensor_tensor(low, k.ps[:, 4 + a, 0:SEQ], scale, high.bitcast(F32),
                                               ALU.mult, ALU.subtract).then_inc(pool_scaled, 1)
                high, low = (k.branchT[:, p, QC + 2 + a, s * SEQ:(s + 1) * SEQ] for p in range(2))
                dve.wait_ge(four_high, u + 1)
                nc.vector.tensor_tensor(low, k.ps[:, 6 + a, 0:SEQ], high.bitcast(F32), ALU.subtract).then_inc(four_kept, 1)

        @block.scalar
        def _(act):
            for u in range(n):
                act.wait_ge(timed, u + 1)
                nc.scalar.activation(k.timedT[:, u, :], k.ps[:, 2 + u % 2, :], ACT.Copy).then_inc(time_kept, 1)
            for u in range(n):
                s, a = u // 2, u % 2
                act.wait_ge(channeled, u + 1)
                nc.scalar.activation(k.branchT[:, 0, QC + 2 + a, s * SEQ:(s + 1) * SEQ], k.ps[:, 6 + a, 0:SEQ],
                                     ACT.Copy).then_inc(four_high, 1)


def merge_stage(k, weights, tokens, ahead):
    nc = k.nc
    gates, parts = 3, ((0, QC), (QC, QC + 2), (QC + 2, DC))
    t = slice(0, tokens)
    n_tiles = (gates + 1) * DC
    with stage(nc, *WEIGHT_SEMS, "gate_ready", "products", "merged", weights=weights) as (
            block, high_ready, low_ready, halves_used, gate_ready, products, merged):
        weights.signals(high_ready, low_ready, halves_used)

        @block.sync
        def _(sp):
            weights.load(sp, ahead)

        @block.tensor
        def _(pe):
            def use(n, s):
                def branch(g):
                    pe.wait_ge(products, n * gates + g + 1)
                    return k.ps[:, gates + g, t]

                if s < gates:
                    pe.wait_ge(gate_ready, n * gates + s + 1)
                    weights.contract(pe, n, s, lambda n: k.ps[:, s, t], lambda c: lambda p: k.hT[:, p, c, t])
                else:
                    weights.contract(pe, n, s, branch, lambda c: lambda p: k.branchT[:, p, c, t], parts)

            weights.slots_free(pe)
            turns(pe, n_tiles, use)

        @block.scalar
        def _(act):
            def keep_gate(n, s):
                if s < gates:
                    act.wait_ge(halves_used, weights.used(n, s))
                    act.wait_ge(products, n * gates + s + 1)
                    nc.scalar.activation(k.gate[:, s, t], k.ps[:, s, t], ACT.Sigmoid).then_inc(gate_ready, 1)

            act.sem_inc(gate_ready, gates)
            turns_ahead(act, n_tiles, lambda i, s: weights.high(act, i, s), keep_gate)

        @block.vector
        def _(dve):
            def merge(n, s):
                if s < gates:
                    return
                y = one(k.yT, n)[:, t]
                dve.wait_ge(halves_used, weights.used(n, s))
                for g in range(gates):
                    dve.wait_ge(gate_ready, (n + 1) * gates + g + 1)
                    if g:
                        dve.wait_ge(merged, n * 2 + g)
                    nc.vector.tensor_tensor(y if g == 0 else k.part[:, t], k.gate[:, g, t], k.ps[:, gates + g, t],
                                            ALU.mult).then_inc(products, 1)
                    if g:
                        dve.wait_ge(products, (n + 1) * gates + g + 1)
                        nc.vector.tensor_tensor(y, y, k.part[:, t], ALU.add).then_inc(merged, 1)

            dve.sem_inc(merged, 1)
            dve.sem_inc(products, gates)
            turns_ahead(dve, n_tiles, lambda i, s: weights.low(dve, i, s), merge)


def ffn_up_stage(k, weights, tokens, ahead):
    nc, streams = k.nc, tokens // SEQ
    t, n_tiles = slice(0, tokens), 2 * FC
    first_tile = lambda i: isinstance(i, int) and i == 0
    tap = [one(k.small1("conv_w").rearrange("p (w n) -> p w n", w=3), w) for w in range(3)]
    with stage(nc, *WEIGHT_SEMS, "centred", "convolved", "activated", "finished", weights=weights) as (
            block, high_ready, low_ready, halves_used, centred, convolved, activated, finished):
        weights.signals(high_ready, low_ready, halves_used)

        @block.sync
        def _(sp):
            weights.load(sp, ahead)

        @block.tensor
        def _(pe):
            def use(i, s):
                pe.wait_ge(convolved, (i * RAW + s) * 2 + 2)
                weights.contract(pe, i, s, lambda n: k.ps[:, s, t], lambda c: lambda p: k.hT[:, p, c, t])

            weights.slots_free(pe)
            turns(pe, n_tiles, use)

        @block.scalar
        def _(act):
            def centre(i, s):
                act.wait_ge(halves_used, weights.used(i, s))
                act.wait_ge(finished, i * 2 + s // 2 + 1)
                nc.scalar.activation(k.conv[:, s, t], k.ps[:, s, t], ACT.Copy,
                                     scale=tap[1][:, bass.ds(i * RAW + s, 1)]).then_inc(centred, 1)

            def activate(i, s):
                act.wait_ge(convolved, (i * RAW + s) * 2 + 10)
                nc.scalar.activation(k.conv[:, s, t], k.conv[:, s, t], ACT.Silu).then_inc(activated, 1)

            def finish(i, s):
                centre(i, s)
                if s == 2:
                    activate(i, 1)
                elif s == 0 and not first_tile(i):
                    activate(i - 1, RAW - 1)

            turns_ahead(act, n_tiles, lambda i, s: weights.high(act, i, s), finish, first=True)
            activate(n_tiles // RAW - 1, RAW - 1)

        @block.vector
        def _(dve):
            def convolve(i, s):
                u = k.ps[:, s, t].rearrange("p (a t) -> p a t", a=streams)
                a = k.conv[:, s, t].rearrange("p (a t) -> p a t", a=streams)
                dve.wait_ge(centred, i * RAW + s + 1)
                nc.vector.scalar_tensor_tensor(a[:, :, 1:SEQ], u[:, :, 0:SEQ - 1], tap[0][:, bass.ds(i * RAW + s, 1)],
                                               a[:, :, 1:SEQ], ALU.mult, ALU.add).then_inc(convolved, 1)
                dve.wait_ge(convolved, (i * RAW + s) * 2 + 9)
                nc.vector.scalar_tensor_tensor(a[:, :, 0:SEQ - 1], u[:, :, 1:SEQ], tap[2][:, bass.ds(i * RAW + s, 1)],
                                               a[:, :, 0:SEQ - 1], ALU.mult, ALU.add).then_inc(convolved, 1)

            def gate(i, s):
                dve.wait_ge(activated, i * 2 + s // 2 + 1)
                nc.vector.tensor_tensor(one(k.actT, i * 2 + s // 2)[:, t], k.conv[:, s - 1, t], k.conv[:, s, t],
                                        ALU.mult).then_inc(finished, 1)

            def finish(i, s):
                convolve(i, s)
                if s == 2:
                    gate(i, 1)
                elif s == 0 and not first_tile(i):
                    gate(i - 1, RAW - 1)

            dve.sem_inc(convolved, 8)
            dve.sem_inc(finished, 2)
            turns_ahead(dve, n_tiles, lambda i, s: weights.low(dve, i, s), finish, first=True)
            gate(n_tiles // RAW - 1, RAW - 1)


def first_block(k, sb):
    tables = [(k.const1_sb[:, :], k.const1_dram), (k.norm_final[:, :], k.norm_final_in)]
    w_mod = [Weights(k, k.w_mod, l * NMOD * DC, NMOD * DC) for l in range(DEPTH)]
    for l in range(DEPTH):
        w_qk, w_natural = Weights(k, k.w_qk, l * (1 + QC), 1 + QC), Weights(k, k.w_natural, l * DC, DC, NATURAL)
        w_merge, w_out = Weights(k, k.w_merge, l * 4 * DC, 4 * DC), Weights(k, k.w_out, l * DC, DC)
        w_up, w_down = Weights(k, k.w_up, l * 2 * FC, 2 * FC), Weights(k, k.w_down, l * FC, FC)
        tokens = SEQ if l == DEPTH - 1 else SEQ + CTX
        every = SEQ + CTX
        with ExitStack() as scope:
            k.mod_rows = sb(scope, f"mod_rows_{l}", 2, D)
            k.cond_split = sb(scope, f"cond_split_{l}", DC, P, dtype=F32R)
            needed = [(k.cond[:, :], k.cond_in), (k.const_sb[:, :], k.const_dram)] if l == 0 else []
            mod_stage(k, w_mod[l], [(k.small1_sb[:, :], k.small1_dram[l]), *needed], [(k.xT[:, :, :], k.x_in)] if l == 0 else [], w_qk)

        def part(m):
            return lambda c, s: k.mod[:, m * DC + c, s:s + 1]

        with ExitStack() as scope:
            k.norm_work = sb(scope, f"mix_norm_{l}", DC, every)
            norm_stage(k, every, part(1), part(0), k.xT, loads=tables if l == 0 else [])
        with ExitStack() as scope:
            k.branchT = sb(scope, f"branchT_{l}", 2, DC, every, dtype=F32R)
            k.natural = sb(scope, f"natural_{l}", every // P, NATURAL)
            with ExitStack() as attend:
                k.qkT = sb(attend, f"qkT_{l}", 1 + QC, every)
                k.qk_split = sb(attend, f"qk_split_{l}", 2, 1 + QC, every, dtype=F32R)
                k.scores, k.exps = sb(attend, f"scores_{l}", 2, every), sb(attend, f"exps_{l}", 2, every)
                k.probs, k.probsT = sb(attend, f"probs_{l}", 2, every), sb(attend, f"probsT_{l}", 2, every)
                qk_stage(k, w_qk, tokens, w_natural)
                natural_stage(k, w_natural, tokens, w_merge)
                attention_stage(k, tokens)
            with ExitStack() as fourier:
                k.pooledT, k.timedT = sb(fourier, f"pooledT_{l}", 4, SEQ), sb(fourier, f"timedT_{l}", 4, 2 * SEQ)
                pool_fourier_stage(k, tokens)
            k.yT = sb(scope, f"yT_{l}", DC, every)
            k.gate, k.part = sb(scope, f"gate_{l}", 3, every), sb(scope, f"part_{l}", every)
            merge_stage(k, w_merge, tokens, w_out)
            k.chunk = sb(scope, f"y_chunk_{l}", SPLIT, 2, every, dtype=F32R)
            residual_stage(k, tokens, w_out, DC, k.yT, part(2), k.xT, w_up)
        with ExitStack() as scope:
            k.norm_work = sb(scope, f"ffn_norm_{l}", DC, every)
            norm_stage(k, tokens, part(4), part(3), k.xT)
        with ExitStack() as scope:
            k.actT = sb(scope, f"actT_{l}", FC, every)
            k.conv = sb(scope, f"conv_{l}", RAW, every)
            k.chunk = sb(scope, f"act_chunk_{l}", SPLIT, 2, every, dtype=F32R)
            ffn_up_stage(k, w_up, tokens, w_down)
            residual_stage(k, tokens, w_down, FC, k.actT, part(5), k.xT, w_mod[l + 1] if l + 1 < DEPTH else None)
    with ExitStack() as scope:
        k.norm_work = sb(scope, "final_norm", DC, SEQ)
        norm_stage(k, SEQ, lambda c, s: k.norm_final[:, c:c + 1], None, k.xT, k.x2T)




def transposed_stage(k, weights, tiles, dst, ahead):
    nc = k.nc
    with stage(nc, *WEIGHT_SEMS, "copied", weights=weights) as (block, high_ready, low_ready, halves_used, copied):
        weights.signals(high_ready, low_ready, halves_used)

        @block.sync
        def _(sp):
            weights.load(sp, ahead)

        @block.scalar
        def _(act):
            turns(act, tiles, lambda i, s: weights.high(act, i, s))

        @block.tensor
        def _(pe):
            def use(i, s):
                pe.wait_ge(copied, i * RAW + s + 1)
                weights.contract(pe, i, s, lambda n: k.ps[:, s, 0:SEQ], lambda c: lambda p: k.hT[:, p, c, :])

            weights.slots_free(pe)
            turns(pe, tiles, use)

        @block.vector
        def _(dve):
            def copy(i, s):
                dve.wait_ge(halves_used, weights.used(i, s))
                nc.vector.tensor_copy(one(dst, i * RAW + s), k.ps[:, s, 0:SEQ]).then_inc(copied, 1)

            dve.sem_inc(copied, RAW)
            turns_ahead(dve, tiles, lambda i, s: weights.low(dve, i, s), copy)


def natural2_stage(k, weights, ahead):
    nc, half = k.nc, NATURAL2 // 2
    parts = [(b, h) for h in range(2) for b in range(TB)]
    h = slice(0, MLH)
    conv_w = k.small2("conv_w").rearrange("p (c w) -> p c w", c=6)
    i_row, f_row = k.gate_rows[h, 0, :], k.gate_rows[h, 1, :]
    bcum, a, M, carry, floor, w_row = (k.rows[h, n, :] for n in range(6))
    chunk = [slice(n * P, (n + 1) * P) for n in range(TB)]
    with stage(nc, *WEIGHT_SEMS, "summed", "copied", "gate_step", "conv_step", "convolved", "conv_ready", "scan_step",
               "log_step", "row_step", "turned", "column_ready", "key_scaled", weights=weights) as (
            block, high_ready, low_ready, halves_used, summed, copied, gate_step, conv_step, convolved, conv_ready, scan_step,
            log_step, row_step, turned, column_ready, key_scaled):
        weights.signals(high_ready, low_ready, halves_used)

        @block.sync
        def _(sp):
            weights.load(sp, ahead)

        @block.gpsimd
        def _(pool):
            turns(pool, DC, lambda i, s: weights.low(pool, i, s, nc.gpsimd))

        @block.tensor
        def _(pe):
            def use(c):
                for b, half_of in parts:
                    if b == 0:
                        weights.ready(pe, c // RAW, c % RAW, half_of)
                    last = product(nc, k.ps[:, 2 * b + half_of, 0:half], lambda p: k.hT[:, p, c, b * P:(b + 1) * P],
                                   weights.part(c % RAW, half_of * half, half), c == 0, c == DC - 1)
                    if c == DC - 1:
                        last.then_inc(summed, 1)
                    elif b == TB - 1:
                        last.then_inc(halves_used, 1)

            weights.slots_free(pe)
            for c in range(DC - 2):
                use(c)
            pe.wait_ge(row_step, 3)
            for n, row in enumerate((a[:, chunk[0]], a[:, chunk[1]], w_row[:, chunk[0]])):
                last = nc.tensor.transpose(k.ps[:, 4, MLW + n * MLH:MLW + (n + 1) * MLH], row, k.const("ident")[h, 0:MLH])
            last.then_inc(turned, 1)
            pair = k.const2("row_of_pair").rearrange("p (c m) -> p c m", c=DC)
            for c in range(MLH // 2):
                nc.tensor.matmul(k.ps[:, 5 + c // 2, c % 2 * SEQ:(c % 2 + 1) * SEQ], pair[h, c, :], floor, start=True, stop=True)
                last = nc.tensor.matmul(k.ps[:, 7, c * P:(c + 1) * P], pair[h, c, :], carry[:, chunk[1]], start=True, stop=True)
            last.then_inc(turned, 1)
            for c in range(DC - 2, DC):
                use(c)
            pe.wait_ge(key_scaled, 1)
            pe.wait_ge(column_ready, 1)
            for c in range(MLH // 2):
                last = nc.tensor.transpose(k.ps[:, 4, c * P:(c + 1) * P], k.qkconv[:, 3 + c, 0:P], k.const("ident"))
            last.then_inc(turned, 1)

        @block.scalar
        def _(act):
            act.wait_ge(gate_step, 4)
            nc.scalar.activation(k.soft[h, :], f_row, ACT.Abs).then_inc(log_step, 1)
            act.wait_ge(log_step, 1)
            nc.scalar.activation(k.soft[h, :], k.soft[h, :], ACT.Exp, scale=-1.0).then_inc(log_step, 1)
            act.wait_ge(log_step, 2)
            nc.scalar.activation(k.soft[h, :], k.soft[h, :], ACT.Ln, bias=1.0).then_inc(log_step, 1)
            for c in range(RAW):
                weights.high(act, 0, c)
            act.wait_ge(scan_step, 10)
            nc.scalar.activation(floor, floor, ACT.Exp, scale=-1.0).then_inc(row_step, 1)
            nc.scalar.activation(carry[:, chunk[1]], M[:, chunk[1]], ACT.Exp, scale=-1.0, bias=k.m_carry[h, :]).then_inc(row_step, 1)
            nc.scalar.activation(w_row[:, chunk[0]], a[:, chunk[0]], ACT.Exp, bias=k.neg_last[h, :]).then_inc(row_step, 1)
            for c in range(RAW):
                weights.high(act, 1, c)
            for c in range(6):
                act.wait_ge(convolved, c + 1)
                nc.scalar.activation(k.qkconv[:, c, :], k.qkconv[:, c, :], ACT.Silu).then_inc(conv_ready, 1)
            for n, (b, half_of) in enumerate(parts):
                if n % 2 == 0:
                    act.wait_ge(summed, n + 1)
                    nc.scalar.activation(k.natural2[:, b, half_of * half:(half_of + 1) * half], k.ps[:, 2 * b + half_of, 0:half],
                                         ACT.Copy).then_inc(copied, 1)

        @block.vector
        def _(dve):
            gate = Steps(dve, gate_step)
            for g in range(2):
                row = k.gate_rows[0:MLH, g, :]
                gate(nc.vector.tensor_copy(row, k.zT[g * GATE_ROWS:g * GATE_ROWS + MLH, ZIF, :]))
                gate(nc.vector.tensor_scalar(row, row, k.small2("if_b")[0:MLH, g:g + 1], None, ALU.add))
            scan = Steps(dve, scan_step)
            dve.wait_ge(log_step, 3)
            scan(nc.vector.tensor_scalar(f_row, f_row, 0.0, None, ALU.min))
            scan(nc.vector.tensor_tensor(f_row, f_row, k.soft[h, :], ALU.subtract))
            for n in range(TB):
                scan.step(nc.vector.tensor_tensor_scan(bcum[:, chunk[n]], k.const("ones")[h, :], f_row[:, chunk[n]], 0.0,
                                                       ALU.mult, ALU.add))
            scan.settle()
            scan(nc.vector.tensor_tensor(a, i_row, bcum, ALU.subtract))
            scan(nc.vector.tensor_tensor_scan(M[:, chunk[0]], a[:, chunk[0]], a[:, chunk[0]], 0.0, ALU.max, ALU.max))
            last = slice(P - 1, P)
            scan.step(nc.vector.tensor_tensor(k.m_carry[h, :], bcum[:, last], M[:, last], ALU.add))
            scan(nc.vector.tensor_scalar(k.neg_last[h, :], M[:, last], -1.0, None, ALU.mult))
            scan(nc.vector.tensor_tensor_scan(M[:, chunk[1]], a[:, chunk[1]], a[:, chunk[1]], k.m_carry[h, :], ALU.max, ALU.max))
            scan.step(nc.vector.tensor_tensor(floor, bcum, M, ALU.add))
            conv = Steps(dve, conv_step)
            for c in range(6):
                x, y = k.zT[:, ZMQ + c, :], k.qkconv[:, c, :]
                conv(nc.vector.tensor_scalar(y, x, conv_w[:, c, ML_CONV - 1:ML_CONV], k.small2("conv_b")[:, c:c + 1],
                                             ALU.mult, ALU.add))
                for back in range(1, ML_CONV):
                    w = conv_w[:, c, ML_CONV - 1 - back:ML_CONV - back]
                    tap = nc.vector.scalar_tensor_tensor(y[:, back:SEQ], x[:, 0:SEQ - back], w, y[:, back:SEQ], ALU.mult, ALU.add)
                    if back < ML_CONV - 1:
                        conv(tap)
                    else:
                        tap.then_inc(convolved, 1)
            dve.wait_ge(conv_ready, 6)
            nc.vector.tensor_scalar(k.qkconv[:, 3:6, :], k.qkconv[:, 3:6, :], float(HD) ** -0.5, None,
                                    ALU.mult).then_inc(key_scaled, 1)
            dve.wait_ge(turned, 1)
            nc.vector.tensor_copy(k.columns[:, :, :], k.ps[:, 4, MLW:MLW + 3 * MLH].rearrange("p (n h) -> p n h", n=3)).then_inc(column_ready, 1)
            dve.wait_ge(turned, 2)
            nc.vector.tensor_copy(k.floor[:, 0:2, :], k.ps[:, 5, :].rearrange("p (n t) -> p n t", n=2)).then_inc(column_ready, 1)
            nc.vector.tensor_copy(k.floor[:, 2, :], k.ps[:, 6, 0:SEQ]).then_inc(column_ready, 1)
            for c in range(MLH // 2):
                nc.vector.tensor_tensor(k.q_carry[:, c, :], k.qkconv[:, c, chunk[1]], k.ps[:, 7, c * P:(c + 1) * P],
                                        ALU.mult).then_inc(column_ready, 1)
            dve.wait_ge(turned, 3)
            dve.wait_ge(column_ready, 1)
            for n in range(MLH):
                nc.vector.tensor_scalar(k.k_keep[:, n * HD:(n + 1) * HD], k.ps[:, 4, n * HD:(n + 1) * HD],
                                        k.columns[:, 2, n:n + 1], None, ALU.mult).then_inc(column_ready, 1)
            for n, (b, half_of) in enumerate(parts):
                if n % 2 == 1:
                    dve.wait_ge(summed, n + 1)
                    nc.vector.tensor_copy(k.natural2[:, b, half_of * half:(half_of + 1) * half],
                                          k.ps[:, 2 * b + half_of, 0:half]).then_inc(copied, 1)


def head_norm_stage(k, src, chunks, gain, gate=None):
    nc = k.nc
    squares, wide = k.squares[:, 0:chunks, :], 2 * SEQ
    parts = chunks * SEQ // wide
    heads = 2 * chunks
    root = k.soft[0:heads, :]
    gather = k.const2("head_of_row").rearrange("p (c m) -> p c m", c=DC)
    spread_to = k.const2("row_of_pair").rearrange("p (c m) -> p c m", c=DC)
    with stage(nc, "squared", "summed", "var_ready", "rooted", "spread", "scaled", "gate_ready", "gated") as (
            block, squared, summed, var_ready, rooted, spread, scaled, gate_ready, gated):

        @block.scalar
        def _(act):
            for n in range(parts):
                nc.scalar.activation(squares[:, 2 * n:2 * n + 2, :], src[:, 2 * n:2 * n + 2, :], ACT.Square).then_inc(squared, 1)
            act.wait_ge(var_ready, 1)
            nc.scalar.activation(root, root, ACT.Sqrt).then_inc(rooted, 1)
            if gate is not None:
                nc.scalar.activation(gate[1], gate[1], ACT.Sigmoid).then_inc(gate_ready, 1)

        @block.tensor
        def _(pe):
            for c in range(chunks):
                if c % 2 == 0:
                    pe.wait_ge(squared, c // 2 + 1)
                last = nc.tensor.matmul(k.ps[0:heads, 0, 0:SEQ], gather[:, c, 0:heads], squares[:, c, :],
                                        start=c == 0, stop=c == chunks - 1)
            last.then_inc(summed, 1)
            pe.wait_ge(var_ready, 2)
            for c in range(chunks):
                nc.tensor.matmul(k.ps[:, 1 + c // 2, c % 2 * SEQ:(c % 2 + 1) * SEQ], spread_to[0:heads, c, :], root,
                                 start=True, stop=True).then_inc(spread, 1)

        @block.vector
        def _(dve):
            dve.wait_ge(summed, 1)
            nc.vector.tensor_scalar(root, k.ps[0:heads, 0, 0:SEQ], 1.0 / HD, EPS, ALU.mult, ALU.add).then_inc(var_ready, 1)
            dve.wait_ge(rooted, 1)
            nc.vector.reciprocal(root, root).then_inc(var_ready, 1)
            for c in range(chunks):
                if c % 2 == 0:
                    dve.wait_ge(spread, c + 2)
                nc.vector.scalar_tensor_tensor(src[:, c, :], src[:, c, :], gain(c), k.ps[:, 1 + c // 2, c % 2 * SEQ:(c % 2 + 1) * SEQ],
                                               ALU.mult, ALU.mult).then_inc(scaled, 1)
            if gate is not None:
                y = src[:, gate[0]:gate[0] + gate[1].shape[1], :]
                dve.wait_ge(gate_ready, 1)
                dve.wait_ge(scaled, chunks)
                nc.vector.tensor_tensor(y, y, gate[1], ALU.mult).then_inc(gated, 1)


def stick_breaking_stage(k):
    nc, width = k.nc, 3 * P
    half = SBH // 2 * width
    z, a, keep = k.z, k.z_abs, k.keep

    def flat(x, part):
        return x.rearrange("p h w -> p (h w)")[:, part * half:(part + 1) * half]

    with stage(nc, "scored", "score_kept", "magnitude", "log_ready", "keep_step", "suffixed", "exponent", "weights_ready",
               "weighed", "kept") as (
            block, scored, score_kept, magnitude, log_ready, keep_step, suffixed, exponent, weights_ready, weighed, kept):

        @block.tensor
        def _(pe):
            for h in range(SBH):
                base, c = HD * (h % 2), h // 2
                rows = slice(base, base + HD)
                if h >= 4:
                    pe.wait_ge(score_kept, h - 3)
                for b in range(TB):
                    last = nc.tensor.matmul(k.ps[:, h % 4, b * SEQ:b * SEQ + SEQ - b * P], k.zT[rows, ZK + c, b * P:(b + 1) * P],
                                            k.zT[rows, ZQ + c, b * P:SEQ], start=True, stop=True)
                last.then_inc(scored, 1)
            for h in range(SBH):
                pe.wait_ge(keep_step, 3 * (h // (SBH // 2)) + 3)
                if h >= 2:
                    pe.wait_ge(exponent, 2 * (h - 2) + 1)
                nc.tensor.matmul(k.ps[:, 4 + h % 2, 0:SEQ], k.const2("suffix"), keep[:, h, 0:SEQ], start=True, stop=False)
                nc.tensor.matmul(k.ps[:, 4 + h % 2, P:SEQ], k.const("ones"), keep[:, h, SEQ:width], start=False, stop=True)
                nc.tensor.matmul(k.ps[:, 4 + h % 2, SEQ:width], k.const2("suffix"), keep[:, h, SEQ:width],
                                 start=True, stop=True).then_inc(suffixed, 1)
            for h in range(SBH):
                base, c = HD * (h % 2), h // 2
                out = k.ps[base:base + HD, 6 + c % 2, 0:SEQ]
                pe.wait_ge(weights_ready, h + 1)
                if h >= 4:
                    pe.wait_ge(kept, h // 2 - 1)
                cols = slice(h * HD, (h + 1) * HD)
                nc.tensor.matmul(out, k.natural2[:, 0, cols], a[:, h, 0:SEQ], start=True, stop=False)
                nc.tensor.matmul(out[:, P:SEQ], k.natural2[:, 1, cols], a[:, h, SEQ:width],
                                 start=False, stop=True).then_inc(weighed, 1)

        @block.scalar
        def _(act):
            for h in range(SBH):
                act.wait_ge(scored, h + 1)
                nc.scalar.activation(z[:, h, :], k.ps[:, h % 4, 0:width], ACT.Copy,
                                     scale=float(HD) ** -0.5).then_inc(score_kept, 1)
            for part in range(2):
                act.wait_ge(score_kept, (part + 1) * SBH // 2)
                nc.scalar.activation(flat(a, part), flat(z, part), ACT.Abs).then_inc(magnitude, 1)
            for part in range(2):
                act.wait_ge(magnitude, part + 1)
                nc.scalar.activation(flat(a, part), flat(a, part), ACT.Exp, scale=-1.0).then_inc(magnitude, 1)
            for part in range(2):
                act.wait_ge(magnitude, part + 3)
                nc.scalar.activation(flat(a, part), flat(a, part), ACT.Ln, bias=1.0).then_inc(log_ready, 1)
            for h in range(SBH):
                act.wait_ge(exponent, 2 * h + 2)
                nc.scalar.activation(a[:, h, :], k.arg[:, h, :], ACT.Exp).then_inc(weights_ready, 1)

        @block.vector
        def _(dve):
            for part in range(2):
                n = 3 * part
                dve.wait_ge(score_kept, (part + 1) * SBH // 2)
                nc.vector.tensor_scalar(flat(keep, part), flat(z, part), -1.0, 0.0, ALU.mult, ALU.min).then_inc(keep_step, 1)
                dve.wait_ge(keep_step, n + 1)
                dve.wait_ge(log_ready, part + 1)
                nc.vector.tensor_tensor(flat(keep, part), flat(keep, part), flat(a, part), ALU.subtract).then_inc(keep_step, 1)
                dve.wait_ge(keep_step, n + 2)
                heads = slice(part * SBH // 2, (part + 1) * SBH // 2)
                nc.vector.tensor_tensor(keep[:, heads, :], keep[:, heads, :],
                                        k.const2("before").unsqueeze(1).broadcast_to([P, SBH // 2, width]),
                                        ALU.mult).then_inc(keep_step, 1)
            for h in range(SBH):
                dve.wait_ge(suffixed, h + 1)
                nc.vector.tensor_tensor(k.arg[:, h, :], z[:, h, :], k.ps[:, 4 + h % 2, 0:width], ALU.add).then_inc(exponent, 1)
                dve.wait_ge(exponent, 2 * h + 1)
                nc.vector.tensor_tensor(k.arg[:, h, :], k.arg[:, h, :], k.const2("not_before"), ALU.add).then_inc(exponent, 1)
            for c in range(SBH // 2):
                dve.wait_ge(weighed, 2 * c + 2)
                nc.vector.tensor_copy(k.y2T[:, c, :], k.ps[:, 6 + c % 2, 0:SEQ]).then_inc(kept, 1)


def mlstm_stage(k):
    nc = k.nc
    first, groups = SBW + MLW, TB * SGG
    sg_w = k.small2("sg_w").rearrange("p (g t) -> p g t", g=SGG)
    h6 = slice(0, MLH)
    M = k.rows[h6, 2, :]
    chunk = [slice(n * P, (n + 1) * P) for n in range(TB)]
    row = k.const2("row_of_head").rearrange("p (h m) -> p h m", h=MLH)
    with stage(nc, "spread", "masked", "decayed", "scored", "probs_ready", "state_summed", "state_kept", "summed",
               "den_step", "finished", "gelu_done", "squared", "var_step", "rooted", "normed", "causal", "gated",
               "gating_done") as (
            block, spread, masked, decayed, scored, probs_ready, state_summed, state_kept, summed, den_step, finished,
            gelu_done, squared, var_step, rooted, normed, causal, gated, gating_done):

        @block.tensor
        def _(pe):
            for h in range(MLH):
                rows = slice(HD * (h % 2), HD * (h % 2 + 1))
                keys = k.k_keep[:, h * HD:(h + 1) * HD]
                nc.tensor.matmul(k.ps[rows, 0, h // 2 * P:h // 2 * P + HD], keys,
                                 k.natural2[:, 0, SBW + h * HD:SBW + (h + 1) * HD], start=True, stop=True)
                last = nc.tensor.matmul(k.ps[rows, 0, h // 2 * P + HD:(h // 2 + 1) * P], keys, k.const("ones")[:, 0:HD],
                                        start=True, stop=True)
            last.then_inc(state_summed, 1)

            def score(h):
                base, c = HD * (h % 2), h // 2
                rows = slice(base, base + HD)
                if h >= 2:
                    pe.wait_ge(masked, h - 1)
                nc.tensor.matmul(k.ps[:, 1 + h % 2, 0:SEQ], row[h6, h, :], M, start=True, stop=True).then_inc(spread, 1)
                if h >= 2:
                    pe.wait_ge(probs_ready, h - 1)
                for n in range(TB):
                    last = nc.tensor.matmul(k.ps[:, 3 + h % 2, chunk[n]], k.qkconv[rows, 3 + c, chunk[n]],
                                            k.qkconv[rows, c, chunk[n]], start=True, stop=True)
                last.then_inc(scored, 1)

            def weigh(h):
                base, c = HD * (h % 2), h // 2
                rows = slice(base, base + HD)
                pe.wait_ge(probs_ready, h + 1)
                if h == 0:
                    pe.wait_ge(state_kept, 1)
                if h % 2 == 0 and c >= 1:
                    pe.wait_ge(finished, c)
                probs = k.ml_probs[:, h % 2, :]
                for bank, within, state in ((5, [k.natural2[:, n, SBW + h * HD:SBW + (h + 1) * HD] for n in range(TB)], 0),
                                            (6, [k.const("ones")[:, 0:HD]] * TB, HD)):
                    nc.tensor.matmul(k.ps[rows, bank, chunk[0]], within[0], probs[:, chunk[0]], start=True, stop=True)
                    nc.tensor.matmul(k.ps[rows, bank, chunk[1]], k.state[rows, c * P + state:c * P + state + HD],
                                     k.q_carry[rows, c, :], start=True, stop=False)
                    last = nc.tensor.matmul(k.ps[rows, bank, chunk[1]], within[1], probs[:, chunk[1]], start=False, stop=True)
                last.then_inc(summed, 1)

            def mix():
                pe.wait_ge(normed, groups)
                pe.wait_ge(causal, SGG)
                for a in range(2):
                    for g in (2 * a, 2 * a + 1):
                        rows = slice(HD * (g % 2), HD * (g % 2 + 1))
                        for b in range(TB):
                            out = k.ps[rows, 7, a * SEQ + b * P:a * SEQ + (b + 1) * P]
                            nc.tensor.matmul(out, k.natural2[:, b, first + g * HD:first + (g + 1) * HD], sg_w[:, g, :],
                                             start=True, stop=False)
                            last = nc.tensor.matmul(out, k.const("ones")[0:1, 0:HD], k.small2("sg_b")[0:1, g * P:(g + 1) * P],
                                                    start=False, stop=True)
                    last.then_inc(gated, 1)

            score(0)
            for h in range(MLH):
                if h + 1 < MLH:
                    score(h + 1)
                weigh(h)
                if h == 1:
                    mix()

        @block.scalar
        def _(act):
            for b in range(TB):
                v = k.natural2[:, b, first:first + SGW]
                nc.scalar.activation(v, v, ACT.Gelu_apprx_tanh).then_inc(gelu_done, 1)
            u = k.zT[:, ZU:ZU + 2, :]
            nc.scalar.activation(u, u, ACT.Gelu_apprx_tanh).then_inc(gelu_done, 1)
            for b in range(TB):
                act.wait_ge(gelu_done, b + 1)
                nc.scalar.activation(k.v_square[:, b * SGW:(b + 1) * SGW], k.natural2[:, b, first:first + SGW],
                                     ACT.Square).then_inc(squared, 1)
            act.wait_ge(var_step, 2)
            nc.scalar.activation(k.v_rstd[:, :], k.v_rstd[:, :], ACT.Sqrt).then_inc(rooted, 1)
            act.wait_ge(state_summed, 1)
            nc.scalar.activation(k.state[:, :], k.ps[:, 0, 0:MLH // 2 * P], ACT.Copy).then_inc(state_kept, 1)

            def decays(h):
                act.wait_ge(masked, h + 1)
                for n in range(TB):
                    nc.scalar.activation(k.decay[:, h % 2, chunk[n]], k.ahead[:, h % 2, chunk[n]], ACT.Exp, scale=-1.0,
                                         bias=k.columns[:, n, h:h + 1]).then_inc(decayed, 1)

            decays(0)
            for h in range(MLH):
                if h + 1 < MLH:
                    decays(h + 1)
                if h % 2:
                    act.wait_ge(summed, h + 1)
                    nc.scalar.activation(k.den[:, :], k.ps[:, 6, 0:SEQ], ACT.Abs).then_inc(den_step, 1)

        @block.vector
        def _(dve):
            def mask(h):
                dve.wait_ge(spread, h + 1)
                if h >= 2:
                    dve.wait_ge(decayed, 2 * (h - 1))
                nc.vector.tensor_tensor(k.ahead[:, h % 2, :], k.ps[:, 1 + h % 2, 0:SEQ], k.const2("ahead"), ALU.add).then_inc(masked, 1)

            for g in range(SGG):
                nc.vector.tensor_tensor(sg_w[:, g, :], sg_w[:, g, :], k.const2("causal"), ALU.mult).then_inc(causal, 1)
            dve.wait_ge(squared, TB)
            nc.vector.reduce_sum(k.v_rstd[:, :], k.v_square[:, :].rearrange("p (g d) -> p g d", g=groups), AX_X).then_inc(var_step, 1)
            dve.wait_ge(var_step, 1)
            nc.vector.tensor_scalar(k.v_rstd[:, :], k.v_rstd[:, :], 1.0 / HD, EPS, ALU.mult, ALU.add).then_inc(var_step, 1)
            dve.wait_ge(rooted, 1)
            nc.vector.reciprocal(k.v_rstd[:, :], k.v_rstd[:, :]).then_inc(var_step, 1)
            dve.wait_ge(var_step, 3)
            for b in range(TB):
                for g in range(SGG):
                    v = k.natural2[:, b, first + g * HD:first + (g + 1) * HD]
                    nc.vector.scalar_tensor_tensor(v, v, k.v_rstd[:, b * SGG + g:b * SGG + g + 1],
                                                   k.small2("vn_g")[:, g * HD:(g + 1) * HD], ALU.mult, ALU.mult).then_inc(normed, 1)
            mask(0)
            for h in range(MLH):
                if h + 1 < MLH:
                    mask(h + 1)
                dve.wait_ge(scored, h + 1)
                dve.wait_ge(decayed, 2 * h + 2)
                if h >= 2:
                    dve.wait_ge(summed, h - 1)
                nc.vector.tensor_tensor(k.ml_probs[:, h % 2, :], k.decay[:, h % 2, :], k.ps[:, 3 + h % 2, 0:SEQ],
                                        ALU.mult).then_inc(probs_ready, 1)
                if h % 2:
                    c = h // 2
                    dve.wait_ge(den_step, 3 * c + 1)
                    nc.vector.tensor_tensor(k.den[:, :], k.den[:, :], k.floor[:, c, :], ALU.max).then_inc(den_step, 1)
                    dve.wait_ge(den_step, 3 * c + 2)
                    nc.vector.reciprocal(k.den[:, :], k.den[:, :]).then_inc(den_step, 1)
                    dve.wait_ge(den_step, 3 * c + 3)
                    nc.vector.tensor_tensor(k.y2T[:, YML + c, :], k.den[:, :], k.ps[:, 5, 0:SEQ], ALU.mult).then_inc(finished, 1)
            dve.wait_ge(gelu_done, TB + 1)
            dve.wait_ge(gated, 2)
            for a in range(2):
                nc.vector.tensor_tensor(k.y2T[:, YSG + a, :], k.zT[:, ZU + a, :], k.ps[:, 7, a * SEQ:(a + 1) * SEQ], ALU.mult).then_inc(gating_done, 1)


def choose_stage(k, l, weights):
    nc, pairs = k.nc, TB * PH
    n_tiles, low = HC + EARLY, -3.0e38
    last_turn = n_tiles // RAW - 1
    best = lambda half: slice(8 * half, 8 * half + 8)
    with stage(nc, *WEIGHT_SEMS, "keys_in", "kept", "scored", "scores_used", "row_step", "step", "gate_step", "turned",
               "slots_ready", weights=weights) as (
            block, high_ready, low_ready, halves_used, keys_in, kept, scored, scores_used, row_step,
            step, gate_step, turned, slots_ready):
        weights.signals(high_ready, low_ready, halves_used)

        @block.sync
        def _(sp):
            sp.dma_start(k.keysT, tile(k.peer_keys, l)).then_inc(keys_in, 16)
            weights.load(sp)

        @block.gpsimd
        def _(pool):
            turns(pool, n_tiles, lambda i, s: weights.low(pool, i, s, nc.gpsimd))

        @block.tensor
        def _(pe):
            def use(i, s):
                pe.wait_ge(kept, i * RAW + s + 1)
                weights.contract(pe, i, s, lambda n: k.ps[:, s, 0:SEQ], lambda c: lambda p: k.hT[:, p, c, :])

            def score(i, s):
                pe.wait_ge(kept, i * RAW + s + 1 + RAW)
                pe.wait_ge(scores_used, i * RAW + s + 1)
                for b in range(TB):
                    last = nc.tensor.matmul(k.ps[:, RAW + s, b * NK:(b + 1) * NK], k.queryT[:, s, b * P:(b + 1) * P],
                                            k.keysT[:, bass.ds((i * RAW + s) * NK, NK)], start=True, stop=True)
                last.then_inc(scored, 1)

            weights.slots_free(pe)
            for s in range(RAW):
                use(0, s)
                if s == 1:
                    pe.wait_ge(keys_in, 16)
                if s:
                    score(0, s - 1)
            with pe.Fori(1, HC // RAW) as i:
                for s in range(RAW):
                    use(i, s)
                    score(i + (s - 1) // RAW, (s - 1) % RAW)
            score(HC // RAW - 1, RAW - 1)
            with pe.Fori(HC // RAW, last_turn + 1) as i:
                for s in range(RAW):
                    use(i, s)
            pe.wait_ge(kept, n_tiles + RAW)
            pe.wait_ge(gate_step, 5)
            for n, x in enumerate((k.key_i, k.key_j, k.gates)):
                for b in range(TB):
                    last = nc.tensor.transpose(k.ps[:, n, b * P:(b + 1) * P], x[:, b * SLOTS:(b + 1) * SLOTS], k.const("ident"))
            last.then_inc(turned, 1)

        @block.scalar
        def _(act):
            def high(i, s):
                weights.high(act, i + (s + SPLIT) // RAW, (s + SPLIT) % RAW)

            def keep_query(i, s):
                act.wait_ge(halves_used, weights.used(i, s))
                act.wait_ge(scored, i * RAW + s + 1)
                nc.scalar.activation(k.queryT[:, s, :], k.ps[:, s, 0:SEQ], ACT.Copy).then_inc(kept, 1)

            def keep_early(i, s):
                act.wait_ge(halves_used, weights.used(i, s))
                nc.scalar.activation(one(k.early, i * RAW + s - HC), k.ps[:, s, 0:SEQ], ACT.Gelu_apprx_tanh).then_inc(kept, 1)

            act.sem_inc(kept, RAW)
            act.sem_inc(scored, RAW)
            for s in range(SPLIT):
                weights.high(act, 0, s)
            with act.Fori(0, HC // RAW) as i:
                for s in range(RAW):
                    high(i, s)
                    keep_query(i, s)
            with act.Fori(HC // RAW, last_turn) as i:
                for s in range(RAW):
                    high(i, s)
                    keep_early(i, s)
            for s in range(RAW):
                if s + SPLIT < RAW:
                    high(last_turn, s)
                keep_early(last_turn, s)
            act.wait_ge(gate_step, 1)
            nc.scalar.activation(k.gates[:, :], k.gates[:, :], ACT.Exp).then_inc(gate_step, 1)

        @block.vector
        def _(dve):
            def best_keys(n):
                scores = lambda b: k.ps[:, RAW + n % RAW, b * NK:(b + 1) * NK]
                spare = lambda b: k.key_spare[:, n % 2, b * NK:(b + 1) * NK]
                value = lambda b, half: k.half_val[:, b * HC + n, best(half)]
                at = lambda b, half: k.half_at[:, b * HC + n, best(half)]
                dve.wait_ge(scored, n + 1 + RAW)
                for b in range(TB):
                    rows.step(nc.vector.max(value(b, 0), scores(b)))
                rows.settle()
                for b in range(TB):
                    rows.step(nc.vector.max_index(at(b, 0), value(b, 0), scores(b)))
                    rows.step(nc.vector.match_replace(spare(b), value(b, 0), scores(b), low))
                rows.settle()
                dve.sem_inc(scores_used, 1)
                for b in range(TB):
                    rows.step(nc.vector.max(value(b, 1), spare(b)))
                rows.settle()
                for b in range(TB):
                    rows.step(nc.vector.max_index(at(b, 1), value(b, 1), spare(b)))

            rows = Steps(dve, row_step)
            dve.sem_inc(scores_used, RAW)
            for n in range(HC):
                best_keys(n)
            rows.settle()
            s = Steps(dve, step)

            def top16(n, scores, spare, values, index, width):
                at = lambda x, r: x[:, r * width:(r + 1) * width]
                for r in range(n):
                    s.step(nc.vector.max(values[:, r, best(0)], at(scores, r)))
                s.settle()
                for r in range(n):
                    s.step(nc.vector.max_index(index[:, r, best(0)], values[:, r, best(0)], at(scores, r)))
                    s.step(nc.vector.match_replace(at(spare, r), values[:, r, best(0)], at(scores, r), low))
                s.settle()
                for r in range(n):
                    s.step(nc.vector.max(values[:, r, best(1)], at(spare, r)))
                s.settle()
                for r in range(n):
                    s.step(nc.vector.max_index(index[:, r, best(1)], values[:, r, best(1)], at(spare, r)))
                s.settle()

            s(nc.vector.tensor_copy(k.half_key[:, :, :], k.half_at[:, :, :]))
            for n in range(pairs):
                cand = k.cand[:, n * 256:(n + 1) * 256].rearrange("p (a b) -> p a b", a=TOPK)
                s.step(nc.vector.tensor_tensor(cand, k.half_val[:, 2 * n, :].unsqueeze(2).broadcast_to([P, TOPK, TOPK]),
                                               k.half_val[:, 2 * n + 1, :].unsqueeze(1).broadcast_to([P, TOPK, TOPK]), ALU.add))
            s.settle()
            top16(pairs, k.cand, k.cand_spare, k.pair_val, k.pair_at, TOPK * TOPK)
            flat_at = k.pair_at[:, :, :].rearrange("p n k -> p (n k)")
            for key, half, op, by in ((k.key_i, 0, ALU.logical_shift_right, 4), (k.key_j, 1, ALU.bitwise_and, TOPK - 1)):
                s(nc.vector.tensor_scalar(k.place_int[:, :], flat_at, by, None, op))
                s(nc.vector.tensor_copy(k.place[:, :], k.place_int[:, :]))
                for n in range(pairs):
                    hot = k.cand[:, n * 256:(n + 1) * 256].rearrange("p (k a) -> p k a", a=TOPK)
                    s.step(nc.vector.tensor_tensor(hot, k.place[:, n * TOPK:(n + 1) * TOPK].unsqueeze(2).broadcast_to([P, TOPK, TOPK]),
                                                   k.const("iota")[:, 0:TOPK].unsqueeze(1).broadcast_to([P, TOPK, TOPK]), ALU.is_equal))
                s.settle()
                for n in range(pairs):
                    hot = k.cand[:, n * 256:(n + 1) * 256].rearrange("p (k a) -> p k a", a=TOPK)
                    s.step(nc.vector.tensor_tensor(hot, hot, k.half_key[:, 2 * n + half, :].unsqueeze(1).broadcast_to([P, TOPK, TOPK]),
                                                   ALU.mult))
                s.settle()
                s(nc.vector.reduce_sum(key[:, :], k.cand[:, :].rearrange("p (m a) -> p m a", a=TOPK), AX_X))
            gates = k.gates[:, :].rearrange("p (n k) -> p n k", k=TOPK)
            nc.vector.tensor_tensor(gates, k.pair_val[:, :, :], k.pair_val[:, :, 0:1].broadcast_to([P, pairs, TOPK]),
                                    ALU.subtract).then_inc(gate_step, 1)
            dve.wait_ge(gate_step, 2)
            nc.vector.reduce_sum(k.gate_sum[:, :], gates, AX_X).then_inc(gate_step, 1)
            dve.wait_ge(gate_step, 3)
            nc.vector.reciprocal(k.gate_sum[:, :], k.gate_sum[:, :]).then_inc(gate_step, 1)
            dve.wait_ge(gate_step, 4)
            nc.vector.tensor_tensor(gates, gates, k.gate_sum[:, :].unsqueeze(2).broadcast_to([P, pairs, TOPK]),
                                    ALU.mult).then_inc(gate_step, 1)
            dve.wait_ge(turned, 1)
            for n, x in enumerate((k.slot_i, k.slot_j, k.slot_gate)):
                nc.vector.tensor_copy(x[:, :], k.ps[:, n, 0:SEQ]).then_inc(slots_ready, 1)


def scatter_stage(k):
    nc, lot, lots, late = k.nc, 4, 4, NK - EARLY
    turns_all = SEQ // (lots * lot)
    iota = k.const("iota").unsqueeze(1).broadcast_to([P, lot, NK])
    token = lambda i, n: (i * lots + n) * lot

    def lagged(eng, make, keep, lag):
        for n in range(lots):
            make(0, n)
            if n >= lag:
                keep(0, n - lag)
        with eng.Fori(1, turns_all) as i:
            for n in range(lots):
                make(i, n)
                keep(i + (n - lag) // lots, (n - lag) % lots)
        for n in range(lots - lag, lots):
            keep(turns_all - 1, n)

    with stage(nc, "one_hot", "gated", "spread", "copied", "weighted") as (block, one_hot, gated, spread, copied, weighted):

        @block.vector
        def _(dve):
            def one_hots(i, n):
                dve.wait_ge(spread, i * lots + n + 1)
                for hot, slot, many in ((k.hot_i, k.slot_i, lot - 1), (k.hot_j, k.slot_j, lot)):
                    keys = slot[:, bass.ds(token(i, n), many)].unsqueeze(2).broadcast_to([P, many, NK])
                    nc.vector.tensor_tensor(hot[:, n * lot:n * lot + many, :], iota[:, 0:many, :], keys,
                                            ALU.is_equal).then_inc(one_hot, 1)
                t = bass.ds(token(i, n) + lot - 1, 1)
                nc.vector.tensor_scalar(k.hot_i[:, n * lot + lot - 1, :], k.const("iota"), k.slot_i[:, t], k.slot_gate[:, t],
                                        ALU.is_equal, ALU.mult).then_inc(one_hot, 1)

            def weigh_early(i, n):
                early = k.early[:, :, bass.ds(token(i, n), lot)]
                dve.wait_ge(copied, i * lots + n + 1)
                nc.vector.tensor_tensor(early, early, k.ps[:, n, :].rearrange("p (t j) -> p j t", t=lot)[:, 0:EARLY, :],
                                        ALU.mult).then_inc(weighted, 1)

            dve.sem_inc(weighted, lots)
            lagged(dve, one_hots, weigh_early, 2)

        @block.tensor
        def _(pe):
            pe.sem_inc(spread, lots)
            with pe.Fori(0, turns_all) as i:
                for n in range(lots):
                    pe.wait_ge(weighted, i * lots + n + 1)
                    pe.wait_ge(one_hot, (i * lots + n) * 3 + 3)
                    for u in range(lot):
                        if u < lot - 1:
                            pe.wait_ge(gated, (i * lots + n) * (lot - 1) + u + 1)
                        last = nc.tensor.matmul(k.ps[:, n, u * NK:(u + 1) * NK], k.hot_i[:, n * lot + u, :],
                                                k.hot_j[:, n * lot + u, :], start=True, stop=True)
                    last.then_inc(spread, 1)

        @block.scalar
        def _(act):
            def gate(i, n):
                act.wait_ge(one_hot, (i * lots + n) * 3 + 1)
                for u in range(lot - 1):
                    hot = k.hot_i[:, n * lot + u, :]
                    nc.scalar.activation(hot, hot, ACT.Copy,
                                         scale=k.slot_gate[:, bass.ds(token(i, n) + u, 1)]).then_inc(gated, 1)

            def keep(i, n):
                act.wait_ge(spread, i * lots + n + 1 + lots)
                nc.scalar.activation(
                    k.dense[:, bass.ds(token(i, n) * late, lot * late)].rearrange("p (t j) -> p t j", t=lot),
                    k.ps[:, n, :].rearrange("p (t j) -> p t j", t=lot)[:, :, EARLY:NK], ACT.Copy).then_inc(copied, 1)

            lagged(act, gate, keep, 1)


def experts_stage(k, weights):
    nc, n_tiles = k.nc, EARLY + 2 * (NK - EARLY)
    first_turn, last_turn = EARLY // RAW, n_tiles // RAW - 1
    dense = k.dense[:, :].rearrange("p (t j) -> p t j", j=NK - EARLY)
    outs = [k.ps[:, 2 + n, :] for n in range(4)]

    def turn_loop(eng, body):
        def turn(i, first=False, last=False):
            j = 2 * (i - first_turn) + EARLY
            tiles = [(True, j, 0) if first else (False, j - 1, 1), (True, j + 1, 1), (False, j, 0),
                     (False, j + 1, 1) if last else (True, j + 2, 0)]
            for s, (is_u, j, buf) in enumerate(tiles):
                body(i, s, is_u, j, buf, first, last)

        turn(first_turn, first=True)
        with eng.Fori(first_turn + 1, last_turn) as i:
            turn(i)
        turn(last_turn, last=True)

    def prepare_ahead(prepare, i, s, last):
        if not last or s + SPLIT < RAW:
            prepare(i + (s + SPLIT) // RAW, (s + SPLIT) % RAW)

    with stage(nc, *WEIGHT_SEMS, "gelu_done", "weight_step", "weighted", "kept", "turned", "added", weights=weights) as (
            block, high_ready, low_ready, halves_used, gelu_done, weight_step, weighted, kept, turned, added):
        weights.signals(high_ready, low_ready, halves_used)

        @block.sync
        def _(sp):
            weights.load(sp)

        @block.tensor
        def _(pe):
            def activate(i, s, j, buf):
                pe.wait_ge(gelu_done, j - EARLY + 1)
                weights.contract(pe, i, s, lambda n: k.ps[:, buf, 0:SEQ], lambda c: lambda p: k.hT[:, p, c, :])

            def combine(i, s, j, buf, first, last):
                pe.wait_ge(weighted, j + 3)
                for half in range(2):
                    weights.ready(pe, i, s, half)
                    for b in range(TB):
                        ins = product(nc, outs[2 * b + half], lambda p: k.weight[:, buf, p, b * P:(b + 1) * P],
                                      weights.part(s, half * 512, 512), first, last)
                    ins.then_inc(halves_used, 1)

            def use(i, s, is_u, j, buf, first, last):
                if is_u:
                    activate(i, s, j, buf)
                else:
                    combine(i, s, j, buf, False, last and s == RAW - 1)

            weights.slots_free(pe)
            for s in range(RAW):
                combine(0, s, s, s % 2, s == 0, False)
            with pe.Fori(1, first_turn) as i:
                for s in range(RAW):
                    combine(i, s, i * RAW + s, s % 2, False, False)
            turn_loop(pe, use)
            pe.wait_ge(kept, len(outs))
            for c in range(DC):
                if c >= 2:
                    pe.wait_ge(added, c - 1)
                for b in range(TB):
                    ins = nc.tensor.transpose(k.ps[:, c % 2, b * P:(b + 1) * P], k.y_natural[:, b, c * P:(c + 1) * P],
                                              k.const("ident"))
                ins.then_inc(turned, 1)

        @block.scalar
        def _(act):
            def activate(i, s, is_u, j, buf, first, last):
                prepare_ahead(lambda i, s: weights.high(act, i, s), i, s, last)
                if is_u:
                    act.wait_ge(halves_used, weights.used(i, s))
                    act.wait_ge(weighted, j + 1)
                    nc.scalar.activation(k.gelu[:, buf, :], k.ps[:, buf, 0:SEQ], ACT.Gelu_apprx_tanh).then_inc(gelu_done, 1)

            act.sem_inc(gelu_done, 2)
            for s in range(SPLIT):
                weights.high(act, 0, s)
            with act.Fori(0, first_turn) as i:
                for s in range(RAW):
                    prepare_ahead(lambda i, s: weights.high(act, i, s), i, s, False)
            turn_loop(act, activate)
            act.wait_ge(halves_used, weights.used(last_turn, RAW - 1))
            for n, out in enumerate(outs):
                nc.scalar.activation(k.y_natural[:, n // 2, n % 2 * 512:(n % 2 + 1) * 512], out, ACT.Copy).then_inc(kept, 1)

        @block.vector
        def _(dve):
            def split_early(i, s):
                j = i * RAW + s
                w, high, low = one(k.early, j), k.weight[:, s % 2, 0, :], k.weight[:, s % 2, 1, :]
                dve.wait_ge(halves_used, (j + SPLIT) * 2 - 2)
                nc.vector.tensor_copy(high, w).then_inc(weight_step, 1)
                dve.wait_ge(weight_step, j + 1)
                nc.vector.tensor_tensor(low, w, high.bitcast(F32), ALU.subtract).then_inc(weighted, 1)

            def weigh(i, s, is_u, j, buf, first, last):
                prepare_ahead(lambda i, s: weights.low(dve, i, s), i, s, last)
                if not is_u:
                    return
                high, low = k.weight[:, buf, 0, :], k.weight[:, buf, 1, :]
                dve.wait_ge(gelu_done, j - EARLY + 3)
                dve.wait_ge(weighted, j + 2)
                if first and s < 2:
                    dve.wait_ge(halves_used, weights.used(first_turn - 1, RAW - 2 + s))
                else:
                    dve.wait_ge(halves_used, weights.used(first_turn, 2) + (j - EARLY - 2) * 4)
                nc.vector.tensor_tensor(k.gated[:, :], k.gelu[:, buf, :], dense[:, :, bass.ds(j - EARLY, 1)].rearrange("p t j -> p (t j)"),
                                        ALU.mult).then_inc(weight_step, 1)
                dve.wait_ge(weight_step, j * 2 - EARLY + 1)
                nc.vector.tensor_copy(high, k.gated[:, :]).then_inc(weight_step, 1)
                dve.wait_ge(weight_step, j * 2 - EARLY + 2)
                nc.vector.tensor_tensor(low, k.gated[:, :], high.bitcast(F32), ALU.subtract).then_inc(weighted, 1)

            dve.sem_inc(weighted, 2)
            def prepare_early(i, s):
                weights.low(dve, i, s)
                split_early(i, s)

            for s in range(SPLIT):
                prepare_early(0, s)
            with dve.Fori(0, first_turn - 1) as i:
                for s in range(RAW):
                    prepare_ahead(prepare_early, i, s, False)
            for s in range(RAW):
                prepare_ahead(prepare_early if s + SPLIT < RAW else lambda i, s: weights.low(dve, i, s), first_turn - 1, s, False)
            turn_loop(dve, weigh)
            for c in range(DC):
                dve.wait_ge(turned, c + 1)
                nc.vector.tensor_tensor(k.x2T[:, c, :], k.x2T[:, c, :], k.ps[:, c % 2, 0:SEQ], ALU.add).then_inc(added, 1)


def second_block(k, scope, sb):
    nc = k.nc
    k.hT = sb(scope, "h2T", 2, DC, SEQ, dtype=F32R)
    k.chunk = sb(scope, "chunk2", SPLIT, 2, SEQ, dtype=F32R)
    k.weight = k.chunk
    k.slot_i, k.slot_j, k.slot_gate = (sb(scope, f"slot_{n}", SEQ) for n in ("i", "j", "gate"))
    k.gelu, k.gated = sb(scope, "gelu", 2, SEQ), sb(scope, "gated", SEQ)
    hot = Carver(k.ring.rearrange("p s m -> p (s m)"))
    k.hot_i, k.hot_j = hot(16, NK), hot(16, NK)
    gates = sb(scope, "gates", SEQ * NK)
    k.early = gates[:, 0:EARLY * SEQ].rearrange("p (j t) -> p j t", j=EARLY)
    k.dense = gates[:, EARLY * SEQ:]

    mix = Carver(gates)
    k.const2_sb, k.small2_sb = mix(CONST2_W), mix(SMALL2_W)
    k.zT, k.natural2 = mix(ZC, SEQ), mix(TB, NATURAL2)
    k.y2T, k.squares = mix(DC, SEQ), mix(DC, SEQ)
    k.z, k.z_abs, k.keep, k.arg = (mix(SBH, 3 * P) for _ in range(4))
    k.norm_work = k.squares
    k.gate_rows, k.rows, k.soft = mix(2, SEQ), mix(6, SEQ), mix(SEQ)
    k.m_carry, k.neg_last, k.columns, k.qkconv = mix(1), mix(1), mix(3, MLH), mix(6, SEQ)
    k.floor, k.q_carry, k.k_keep = mix(MLH // 2, SEQ), mix(MLH // 2, P), mix(MLW)
    more = Carver(k.keep.rearrange("p h w -> p (h w)"))
    k.state, k.ahead, k.decay, k.ml_probs = more(MLH // 2 * P), more(2, SEQ), more(2, SEQ), more(2, SEQ)
    more = Carver(k.arg.rearrange("p h w -> p (h w)"))
    k.den, k.v_square, k.v_rstd = more(SEQ), more(TB * SGW), more(TB * SGG)

    choose = Carver(k.dense)
    k.queryT, k.keysT = choose(RAW, SEQ), choose(HC * NK)
    k.key_spare = choose(2, TB * NK)
    k.half_val, k.half_key = choose(TB * HC, TOPK), choose(TB * HC, TOPK)
    k.half_at = choose(TB * HC, TOPK).bitcast(U32)
    pairs = TB * PH
    k.pair_val, k.pair_at = choose(pairs, TOPK), choose(pairs, TOPK).bitcast(U32)
    k.place, k.place_int = choose(pairs * TOPK), choose(pairs * TOPK).bitcast(U32)
    k.key_i, k.key_j, k.gates, k.gate_sum = choose(TB * SLOTS), choose(TB * SLOTS), choose(TB * SLOTS), choose(pairs)
    k.cand, k.cand_spare = choose(pairs * TOPK * TOPK), choose(pairs * TOPK * TOPK)
    k.y_natural = Carver(k.dense)(TB, D)

    with nc.Fori(0, DEPTH) as l:
        w_transposed, w_natural = Weights(k, k.w_transposed2, l * ZC, ZC), Weights(k, k.w_natural2, l * DC, DC, NATURAL2)
        w_out, w_choose = Weights(k, k.w_out2, l * DC, DC), Weights(k, k.w_choose, l * (HC + EARLY), HC + EARLY)
        expert_tiles = EARLY + 2 * (NK - EARLY)
        w_experts = Weights(k, k.peer_uv, l * expert_tiles, expert_tiles)
        norm_stage(k, SEQ, lambda c, s: k.small2("norm1")[:, c:c + 1], None, k.x2T,
                   loads=[(k.small2_sb, tile(k.small2_dram, l)), (k.const2_sb, k.const2_dram)], ahead=w_transposed)
        transposed_stage(k, w_transposed, ZC, k.zT, w_natural)
        natural2_stage(k, w_natural, w_out)
        head_norm_stage(k, k.zT[:, 0:6, :], 6, lambda c: k.small2("qn_g" if c < ZK else "kn_g"))
        stick_breaking_stage(k)
        mlstm_stage(k)
        head_norm_stage(k, k.y2T, DC, lambda c: k.small2("out_g")[:, c:c + 1], (YML, k.zT[:, ZO:ZO + 3, :]))
        residual_stage(k, SEQ, w_out, DC, k.y2T, None, k.x2T, w_choose)
        norm_stage(k, SEQ, lambda c, s: k.small2("norm2")[:, c:c + 1], None, k.x2T)
        choose_stage(k, l, w_choose)
        scatter_stage(k)
        experts_stage(k, w_experts)


def layout2(x):
    x = {name[:-2]: a for name, a in x.items() if name.endswith("_2")}
    L = DEPTH
    cuts = np.cumsum([SBW, SBW, SBW, 2 * MLW, MLW, MLW, MLH, MLH, SGW])
    q, kk, v, mqk, mv, mo, mi, mf, su, sv = np.split(x["w_in"], cuts, axis=-1)
    w_if = np.zeros((L, D, P), np.float32)
    w_if[..., 0:MLH], w_if[..., GATE_ROWS:GATE_ROWS + MLH] = mi, mf
    pair = lambda g: np.tile(g, 2)[:, None]
    small2 = np.stack([packed(SMALL2, SMALL2_W, {
        "norm1": chunked(x["norm1_g"][l]), "norm2": chunked(x["norm2_g"][l]),
        "qn_g": pair(x["sb_qn_g"][l]), "kn_g": pair(x["sb_kn_g"][l]),
        "conv_w": chunked(x["ml_conv_w"][l]).transpose(1, 2, 0), "conv_b": chunked(x["ml_conv_b"][l]),
        "out_g": chunked(x["out_g"][l]), "if_b": np.stack([x["ml_i_b"][l], x["ml_f_b"][l]], -1),
        "vn_g": np.broadcast_to(x["sg_vn_g"][l], (P, SGW)), "sg_b": x["sg_b"][l].reshape(1, -1),
        "sg_w": x["sg_w"][l].transpose(2, 0, 1)}) for l in range(L)])
    pu = x["peer_u"].reshape(L, NK, NK, DC, P).transpose(0, 2, 4, 3, 1).reshape(L, NK, P, D)
    pv = x["peer_v"].reshape(L, NK, NK, D).transpose(0, 2, 1, 3)
    query = tiled(x["peer_wq"]).reshape(L, HC, P, D)
    uv = np.empty((L, EARLY + 2 * (NK - EARLY), P, D), np.float32)
    uv[:, :EARLY], late = pv[:, :EARLY], uv[:, EARLY:]
    late[:, 0], late[:, 1:-1:2], late[:, 2:-1:2], late[:, -1] = pu[:, EARLY], pu[:, EARLY + 1:], pv[:, EARLY:-1], pv[:, -1]
    return {
        "small2_dram": small2, "w_transposed2": tiled(np.concatenate([q, kk, mqk, mo, su, w_if], -1)),
        "w_natural2": np.concatenate([v, mv, sv], -1).reshape(L * DC, P, NATURAL2),
        "w_out2": x["w_out"].reshape(L * DC, P, D), "w_choose": np.concatenate([query, pu[:, :EARLY]], axis=1).reshape(-1, P, D),
        "peer_keys": x["peer_keys"].transpose(0, 4, 1, 2, 3).reshape(L, P, HC * NK),
        "peer_uv": uv.reshape(-1, P, D),
    }




class Kit:

    def __init__(self, nc):
        self.nc = nc

    def const(self, name):
        at, width = CONST[name]
        return self.const_sb[:, at:at + width]

    def const2(self, name):
        at, width = CONST2[name]
        return self.const2_sb[:, at:at + width]

    def const1(self, name):
        at, width = CONST1[name]
        return self.const1_sb[:, at:at + width]

    def small1(self, name):
        at, width = SMALL1[name]
        return self.small1_sb[:, at:at + width]

    def small2(self, name):
        at, width = SMALL2[name]
        return self.small2_sb[:, at:at + width]


class Carver:

    def __init__(self, whole):
        self.whole, self.at = whole, 0

    def __call__(self, *shape):
        width = int(np.prod(shape))
        cut = self.whole[:, self.at:self.at + width]
        self.at += width
        assert self.at <= self.whole.shape[1], self.at
        if len(shape) == 2:
            return cut.rearrange("p (a b) -> p a b", a=shape[0])
        if len(shape) == 3:
            return cut.rearrange("p (a b c) -> p a b c", a=shape[0], b=shape[1])
        return cut


def program(nc, dram, out):
    k = Kit(nc)
    tokens = SEQ + CTX
    k.x_in, k.cond_in, k.norm_final_in = dram["x_in"], dram["cond_in"], dram["norm_final_in"]
    k.const_dram, k.const1_dram, k.const2_dram = dram["const_dram"], dram["const1_dram"], dram["const2_dram"]
    k.small1_dram, k.small2_dram = dram["small1_dram"], dram["small2_dram"]
    k.w_mod, k.w_qk, k.w_natural = dram["w_mod"], dram["w_qk"], dram["w_natural"]
    k.w_merge, k.w_out, k.w_up, k.w_down = dram["w_merge"], dram["w_out"], dram["w_up"], dram["w_down"]
    k.w_transposed2, k.w_natural2 = dram["w_transposed2"], dram["w_natural2"]
    k.w_out2, k.w_choose = dram["w_out2"], dram["w_choose"]
    k.peer_keys, k.peer_uv = dram["peer_keys"], dram["peer_uv"]
    with ExitStack() as ctx:

        def sb(scope, name, *shape, dtype=F32):
            return scope.enter_context(nc.sbuf_tensor(name, [P, *shape], dtype))

        k.ps = ctx.enter_context(nc.psum_tensor("ps", [P, 8, 512], F32))
        k.const_sb = sb(ctx, "const_sb", CONST_W)
        k.rstd = sb(ctx, "rstd", tokens)
        k.x2T = sb(ctx, "x2T", DC, SEQ)
        k.ring = sb(ctx, "ring", RAW, D)
        k.split = sb(ctx, "split", SPLIT, 2, D, dtype=F32R)
        with ExitStack() as scope:
            k.const1_sb = sb(scope, "const1_sb", CONST1_W)
            k.small1_sb = sb(scope, "small1_sb", SMALL1_W)
            k.cond = sb(scope, "cond", DC * 2)
            k.cond_silu = sb(scope, "cond_silu", DC * 2)
            k.norm_final = sb(scope, "norm_final_sb", DC)
            k.mod = sb(scope, "mod", NMOD * DC, 2)
            k.xT = sb(scope, "xT", DC, tokens)
            k.hT = sb(scope, "hT", 2, DC, tokens, dtype=F32R)
            k.stat = sb(scope, "stat", 2, 4)
            first_block(k, sb)
        with ExitStack() as scope:
            second_block(k, scope, sb)
        with stage(nc, "stored") as (block, stored):

            @block.sync
            def _(sp):
                sp.dma_start(out, k.x2T[:, :, :]).then_inc(stored, 16)
                sp.wait_ge(stored, 16)


def packed(table, width, parts):
    out = np.zeros((P, width), np.float32)
    for name, part in parts.items():
        at, n = table[name]
        part = np.asarray(part, np.float32)
        part = part.reshape(part.shape[0], n)
        out[:part.shape[0], at:at + n] = part
    return out


def constants():
    i = np.arange(P)
    q, key = np.arange(SEQ)[None, :], np.arange(P)[:, None]
    before = np.concatenate([key < q, (key < np.arange(P)[None, :])], axis=1).astype(np.float32)
    causal = (i[:, None] <= i[None, :]).astype(np.float32)
    heads = np.zeros((P, MLH, P), np.float32)
    pairs = np.zeros((P, DC, P), np.float32)
    for h in range(MLH):
        heads[h, h] = 1
    for h in range(2 * DC):
        pairs[h, h // 2, (h % 2) * HD:(h % 2 + 1) * HD] = 1
    of_row = pairs[0:2 * DC].transpose(2, 1, 0)
    return packed(CONST, CONST_W, {
        "ident": np.eye(P), "ones": np.ones((P, P)),
        "iota": np.broadcast_to(np.arange(NK), (P, NK))}), packed(CONST2, CONST2_W, {
        "suffix": i[:, None] >= i[None, :], "causal": causal,
        "before": before, "not_before": (1 - before) * MASKED, "ahead": np.tile((1 - causal) * -MASKED, (1, 2)),
        "row_of_head": heads, "row_of_pair": pairs,
        "head_of_row": of_row})


def constants1():
    tokens = SEQ + CTX
    freq = (ROPE_BASE ** (-np.arange(HD // 4) / (HD // 4))).astype(np.float32)
    pos = np.arange(SEQ)
    angle = np.stack([np.float32(pos // GRID_W)[:, None] * freq, np.float32(pos % GRID_W)[:, None] * freq], 1)
    cos, sin = np.ones((2, 2, 2, HD // 4, tokens)), np.zeros((2, 2, 2, HD // 4, tokens))
    cos[..., :SEQ] = np.cos(angle).transpose(1, 2, 0)[None, :, None]
    sin[..., :SEQ] = np.sin(angle).transpose(1, 2, 0)[None, :, None]
    swap = np.zeros((P, P))
    for m in range(P):
        quarter = HD // 4
        if m // quarter % 2 == 0:
            swap[m + quarter, m] = -1
        else:
            swap[m - quarter, m] = 1
    window = np.zeros((P, TB, 2 * SEQ))
    for b in range(TB):
        rel = np.arange(SEQ)[None, :] - (b * P + np.arange(P))[:, None]
        window[:, b, :SEQ] = np.where(np.abs(rel) <= WINDOW, 0, MASKED)
    pool = np.zeros((SEQ, len(POOL_WINDOWS), SEQ))
    for g, w in enumerate(POOL_WINDOWS):
        for t in range(SEQ):
            lo, hi = max(t - w // 2, 0), min(t - w // 2 + w, SEQ)
            pool[lo:hi, g, t] += 1.0 / (hi - lo)
            pool[t, g, t] -= 1
    tt = 2 * np.pi * np.outer(np.arange(SEQ), np.arange(SEQ)) / SEQ
    cc = 2 * np.pi * np.outer(np.arange(HD), np.arange(HD)) / HD
    time = np.concatenate([np.cos(tt), np.sin(tt)], 1) / np.sqrt(SEQ)
    chan = np.concatenate([np.kron(np.eye(2), np.cos(cc)), -np.kron(np.eye(2), np.sin(cc))], 1) / np.sqrt(HD)

    def by_block(a):
        return a.reshape(TB, P, -1).transpose(1, 0, 2)

    return packed(CONST1, CONST1_W, {
        "rope_swap": swap, "rope_cos": cos.reshape(P, tokens), "rope_sin": sin.reshape(P, tokens), "window": window,
        "pool": by_block(pool), "dft_time": by_block(time), "dft_chan": chan})


def chunked(a):
    return np.moveaxis(a.reshape(*a.shape[:-1], -1, P), -2, -1)


def tiled(w):
    l, rows, cols = w.shape
    a = w.reshape(l, rows // P, P, cols // P, P).transpose(0, 3, 2, 1, 4)
    return np.ascontiguousarray(a).reshape(l * cols // P, P, rows)


def layout(x):
    x = {name: np.asarray(a) for name, a in x.items()}
    L = DEPTH
    w_in = x["w_in"]
    cuts = np.cumsum([KW, KW, QW, POOLW, FOURW])
    wk, wv, wq, wu, wf, wg = np.split(w_in, cuts, axis=-1)
    heads = np.array([[c, c + QC] for c in range(QC)]).ravel()
    wq = wq.reshape(L, D, QH, HD)[:, :, heads].reshape(L, D, QW)
    br_attn = x["w_br_attn"].reshape(L, QH, HD, D)[:, heads].reshape(L, QW, D)
    branches = np.concatenate([br_attn, x["w_br_pool"], x["w_br_four"]], axis=1)
    merge = np.stack([*(a.reshape(L, DC, P, D) for a in np.split(tiled(wg).reshape(L, 3 * DC, P, D), 3, axis=1)),
                      tiled(branches).reshape(L, DC, P, D)], axis=2)
    up = tiled(x["w_up"]).reshape(L, 2, FC, P, D).transpose(0, 2, 1, 3, 4)
    conv = chunked(x["conv_w"]).reshape(L, 3, P, 2, FC).transpose(0, 2, 1, 4, 3)
    twice = lambda a: np.repeat(chunked(a)[..., None], 2, axis=-1)
    small1 = np.stack([packed(SMALL1, SMALL1_W, {
        "b_mod": twice(x["b_mod"][l]), "norm_mix": twice(x["norm_mix"][l]), "norm_ffn": twice(x["norm_ffn"][l]),
        "sink": np.broadcast_to(x["attn_sink"][l], (P, QH)),
        "pool_w": x["pool_w"][l].reshape(2, 2 * HD, HD).transpose(1, 0, 2), "pool_scale": chunked(x["pool_scale"][l]),
        "conv_w": conv[l]}) for l in range(L)])
    const, const2 = constants()
    feed = {
        "x_in": np.concatenate([chunked(x["x"][0].T.reshape(D, SEQ).T).transpose(1, 2, 0),
                                chunked(x["ctx"][0]).transpose(1, 2, 0)], axis=-1),
        "cond_in": np.stack([chunked(x["c"][0]), chunked(x["c_ctx"])], axis=-1).reshape(P, DC * 2),
        "norm_final_in": chunked(x["norm_final"]),
        "const_dram": const, "const2_dram": const2, "const1_dram": constants1(), "small1_dram": small1,
        "w_mod": x["w_mod"].reshape(L, DC, P, NMOD, D).transpose(0, 3, 1, 2, 4).reshape(L * NMOD * DC, P, D),
        "w_qk": tiled(np.concatenate([wk, wq], -1)),
        "w_natural": np.concatenate([wv, wu, wf], -1).reshape(L * DC, P, NATURAL),
        "w_merge": merge.reshape(L * DC * 4, P, D), "w_out": x["w_out"].reshape(L * DC, P, D), "w_up": up.reshape(-1, P, D),
        "w_down": x["w_down"].reshape(L * FC, P, D),
    }
    feed.update(layout2(x))
    return {name: np.ascontiguousarray(a, np.float32) for name, a in feed.items()}


def kernel(**inputs):
    import concourse.bacc as bacc
    from concourse.bass_utils import run_bass_kernel_spmd

    feed = layout(inputs)
    nc = bacc.Bacc("TRN2", target_bir_lowering=False, num_devices=1)
    dram = {name: nc.dram_tensor(name, a.shape, F32, kind="ExternalInput").ap() for name, a in feed.items()}
    out = nc.dram_tensor("out", (P, DC, SEQ), F32, kind="ExternalOutput").ap()
    program(nc, dram, out)
    got = run_bass_kernel_spmd(nc, [feed], core_ids=[0]).results[0]["out"]
    return np.ascontiguousarray(np.asarray(got).transpose(2, 1, 0)).reshape(1, SEQ, D)
```
